# Optimizing a Trainium2 kernel written in Bass

```python
import math
import jax, jax.numpy as jnp
from jax import lax
import numpy as np

D_MODEL = 1024
BATCH = 1
SEQ = 512
DEPTH = 1

MEM_LEN = 256
GROUP_WIDTH = D_MODEL // 2
D_MIX = 3 * GROUP_WIDTH
LRU_HEADS = 8
LRU_BLOCK = GROUP_WIDTH // LRU_HEADS
CONV_WIDTH = 4
LRU_C = 8.0
DIFF_HEADS = 4
DIFF_HEAD_DIM = GROUP_WIDTH // DIFF_HEADS
DIFF_QK_DIM = DIFF_HEAD_DIM // 2
MEM_HEADS = 4
MEM_HEAD_DIM = GROUP_WIDTH // MEM_HEADS
Q_BLOCK = 128
N_GROUPS = 4
EXPERTS_PER_GROUP = 8
N_EXPERTS = N_GROUPS * EXPERTS_PER_GROUP
TOP_K = 2
D_EXPERT = 256
EPS = 1e-6

LRU_X_OFF = 0
LRU_G_OFF = LRU_X_OFF + GROUP_WIDTH
DIFF_Q_OFF = LRU_G_OFF + GROUP_WIDTH
DIFF_K_OFF = DIFF_Q_OFF + GROUP_WIDTH
DIFF_V_OFF = DIFF_K_OFF + GROUP_WIDTH
MEM_Q_OFF = DIFF_V_OFF + GROUP_WIDTH
D_IN_PROJ = MEM_Q_OFF + GROUP_WIDTH

kernel_name = 'hymba_rglru_diffattn_hiermoe'

def rms_norm(x, g):
    xf = x.astype(jnp.float32)
    xf = xf * lax.rsqrt(jnp.mean(xf * xf, axis=-1, keepdims=True) + EPS)
    return (xf * g.astype(jnp.float32)).astype(x.dtype)

def _lin_combine(c1, c2):
    a1, b1 = c1
    a2, b2 = c2
    return a1 * a2, a2 * b1 + b2

def rg_lru_group(xb, gb, conv_w, conv_b, wa, ba, wx, bx, lam):
    B, S, C = xb.shape
    xc = lax.conv_general_dilated(xb, conv_w[:, None, :], window_strides=(1,), padding=[(CONV_WIDTH - 1, 0)],
                                  dimension_numbers=('NWC', 'WIO', 'NWC'), feature_group_count=C) + conv_b
    xh = xc.reshape(B, S, LRU_HEADS, LRU_BLOCK)
    r = jax.nn.sigmoid(jnp.einsum('bshi,hij->bshj', xh, wa).reshape(B, S, C) + ba)
    i = jax.nn.sigmoid(jnp.einsum('bshi,hij->bshj', xh, wx).reshape(B, S, C) + bx)
    log_a = (-LRU_C * r.astype(jnp.float32)) * jax.nn.softplus(-lam.astype(jnp.float32))
    a = jnp.exp(log_a)
    b = jnp.sqrt(-jnp.expm1(2.0 * log_a)) * (i * xc).astype(jnp.float32)
    _, h = lax.associative_scan(_lin_combine, (a, b), axis=1)
    return h.astype(xb.dtype) * jax.nn.gelu(gb)

def diff_attention(q, k, v, lam):
    B, S, H, _, d = q.shape
    dv = v.shape[-1]
    nb = S // Q_BLOCK
    qb = jnp.moveaxis(q.reshape(B, nb, Q_BLOCK, H, 2, d), 1, 0)
    key_pos = jnp.arange(S)
    scale = d ** -0.5

    def one_block(args):
        q_blk, blk = args
        s = jnp.einsum('bqhcd,bkhcd->bhcqk', q_blk, k).astype(jnp.float32) * scale
        q_pos = blk * Q_BLOCK + jnp.arange(Q_BLOCK)
        mask = key_pos[None, :] <= q_pos[:, None]
        p = jax.nn.softmax(jnp.where(mask, s, -jnp.inf), axis=-1)
        p = p[:, :, 0] - lam * p[:, :, 1]
        return jnp.einsum('bhqk,bkhv->bqhv', p.astype(v.dtype), v)

    o = lax.map(one_block, (qb, jnp.arange(nb)))
    return jnp.moveaxis(o, 0, 1).reshape(B, S, H, dv)

def memory_attention(q, k, v):
    B, S, H, d = q.shape
    s = jnp.einsum('bshd,bmhd->bhsm', q, k).astype(jnp.float32) * (d ** -0.5)
    p = jax.nn.softmax(s, axis=-1)
    return jnp.einsum('bhsm,bmhd->bshd', p.astype(v.dtype), v).reshape(B, S, H * d)

def hier_moe(xn, w_rg, b_rg, w_re, b_re, w_g, w_u, w_d):
    B, S, D = xn.shape
    xt = xn.reshape(B * S, D)
    pg = jax.nn.softmax((xt @ w_rg + b_rg).astype(jnp.float32), axis=-1)
    g_idx = jnp.argmax(pg, axis=-1)
    g_gate = jnp.max(pg, axis=-1)
    le = (xt @ w_re + b_re).astype(jnp.float32).reshape(-1, N_GROUPS, EXPERTS_PER_GROUP)
    le_sel = jnp.take_along_axis(le, g_idx[:, None, None], axis=1)[:, 0]
    top_w, top_i = lax.top_k(jax.nn.softmax(le_sel, axis=-1), TOP_K)
    top_w = top_w / jnp.sum(top_w, axis=-1, keepdims=True)
    e_w = jnp.sum(jax.nn.one_hot(top_i, EXPERTS_PER_GROUP, dtype=jnp.float32) * top_w[..., None], axis=1)
    combine = (jax.nn.one_hot(g_idx, N_GROUPS, dtype=jnp.float32)[:, :, None]
               * (g_gate[:, None] * e_w)[:, None, :]).astype(xn.dtype)
    wg = w_g.reshape(N_GROUPS, EXPERTS_PER_GROUP, D, D_EXPERT)
    wu = w_u.reshape(N_GROUPS, EXPERTS_PER_GROUP, D, D_EXPERT)
    wd = w_d.reshape(N_GROUPS, EXPERTS_PER_GROUP, D_EXPERT, D)
    out = jnp.zeros_like(xt)
    for g in range(N_GROUPS):
        h = jax.nn.silu(jnp.einsum('td,edf->tef', xt, wg[g])) * jnp.einsum('td,edf->tef', xt, wu[g])
        out = out + jnp.einsum('tef,efd->td', h * combine[:, g, :, None], wd[g])
    return out.reshape(B, S, D)

def setup_inputs(seed: int = 0) -> dict:
    key = jax.random.key(seed)
    ks = jax.random.split(key, 32)
    f32 = jnp.float32
    nrm = lambda k, shape, s: jax.random.normal(k, shape, f32) * s
    gain = lambda k, shape: 1.0 + 0.02 * jax.random.normal(k, shape, f32)
    a_c = jax.random.uniform(ks[10], (DEPTH, GROUP_WIDTH), f32, 0.9, 0.999)
    a_base = a_c ** (1.0 / LRU_C)
    rg_lambda = jnp.log(a_base) - jnp.log1p(-a_base)
    return {
        'x': nrm(ks[0], (BATCH, SEQ, D_MODEL), 1.0),
        'mem': nrm(ks[1], (BATCH, MEM_LEN, D_MODEL), 1.0),
        'norm1_g': gain(ks[2], (DEPTH, D_MODEL)),
        'w_in': nrm(ks[3], (DEPTH, D_MODEL, D_IN_PROJ), D_MODEL ** -0.5),
        'conv_w': nrm(ks[4], (DEPTH, CONV_WIDTH, GROUP_WIDTH), CONV_WIDTH ** -0.5),
        'conv_b': nrm(ks[5], (DEPTH, GROUP_WIDTH), 0.02),
        'rg_wa': nrm(ks[6], (DEPTH, LRU_HEADS, LRU_BLOCK, LRU_BLOCK), LRU_BLOCK ** -0.5),
        'rg_ba': nrm(ks[7], (DEPTH, GROUP_WIDTH), 0.02),
        'rg_wx': nrm(ks[8], (DEPTH, LRU_HEADS, LRU_BLOCK, LRU_BLOCK), LRU_BLOCK ** -0.5),
        'rg_bx': nrm(ks[9], (DEPTH, GROUP_WIDTH), 0.02),
        'rg_lambda': rg_lambda,
        'dq_norm_g': gain(ks[11], (DEPTH, DIFF_QK_DIM)),
        'dk_norm_g': gain(ks[12], (DEPTH, DIFF_QK_DIM)),
        'lambda_q1': nrm(ks[13], (DEPTH, DIFF_QK_DIM), 0.1),
        'lambda_k1': nrm(ks[14], (DEPTH, DIFF_QK_DIM), 0.1),
        'lambda_q2': nrm(ks[15], (DEPTH, DIFF_QK_DIM), 0.1),
        'lambda_k2': nrm(ks[16], (DEPTH, DIFF_QK_DIM), 0.1),
        'diff_head_norm_g': gain(ks[17], (DEPTH, DIFF_HEAD_DIM)),
        'mem_norm_g': gain(ks[18], (D_MODEL,)),
        'w_mem_kv': nrm(ks[19], (DEPTH, D_MODEL, 2 * GROUP_WIDTH), D_MODEL ** -0.5),
        'mq_norm_g': gain(ks[20], (DEPTH, MEM_HEAD_DIM)),
        'mk_norm_g': gain(ks[21], (DEPTH, MEM_HEAD_DIM)),
        'w_out': nrm(ks[22], (DEPTH, D_MIX, D_MODEL), D_MIX ** -0.5),
        'norm2_g': gain(ks[23], (DEPTH, D_MODEL)),
        'w_router_group': nrm(ks[24], (DEPTH, D_MODEL, N_GROUPS), D_MODEL ** -0.5),
        'b_router_group': nrm(ks[25], (DEPTH, N_GROUPS), 0.01),
        'w_router_expert': nrm(ks[26], (DEPTH, D_MODEL, N_EXPERTS), D_MODEL ** -0.5),
        'b_router_expert': nrm(ks[27], (DEPTH, N_EXPERTS), 0.01),
        'w_expert_gate': nrm(ks[28], (DEPTH, N_EXPERTS, D_MODEL, D_EXPERT), D_MODEL ** -0.5),
        'w_expert_up': nrm(ks[29], (DEPTH, N_EXPERTS, D_MODEL, D_EXPERT), D_MODEL ** -0.5),
        'w_expert_down': nrm(ks[30], (DEPTH, N_EXPERTS, D_EXPERT, D_MODEL), D_EXPERT ** -0.5),
    }

def reference(x, mem, norm1_g, w_in, conv_w, conv_b, rg_wa, rg_ba, rg_wx, rg_bx, rg_lambda,
              dq_norm_g, dk_norm_g, lambda_q1, lambda_k1, lambda_q2, lambda_k2, diff_head_norm_g,
              mem_norm_g, w_mem_kv, mq_norm_g, mk_norm_g, w_out, norm2_g,
              w_router_group, b_router_group, w_router_expert, b_router_expert,
              w_expert_gate, w_expert_up, w_expert_down):
    B, S, _ = x.shape
    M = mem.shape[1]
    memn = rms_norm(mem, mem_norm_g)
    for l in range(DEPTH):
        lam_init = 0.8 - 0.6 * math.exp(-0.3 * l)
        xn = rms_norm(x, norm1_g[l])
        u = xn @ w_in[l]

        y_lru = rg_lru_group(u[..., LRU_X_OFF:LRU_X_OFF + GROUP_WIDTH], u[..., LRU_G_OFF:LRU_G_OFF + GROUP_WIDTH],
                             conv_w[l], conv_b[l], rg_wa[l], rg_ba[l], rg_wx[l], rg_bx[l], rg_lambda[l])

        q = rms_norm(u[..., DIFF_Q_OFF:DIFF_Q_OFF + GROUP_WIDTH].reshape(B, S, DIFF_HEADS, 2, DIFF_QK_DIM), dq_norm_g[l])
        k = rms_norm(u[..., DIFF_K_OFF:DIFF_K_OFF + GROUP_WIDTH].reshape(B, S, DIFF_HEADS, 2, DIFF_QK_DIM), dk_norm_g[l])
        v = u[..., DIFF_V_OFF:DIFF_V_OFF + GROUP_WIDTH].reshape(B, S, DIFF_HEADS, DIFF_HEAD_DIM)
        lam = (jnp.exp(jnp.sum(lambda_q1[l].astype(jnp.float32) * lambda_k1[l].astype(jnp.float32)))
               - jnp.exp(jnp.sum(lambda_q2[l].astype(jnp.float32) * lambda_k2[l].astype(jnp.float32)))
               + lam_init)
        o = diff_attention(q, k, v, lam)
        y_diff = (rms_norm(o, diff_head_norm_g[l]) * (1.0 - lam_init)).reshape(B, S, GROUP_WIDTH)

        mq = rms_norm(u[..., MEM_Q_OFF:MEM_Q_OFF + GROUP_WIDTH].reshape(B, S, MEM_HEADS, MEM_HEAD_DIM), mq_norm_g[l])
        kv = memn @ w_mem_kv[l]
        mk = rms_norm(kv[..., :GROUP_WIDTH].reshape(B, M, MEM_HEADS, MEM_HEAD_DIM), mk_norm_g[l])
        mv = kv[..., GROUP_WIDTH:].reshape(B, M, MEM_HEADS, MEM_HEAD_DIM)
        y_mem = memory_attention(mq, mk, mv)

        x = x + jnp.concatenate([y_lru, y_diff, y_mem], axis=-1) @ w_out[l]

        x = x + hier_moe(rms_norm(x, norm2_g[l]), w_router_group[l], b_router_group[l],
                         w_router_expert[l], b_router_expert[l],
                         w_expert_gate[l], w_expert_up[l], w_expert_down[l])
    return x


_drawn_inputs = setup_inputs


def setup_inputs(seed=0):
    import zlib

    import numpy as np

    out = dict(_drawn_inputs(seed))
    spreads = {}
    factors = {'rg_ba': 200.0,
     'rg_bx': 200.0,
     'dq_norm_g': 2.794,
     'dk_norm_g': 9.052,
     'diff_head_norm_g': 26.848,
     'mem_norm_g': 8.0,
     'mq_norm_g': 8.0,
     'mk_norm_g': 8.0,
     'b_router_group': 23.68,
     'b_router_expert': 35.218,
     'conv_b': 19.656,
     'rg_wa': 28.216,
     'rg_lambda': 26.864,
     'lambda_q1': 3.019,
     'lambda_k1': 4.293,
     'lambda_q2': 2.981,
     'lambda_k2': 3.93,
     'norm2_g': 8.0,
     'conv_w': 8.0,
     'rg_wx': 8.0}
    for name, (base, spread) in spreads.items():
        noise = np.random.default_rng([zlib.crc32(name.encode()), seed]).standard_normal(out[name].shape)
        drawn = base * np.exp(spread * noise) if base else spread * noise
        out[name] = __import__('jax').numpy.asarray(drawn.astype(out[name].dtype))
    for name, factor in factors.items():
        out[name] = (out[name] * factor).astype(out[name].dtype)
    return out
```

```python
from contextlib import ExitStack

import concourse.bass as bass
from concourse import mybir

P = 128
D = 1024
KT = D // P
S = 512
TB = S // P
M = 256
MB = M // P
GW = 512
NF = GW // P
CONV = 4
LRU_BLOCK = 64
LRU_C = 8.0
QK_DIM = 64
HD = 128
NG, NE_G = 4, 8
NE = NG * NE_G
FE = 256
EPS = 1e-6
LAM_INIT = 0.2
CAP = 64
ROUNDS = S // CAP
NR = NG + NE
BIG = 2048.0
NEG = -1e30

RING = 3
SLOT = KT * 2 * FE + 2 * D
UN = 2 * RING

F32 = mybir.dt.float32
I32 = mybir.dt.int32
U32 = mybir.dt.uint32
ALU = mybir.AluOpType
ACT = mybir.ActivationFunctionType
AX = mybir.AxisListType.X

INS = ['x', 'mem', 'norm1_g', 'w_in', 'conv_w', 'conv_b', 'rg_wa', 'rg_ba', 'rg_wx', 'rg_bx', 'rg_lambda',
       'dq_norm_g', 'dk_norm_g', 'lambda_q1', 'lambda_k1', 'lambda_q2', 'lambda_k2', 'diff_head_norm_g',
       'mem_norm_g', 'w_mem_kv', 'mq_norm_g', 'mk_norm_g', 'w_out', 'norm2_g',
       'w_router_group', 'b_router_group', 'w_router_expert', 'b_router_expert',
       'w_expert_gate', 'w_expert_up', 'w_expert_down']


def build(nc, a, out):
    chunks = ['lx', 'lg', 'mk', 'mv', 'mq', 'wo0', 'k', 'q', 'v', 'wo2', 'wo1']
    NCH = len(chunks)
    CH = {k: n for n, k in enumerate(chunks)}
    tb, mb = range(TB), range(MB)

    def wo_tiles(c):
        return [(f'wo{c}', b, h) for b in tb for h in range(2)]

    part_a = ([('lx', f) for f in range(NF)] + [('lg', f) for f in range(NF)] + [('mk', m) for m in mb]
              + [('mv', m) for m in mb] + [('mq', b) for b in tb] + wo_tiles(0))
    part_b = [('k', b) for b in tb] + [('q', b) for b in tb] + [('v', b) for b in tb] + wo_tiles(2)
    tiles = part_a + part_b + wo_tiles(1)
    PA = {k: n for n, k in enumerate(tiles)}
    normed = ([('mk', m) for m in mb] + [('mq', b) for b in tb] + [('ym', b) for b in tb]
              + [('k', b) for b in tb] + [('q', b) for b in tb] + [('yd', b) for b in tb])
    NT = {k: n for n, k in enumerate(normed)}
    sums = [k for k in normed if k[0] != 'ym']
    SM = {k: n for n, k in enumerate(sums)}
    copies = [('mv', m) for m in mb] + [('v', b) for b in tb]
    CP = {k: n for n, k in enumerate(copies)}
    mem_units = [(b, hp) for b in tb for hp in range(2)]
    diff_units = [(b, h) for b in tb for h in range(NF)]
    scores = [(g, f) for f in range(NF) for g in ('ga', 'gx')]
    scores += [('sm', u) for u in range(len(mem_units))]
    scores += [('sd', u, c) for u in range(len(diff_units)) for c in range(2)]
    scores += [('lo', b) for b in tb] + [('cum', b) for b in tb] + [('cnt', 0)]
    PS = {k: n for n, k in enumerate(scores)}
    turns = [('par', 0)] + [('in', rb, h) for rb in (2, 3, 4, 5, 0, 1) for h in range(2)]
    turns += [('mk', m) for m in mb] + [('mq', b) for b in tb]
    for u, (b, hp) in enumerate(mem_units):
        turns.append(('pm', u))
        if hp == 0 and b >= 1:
            turns.append(('ym', b - 1))
    turns.append(('ym', TB - 1))
    turns += [('k', b) for b in tb] + [('q', b) for b in tb]
    for u, (b, h) in enumerate(diff_units):
        turns.append(('pd', u))
        if h == 0 and b >= 1:
            turns.append(('yd', b - 1))
    turns.append(('yd', TB - 1))
    turns += [('x2', b, h) for b in tb for h in range(2)]
    PT = {k: n for n, k in enumerate(turns)}
    FT = {k: n for n, k in enumerate([k for k in turns if k in NT])}
    PB = {k: n for n, k in enumerate([k for k in turns if k[0] in ('pm', 'pd')])}
    IN = {k: n for n, k in enumerate([k for k in turns if k[0] == 'in'])}
    X2 = {k: n for n, k in enumerate([k for k in turns if k[0] == 'x2'])}
    WO = {k: n for n, k in enumerate([k for k in tiles if k[0][:2] == 'wo'])}
    in_order = (2, 3, 4, 5, 0, 1)

    with ExitStack() as ctx:
        def sb(name, shape, dt=F32):
            return ctx.enter_context(nc.sbuf_tensor(name, shape, dt))

        def sem(name):
            return ctx.enter_context(nc.semaphore(name))

        pa = [ctx.enter_context(nc.psum_tensor(f"pa{i}", [P, 512], F32)) for i in range(2)]
        pt = [ctx.enter_context(nc.psum_tensor(f"pt{i}", [P, 512], F32)) for i in range(2)]
        ps = [ctx.enter_context(nc.psum_tensor(f"ps{i}", [P, 512], F32)) for i in range(2)]
        po = [ctx.enter_context(nc.psum_tensor(f"po{i}", [P, 512], F32)) for i in range(2)]

        xn_dram = nc.dram_tensor("xn_scratch", (S, D), F32, kind="Internal").ap()
        y_dram = nc.dram_tensor("y_scratch", (2 * S, D), F32, kind="Internal").ap()

        ring = sb("ring", [P, RING, SLOT])
        x_sb = sb("x_sb", [P, TB, D])
        act_t = sb("act_t", [P, KT * (M + S)])
        act = act_t[:, :].rearrange("p (k n) -> p k n", k=KT)
        sq = sb("sq", [P, 2, GW])
        sc = sb("sc", [P, 2, GW])
        y_t = sb("y_t", [P, 2 * NF, S])
        p_t = sb("p_t", [P, 2, S])
        memq = sb("memq", [P, 4096])
        mk_t = memq[:, 0:1024].rearrange("p (h m) -> p h m", h=NF)
        mv = memq[:, 1024:2048].rearrange("p (t v) -> p t v", t=MB)
        mq_t = memq[:, 2048:4096].rearrange("p (h s) -> p h s", h=NF)
        xpad = sb("xpad", [P, 2, S + CONV])
        area = sb("area", [P, 4, NF * S])
        lru = area[:, :, :].rearrange("p w (f s) -> p w f s", f=NF)
        xc, ra, ix, th = lru[:, 0], lru[:, 1], lru[:, 2], lru[:, 3]
        mem_sb = area[:, 3, :].rearrange("p (t d) -> p t d", t=2)
        xs = area[:, 2, :].rearrange("p (t d) -> p t d", t=2)
        k_t, q_t, v_sb = lru[:, 0], lru[:, 1], lru[:, 2]
        e_sb = area[:, 3, :].rearrange("p (u c n) -> p u c n", u=2, c=2)
        x2_t = area[:, 0, :].rearrange("p (u k n) -> p u k n", u=2, k=KT)
        xs2 = area[:, 1, :].rearrange("p (u d) -> p u d", u=2)
        y_sb = area[0:CAP, 2, :].rearrange("p (u d) -> p u d", u=2)
        xg = act_t[:, 0:3 * D].rearrange("p (u d) -> p u d", u=3)
        xg_t = act_t[:, 3072:4096].rearrange("p (u k s) -> p u k s", u=2, k=KT)
        silu = act_t[0:CAP, 4096:4608].rearrange("p (u f) -> p u f", u=2)
        h_sb = act_t[:, 4608:5120].rearrange("p (u f) -> p u f", u=2)
        h_t = act_t[:, 5120:5376].rearrange("p (u j s) -> p u j s", u=2, j=2)

        res = ring[:, 0:2, :].rearrange("p r n -> p (r n)")[:, 0:TB * 2 * D].rearrange("p (b c d) -> p b c d", b=TB, c=2)

        ident = sb("ident", [P, P])
        ones = sb("ones", [P, P])
        tri = sb("tri", [P, P])
        cmask = sb("cmask", [P, P])
        gates_w = sb("gates_w", [P, 2, NF, P])
        rows = sb("rows", [P, P])
        cols = sb("cols", [P, P])
        gain_in = sb("gain_in", [P, 3, KT])
        lam4 = sb("lam4", [P, 4, QK_DIM])
        lam_s = sb("lam_s", [P, 4])
        wr = sb("wr", [P, KT, NR])
        wr_g = sb("wr_g", [P, KT, NG])
        wr_e = sb("wr_e", [P, KT, NE])
        br = sb("br", [P, NR])
        sp = sb("sp", [P, 10, NF])
        half_neg = sb("half_neg", [P, 8])
        st_in = sb("st_in", [P, 2, 12])
        st = sb("st", [P, 2, len(sums), 8])
        mx = sb("mx", [P, 64])
        nb = sb("nb", [P, 64])
        rs = sb("rs", [P, 64])
        rr = sb("rr", [P, 64])
        idx_i = sb("idx_i", [P, CAP], I32)
        iota_s = sb("iota_s", [P, CAP])
        tok_i = sb("tok_i", [P, TB], I32)
        tok = sb("tok", [P, TB])
        lg_sb = sb("lg_sb", [P, TB, NR])
        spare = [0]

        def table(*shape):
            n = 1
            for x in shape:
                n *= x
            o = spare[0]
            spare[0] += n
            names = "abcd"[0:len(shape)]
            return memq[:, o:o + n].rearrange(f"p ({' '.join(names)}) -> p {' '.join(names)}",
                                              **{c: x for c, x in zip(names, shape)})
        rt = table(12, TB, 8)
        rprod = table(TB, NE)
        sel, comb, posm = table(TB, NE), table(TB, NE), table(TB, NE)
        tab_r = table(TB, NE, 3)
        onehot = table(2, TB, CAP)
        rti = sb("rti", [P, 2, TB, 8], U32)
        tab = sb("tab", [P, NE, 3])
        carrier = sb("carrier", [1, 4])
        idx = sb("idx", [P, UN, 1], U32)
        idy = sb("idy", [P, UN, 1], U32)
        gw = sb("gw", [P, UN, 1])
        nr_i = sb("nr_i", [P, 1], I32)
        cnt = sb("cnt", [P, 16])

        C_CONV, C_CB, C_BA, C_BX, C_LAM, C_DQ, C_DK, C_DH, C_MQ, C_MK, N_ROWS = 0, 16, 20, 24, 28, 32, 33, 34, 35, 36, 37
        gain_of = {'q': C_DQ, 'k': C_DK, 'yd': C_DH, 'mq': C_MQ, 'mk': C_MK}
        groups_of = {'q': 8, 'k': 8, 'yd': 4, 'mq': 4, 'mk': 4, 'ym': 4}

        s_mem = sem("s_mem")
        s_x = [sem(f"s_x{b}") for b in tb]
        s_par = sem("s_par")
        s_rows = sem("s_rows")
        s_gw = sem("s_gw")
        chunk_in = [sem(f"chunk_in{c}") for c in range(NCH)]
        expert_in = [sem(f"expert_in{j}") for j in range(UN)]
        consts, pool_step, act_step, dve_step = sem("consts"), sem("pool_step"), sem("act_step"), sem("dve_step")
        pads_ready = sem("pads_ready")
        pa_done, pt_done, ps_done = sem("pa_done"), sem("pt_done"), sem("ps_done")
        cols_ready = sem("cols_ready")
        in_sum, in_rstd, in_scaled, in_feat = sem("in_sum"), sem("in_rstd"), sem("in_scaled"), sem("in_feat")
        abs_ready, sp_exp, sp_ready, lam_sum, lam_exp, lam_ready = (
            sem(n) for n in ("abs_ready", "sp_exp", "sp_ready", "lam_sum", "lam_exp", "lam_ready"))
        xpad_ready, xc_ready, gelu_ready, sig_ready, a_ready = (
            sem(n) for n in ("xpad_ready", "xc_ready", "gelu_ready", "sig_ready", "a_ready"))
        b2_ready, b_ready, lru_ready = sem("b2_ready"), sem("b_ready"), sem("lru_ready")
        sq_ready, ss_ready, rstd_ready, sc_ready, feat_ready = (
            sem(n) for n in ("sq_ready", "ss_ready", "rstd_ready", "sc_ready", "feat_ready"))
        copied = sem("copied")
        mem_nb, mem_exp, diff_nb, diff_exp, p_ready, pt_ready, pv_done = (
            sem(n) for n in ("mem_nb", "mem_exp", "diff_nb", "diff_exp", "p_ready", "pt_ready", "pv_done"))
        wo_added, x1_stored, sum2, rstd2, scaled2, x2_ready, logits_ready = (
            sem(n) for n in ("wo_added", "x1_stored", "sum2", "rstd2", "scaled2", "x2_ready", "logits_ready"))
        wr_ready, r_exp_in, r_exp_out, sel_ready, cum_read, nr_ready = (
            sem(n) for n in ("wr_ready", "r_exp_in", "r_exp_out", "sel_ready", "cum_read", "nr_ready"))
        xg_loaded = [sem(f"xg_loaded{g}") for g in range(3)]
        res_in = [[sem(f"res_in{b}_{c}") for c in range(2)] for b in tb]
        res_added, out_stored, all_scattered = sem("res_added"), sem("out_stored"), sem("all_scattered")
        carried = [sem("gather_carried"), sem("scatter_carried")]
        xn_stored = [sem(f"xn_stored{b}") for b in tb]
        oh_ready, tab_done, tab_ready = sem("oh_ready"), sem("tab_done"), sem("tab_ready")
        idx_ready, xt_done, xt_ready = (
            sem(n) for n in ("idx_ready", "xt_done", "xt_ready"))
        scattered = [sem("scattered0"), sem("scattered1")]
        gu_done, silu_ready, h_ready, ht_done, ht_ready, y_done, y_copied0, y_copied1, round_done = (
            sem(n) for n in ("gu_done", "silu_ready", "h_ready", "ht_done", "ht_ready", "y_done", "y_copied0",
                             "y_copied1", "round_done"))

        def pa_freed(n):
            k = tiles[n]
            if k[0] == 'lx':
                return xpad_ready, k[1] + 1
            if k[0] == 'lg':
                return gelu_ready, k[1] + 1
            if k in CP:
                return copied, CP[k] + 1
            if k in WO:
                return wo_added, WO[k] + 1
            return sc_ready, NT[k] + 1

        def pt_freed(n):
            k = turns[n]
            if k[0] == 'par':
                return cols_ready, 1
            if k[0] == 'in':
                return in_feat, IN[k] + 1
            if k in PB:
                return pt_ready, PB[k] + 1
            if k in X2:
                return x2_ready, X2[k] + 1
            return feat_ready, FT[k] + 1

        def ps_freed(n):
            k = scores[n]
            if k[0] in ('ga', 'gx'):
                return sig_ready, n + 1
            if k[0] == 'sm':
                return mem_exp, 2 * (k[1] + 1)
            if k[0] == 'sd':
                return diff_exp, 2 * k[1] + k[2] + 1
            if k[0] == 'lo':
                return logits_ready, k[1] + 1
            return cum_read, (k[1] if k[0] == 'cum' else TB) + 1

        w_in_v = a['w_in'][0].rearrange("(p k) n -> p k n", k=KT)
        w_kv_v = a['w_mem_kv'][0].rearrange("(p k) n -> p k n", k=KT)
        w_out_v = a['w_out'][0].rearrange("(c k p) n -> c p k n", p=P, k=NF)
        col_of = {'lx': 0, 'lg': 512, 'q': 1024, 'k': 1536, 'v': 2048, 'mq': 2560}
        wg_v = a['w_expert_gate'][0].rearrange("e (p k) f -> e p (k f)", k=KT)
        wu_v = a['w_expert_up'][0].rearrange("e (p k) f -> e p (k f)", k=KT)
        wd_v = a['w_expert_down'][0].rearrange("e (p j) n -> e p (j n)", j=2)

        def chunk(name):
            k = NF if name[:2] == 'wo' else KT
            return ring[:, CH[name] % RING, 0:KT * 512].rearrange("p (k n) -> p k n", k=k)

        def chunk_end(c):
            return max(i for i, k in enumerate(tiles) if k[0] == chunks[c]) + 1

        def slot_of(j):
            return (NCH + j) % RING

        def expert_gu(j):
            return ring[:, slot_of(j), 0:2 * KT * FE].rearrange("p (w k f) -> p w k f", w=2, k=KT)

        def expert_d(j):
            return ring[:, slot_of(j), 2 * KT * FE:SLOT].rearrange("p (j n) -> p j n", j=2)

        full = (NE - 3) // UN
        left = NE - full * UN

        def bodies(eng, body):
            for j in range(UN):
                body(j, j, j == 0, False)
            with eng.Fori(1, full) as i:
                e_iter[0] = i
                for j in range(UN):
                    body(i * UN + j, j, False, False)
            for j in range(left):
                body(full * UN + j, j % UN, False, j == left - 1)
        e_iter = [0]

        def all_rounds(eng, round_):
            round_(0)
            eng.wait_ge(nr_ready, 1)
            rounds = eng.value_load(nr_i[0:1, 0:1], min_val=0, max_val=ROUNDS)
            with eng.Fori(1, ROUNDS) as r:
                with eng.If(r < rounds):
                    round_(r)

        block = ctx.enter_context(nc.Block())

        @block.sync
        def _(sync):
            x_v = a['x'][0].rearrange("(t p) d -> t p d", p=P)
            for b in tb:
                sync.dma_start(x_sb[:, b, :], x_v[b]).then_inc(s_x[b], 16)
                if b == 0:
                    sync.dma_start(chunk('lx'), w_in_v[:, :, 0:512]).then_inc(chunk_in[0], 16)
            sync.dma_start(mem_sb, a['mem'][0].rearrange("(t p) d -> p t d", p=P)).then_inc(s_mem, 16)
            for c, name in enumerate(chunks):
                if c == 0:
                    continue
                if c >= RING:
                    sync.wait_ge(pa_done, chunk_end(c - RING))
                if name in col_of:
                    src = w_in_v[:, :, col_of[name]:col_of[name] + 512]
                elif name in ('mk', 'mv'):
                    o = 0 if name == 'mk' else 512
                    src = w_kv_v[:, :, o:o + 512]
                else:
                    src = w_out_v[int(name[2])]
                sync.dma_start(chunk(name), src).then_inc(chunk_in[c], 16)

            def load(n, e, j):
                if isinstance(n, int) and n < RING:
                    sync.wait_ge(pa_done, chunk_end(NCH - RING + n))
                else:
                    sync.wait_ge(y_done, n - RING + 1)
                w = KT * FE
                slot = ring[:, slot_of(j), :]
                for m, src in enumerate((wg_v, wu_v, wd_v)):
                    row = src[e] if isinstance(e, int) else src[bass.ds(e, 1)].rearrange("o p n -> (o p) n")
                    sync.dma_start(slot[:, m * w:(m + 1) * w], row).then_inc(expert_in[j], 16)

            all_rounds(sync, lambda r: bodies(sync, lambda e, j, first, last: load(r * NE + e, e, j)))

            sync.wait_ge(all_scattered, 2)
            y_v = y_dram.rearrange("(c t p) d -> c t p d", c=2, p=P)
            for b in tb:
                for c in range(2):
                    sync.dma_start(res[:, b, c, :], y_v[c, b]).then_inc(res_in[b][c], 16)
            o_v = out[0].rearrange("(t p) d -> t p d", p=P)
            for b in tb:
                sync.wait_ge(res_added, b + 1)
                sync.dma_start(o_v[b], x_sb[:, b, :]).then_inc(out_stored, 16)
            sync.wait_ge(out_stored, 16 * TB)

        @block.gpsimd
        def _(pool):
            steps = [0]

            def link(ins):
                steps[0] += 1
                ins.then_inc(pool_step, 1)
                pool.wait_ge(pool_step, steps[0])

            link(pool.memset(gates_w[:, :, :, :], 0.0))
            for g, w in enumerate((a['rg_wa'], a['rg_wx'])):
                v = w[0].rearrange("(f h) i j -> h i f j", h=2)
                for h in range(2):
                    pool.dma_start(gates_w[64 * h:64 * h + 64, g, :, 64 * h:64 * h + 64], v[h]).then_inc(s_gw, 16)
            link(pool.memset(ident[:, :], 0.0))
            link(pool.memset(ones[:, :], 1.0))
            link(pool.memset(cmask[:, :], 0.0))
            link(pool.memset(half_neg[:, :], -0.5))
            link(pool.affine_select(out=ident[:, :], in_=ident[:, :], compare_op=ALU.not_equal, fill=1.0,
                                    base=0, pattern=[[-1, P]], channel_multiplier=1))
            link(pool.affine_select(out=cmask[:, :], in_=cmask[:, :], compare_op=ALU.is_ge, fill=NEG,
                                    base=0, pattern=[[-1, P]], channel_multiplier=1))
            link(pool.affine_select(out=tri[:, :], in_=ones[:, :], compare_op=ALU.is_gt, fill=0.0,
                                    base=0, pattern=[[1, P]], channel_multiplier=-1))
            link(pool.iota(idx_i[:, :], pattern=[[1, CAP]], base=0, channel_multiplier=0))
            link(pool.iota(tok_i[:, :], pattern=[[P, TB]], base=-int(BIG), channel_multiplier=1))
            link(pool.tensor_copy(iota_s[:, :], idx_i[:, :]))
            pool.tensor_copy(tok[:, :], tok_i[:, :]).then_inc(consts, 1)

            def rsqrt(src, dst, div, const, done):
                link(pool.tensor_scalar(dst, src, div, EPS, ALU.mult, ALU.add))
                pool.tensor_tensor(dst, dst, const, ALU.pow).then_inc(done, 1)

            for n in range(TB + MB):
                pool.wait_ge(in_sum, n + 1)
                rsqrt(st_in[:, 0, n:n + 1], st_in[:, 1, n:n + 1], 1.0 / D, half_neg[:, 0:1], in_rstd)
            for n, k in enumerate(sums):
                g = groups_of[k[0]]
                pool.wait_ge(ss_ready, n + 1)
                rsqrt(st[:, 0, n, 0:g], st[:, 1, n, 0:g], g / GW, half_neg[:, 0:g], rstd_ready)
            for b in tb:
                n = TB + MB + b
                pool.wait_ge(sum2, b + 1)
                rsqrt(st_in[:, 0, n:n + 1], st_in[:, 1, n:n + 1], 1.0 / D, half_neg[:, 0:1], rstd2)

            for b in tb:
                pool.wait_ge(xn_stored[b], 16)

            def carry_waits(n, i):
                pool.wait_ge(carried[i], n)
                pool.tensor_tensor(carrier[0:1, i:i + 1], half_neg[0:1, 0:1], half_neg[0:1, 0:1], ALU.mult).then_inc(carried[i], 1)

            def gather(n, j):
                g = j % 3
                pool.wait_ge(idx_ready, n + 1)
                pool.wait_ge(xt_done, n + 1)
                carry_waits(n, 0)
                pool.indirect_dma_start(
                    out=xg[0:CAP, g, :], out_offset=None, in_=xn_dram,
                    in_offset=bass.IndirectOffsetOnAxis(ap=idx[0:CAP, j, :], axis=0),
                    bounds_check=S - 1, oob_is_err=False).then_inc(xg_loaded[g], 16)

            def scatter(n, j, u):
                pool.wait_ge(y_copied0, n + 1)
                pool.wait_ge(y_copied1, n + 1)
                carry_waits(n, 1)
                pool.indirect_dma_start(
                    out=y_dram, out_offset=bass.IndirectOffsetOnAxis(ap=idy[0:CAP, j, :], axis=0),
                    in_=y_sb[:, u, :], in_offset=None,
                    bounds_check=2 * S - 1, oob_is_err=False).then_inc(scattered[u], 16)

            def round_(r):
                pool.wait_ge(xt_done, r * NE + 3)
                gather(r * NE, 0)
                gather(r * NE + 1, 1)

                def expert(e, j, first, last):
                    if not isinstance(e, int) or e + 2 < NE:
                        gather(r * NE + e + 2, (j + 2) % UN)
                    if not first:
                        scatter(r * NE + e - 1, (j - 1) % UN, (j - 1) % 2)
                bodies(pool, expert)
                scatter(r * NE + NE - 1, (NE - 1) % UN, (NE - 1) % 2)
            all_rounds(pool, round_)
            rounds = pool.value_load(nr_i[0:1, 0:1], min_val=0, max_val=ROUNDS)
            for u in range(2):
                pool.wait_ge(scattered[u], rounds * (8 * NE))
                pool.tensor_tensor(carrier[0:1, 2 + u:3 + u], half_neg[0:1, 0:1], half_neg[0:1, 0:1], ALU.mult).then_inc(all_scattered, 1)

        @block.scalar
        def _(act_e):
            steps = [0]

            def link(ins):
                steps[0] += 1
                ins.then_inc(act_step, 1)
                act_e.wait_ge(act_step, steps[0])

            o = 0
            for src in (a['conv_w'][0].rearrange("j (f p) -> (j f) p", p=P),
                        a['conv_b'].rearrange("o (f p) -> (o f) p", p=P), a['rg_ba'].rearrange("o (f p) -> (o f) p", p=P),
                        a['rg_bx'].rearrange("o (f p) -> (o f) p", p=P), a['rg_lambda'].rearrange("o (f p) -> (o f) p", p=P)):
                n = src.shape[0]
                act_e.dma_start(rows[o:o + n, :], src).then_inc(s_rows, 16)
                o += n
            for c, src in ((C_DQ, a['dq_norm_g']), (C_DK, a['dk_norm_g'])):
                for h in range(2):
                    act_e.dma_start(rows[c:c + 1, 64 * h:64 * h + 64], src).then_inc(s_rows, 16)
            for c, src in ((C_DH, a['diff_head_norm_g']), (C_MQ, a['mq_norm_g']), (C_MK, a['mk_norm_g'])):
                act_e.dma_start(rows[c:c + 1, :], src).then_inc(s_rows, 16)
            N_ROW_DMAS = 12
            act_e.dma_start(gain_in[:, 0, :], a['mem_norm_g'].rearrange("(p k) -> p k", k=KT)).then_inc(s_par, 16)
            act_e.dma_start(gain_in[:, 1, :], a['norm1_g'][0].rearrange("(p k) -> p k", k=KT)).then_inc(s_par, 16)
            act_e.dma_start(gain_in[:, 2, :], a['norm2_g'][0].rearrange("(p k) -> p k", k=KT)).then_inc(s_par, 16)
            act_e.dma_start(wr_g[:, :, :], a['w_router_group'][0].rearrange("(p k) g -> p k g", k=KT)).then_inc(s_par, 16)
            act_e.dma_start(wr_e[:, :, :], a['w_router_expert'][0].rearrange("(p k) g -> p k g", k=KT)).then_inc(s_par, 16)
            act_e.dma_start(br[:, 0:NG], a['b_router_group'].to_broadcast([P, NG])).then_inc(s_par, 16)
            act_e.dma_start(br[:, NG:NR], a['b_router_expert'].to_broadcast([P, NE])).then_inc(s_par, 16)
            for n, w in enumerate(('lambda_q1', 'lambda_k1', 'lambda_q2', 'lambda_k2')):
                act_e.dma_start(lam4[:, n, :], a[w].to_broadcast([P, QK_DIM])).then_inc(s_par, 16)

            for n, rb in enumerate(in_order):
                if rb >= MB:
                    act_e.wait_ge(s_x[rb - MB], 16)
                    src = x_sb[:, rb - MB, :]
                else:
                    act_e.wait_ge(s_mem, 16)
                    src = mem_sb[:, rb, :]
                link(act_e.activation(y_t[:, 2 * (n % 2):2 * (n % 2) + 2, :].rearrange("p a b -> p (a b)"), src, ACT.Square,
                                      accum_out=st_in[:, 0, n:n + 1]))
                act_e.activation(cnt[:, 15:16], st_in[:, 0, n:n + 1], ACT.Copy).then_inc(in_sum, 1)

            act_e.wait_ge(abs_ready, 1)
            act_e.activation(sp[:, 1, :], sp[:, 0, :], ACT.Exp, scale=-1.0).then_inc(sp_exp, 1)
            act_e.wait_ge(lam_sum, 1)
            act_e.activation(lam_s[:, 2:4], lam_s[:, 0:2], ACT.Exp).then_inc(lam_exp, 1)

            act_e.wait_ge(pads_ready, 1)
            for f in range(NF):
                act_e.wait_ge(pa_done, PA[('lx', f)] + 1)
                if f >= 2:
                    act_e.wait_ge(xc_ready, f - 1)
                act_e.activation(xpad[:, f % 2, CONV - 1:CONV - 1 + S], pa[PA[('lx', f)] % 2][:, :], ACT.Copy).then_inc(xpad_ready, 1)
            for f in range(NF):
                act_e.wait_ge(pa_done, PA[('lg', f)] + 1)
                act_e.activation(y_t[:, f, :], pa[PA[('lg', f)] % 2][:, :], ACT.Gelu_apprx_tanh).then_inc(gelu_ready, 1)
            for n, (g, f) in enumerate(scores[0:2 * NF]):
                act_e.wait_ge(ps_done, n + 1)
                c = (C_BA if g == 'ga' else C_BX) + f
                dst = ra[:, f, :] if g == 'ga' else ix[:, f, :]
                act_e.activation(dst, ps[n % 2][:, :], ACT.Sigmoid, bias=cols[:, c:c + 1]).then_inc(sig_ready, 1)
            act_e.wait_ge(sp_ready, 1)
            act_e.wait_ge(sig_ready, 2 * NF)
            for f in range(NF):
                act_e.activation(th[:, f, :], ra[:, f, :], ACT.Tanh, scale=sp[:, 8, f:f + 1]).then_inc(act_step, 1)
                steps[0] += 1
            act_e.wait_ge(act_step, steps[0])
            for f in range(NF):
                act_e.activation(ra[:, f, :], ra[:, f, :], ACT.Exp, scale=sp[:, 9, f:f + 1]).then_inc(a_ready, 1)
            for f in range(NF):
                act_e.wait_ge(b2_ready, f + 1)
                act_e.activation(th[:, f, :], th[:, f, :], ACT.Sqrt).then_inc(b_ready, 1)

            def square(k, src, wait):
                n = SM[k]
                act_e.wait_ge(*wait)
                if n >= 2:
                    act_e.wait_ge(ss_ready, n - 1)
                act_e.activation(sq[:, n % 2, :], src, ACT.Square).then_inc(sq_ready, 1)

            def features(k):
                kind, b = k
                dst = {'mk': mk_t, 'mq': mq_t, 'k': k_t, 'q': q_t, 'yd': y_t[:, 0:NF, :], 'ym': y_t[:, NF:2 * NF, :]}[kind]
                act_e.wait_ge(pt_done, PT[k] + 1)
                if k == ('yd', 0):
                    act_e.wait_ge(pa_done, PA[('wo0', TB - 1, 1)] + 1)
                src = pt[PT[k] % 2][:, :].rearrange("p (h t) -> p h t", h=NF)
                sc_ = 1.0 if kind == 'ym' else cols[:, gain_of[kind]:gain_of[kind] + 1]
                act_e.activation(dst[:, :, b * P:(b + 1) * P], src, ACT.Copy, scale=sc_).then_inc(feat_ready, 1)

            def copy(k):
                dst = (mv if k[0] == 'mv' else v_sb)[:, k[1], :]
                act_e.wait_ge(pa_done, PA[k] + 1)
                act_e.activation(dst, pa[PA[k] % 2][:, :], ACT.Copy).then_inc(copied, 1)

            def project(part):
                before = None
                for k in part:
                    if k in SM:
                        square(k, pa[PA[k] % 2][:, :], (pa_done, PA[k] + 1))
                    if k in CP:
                        copy(k)
                    if before in SM:
                        features(before)
                    before = k

            def probs(k, n):
                i = PB[k]
                act_e.wait_ge(pt_done, PT[k] + 1)
                if i >= 2:
                    act_e.wait_ge(pv_done, i - 1)
                act_e.activation(p_t[:, i % 2, 0:n], pt[PT[k] % 2][:, 0:n], ACT.Copy).then_inc(pt_ready, 1)

            project(part_a[2 * NF:])

            def mem_exps(u):
                act_e.wait_ge(mem_nb, u + 1)
                if u >= 2:
                    act_e.wait_ge(pt_done, PT[('pm', u - 2)] + 1)
                for i in range(2):
                    act_e.activation(e_sb[:, u % 2, 0, i * M:(i + 1) * M], ps[PS[('sm', u)] % 2][:, i * M:(i + 1) * M],
                                     ACT.Exp, bias=nb[:, 2 * u + i:2 * u + i + 1], scale=HD ** -0.5,
                                     accum_out=rs[:, 2 * u + i:2 * u + i + 1]).then_inc(mem_exp, 1)
            act_e.wait_ge(lru_ready, NF)
            mem_exps(0)
            for u, (b, hp) in enumerate(mem_units):
                if u + 1 < len(mem_units):
                    mem_exps(u + 1)
                probs(('pm', u), 512)
                if hp == 0 and b >= 1:
                    features(('ym', b - 1))
            features(('ym', TB - 1))
            act_e.wait_ge(lru_ready, NF)
            project(part_b)

            def diff_exps(u):
                b, h = diff_units[u]
                n = (b + 1) * P
                for c in range(2):
                    act_e.wait_ge(diff_nb, 2 * u + c + 1)
                    if u >= 2 and c == 0:
                        act_e.wait_ge(pt_done, PT[('pd', u - 2)] + 1)
                    i = 16 + 2 * (u % 16) + c
                    act_e.activation(e_sb[:, u % 2, c, 0:n], ps[PS[('sd', u, c)] % 2][:, 0:n], ACT.Exp,
                                     bias=nb[:, i:i + 1], scale=QK_DIM ** -0.5, accum_out=rs[:, i:i + 1]).then_inc(diff_exp, 1)
            diff_exps(0)
            for u, (b, h) in enumerate(diff_units):
                if u + 1 < len(diff_units):
                    diff_exps(u + 1)
                probs(('pd', u), (b + 1) * P)
                if h == NF - 1:
                    square(('yd', b), po[(TB + b) % 2][:, :], (pv_done, len(mem_units) + u + 1))
                if h == 0 and b >= 1:
                    features(('yd', b - 1))
            features(('yd', TB - 1))

            n_v = xn_dram.rearrange("(t p) d -> t p d", p=P)
            for b in tb:
                act_e.wait_ge(wo_added, WO[('wo1', b, 1)] + 1)
                link(act_e.activation(e_sb[:, b % 2, :, :].rearrange("p c n -> p (c n)"), x_sb[:, b, :], ACT.Square,
                                      accum_out=st_in[:, 0, TB + MB + b:TB + MB + b + 1]))
                act_e.activation(cnt[:, 15:16], st_in[:, 0, TB + MB + b:TB + MB + b + 1], ACT.Copy).then_inc(sum2, 1)
                act_e.wait_ge(scaled2, b + 1)
                act_e.dma_start(n_v[b], xs2[:, b % 2, :]).then_inc(xn_stored[b], 16)
            act_e.wait_ge(r_exp_in, 1)
            act_e.activation(rt[:, 1, :, 0:NG], rt[:, 1, :, 0:NG], ACT.Exp).then_inc(r_exp_out, 1)
            act_e.wait_ge(r_exp_in, 2)
            act_e.activation(rt[:, 5, :, 0:1], rt[:, 5, :, 0:1], ACT.Exp).then_inc(r_exp_out, 1)

            def expert(r, e, j, first, last):
                n = r * NE + e
                u = j % 2
                act_e.wait_ge(gu_done, n + 1)
                act_e.activation(silu[:, u, :], pa[u][0:CAP, 0:FE], ACT.Silu).then_inc(silu_ready, 1)
                if not first:
                    y_half(n - 1, (j - 1) % 2)
                act_e.wait_ge(ht_done, n + 1)
                act_e.activation(h_t[:, u, :, :], ps[0][:, 0:2 * CAP].rearrange("p (j s) -> p j s", j=2), ACT.Copy).then_inc(ht_ready, 1)

            def y_half(n, u):
                act_e.wait_ge(y_done, n + 1)
                act_e.wait_ge(scattered[u], n * 8 - 8 * u)
                act_e.activation(y_sb[:, u, 0:512], po[0][0:CAP, :], ACT.Copy).then_inc(y_copied0, 1)

            def round_(r):
                bodies(act_e, lambda e, j, first, last: expert(r, e, j, first, last))
                y_half(r * NE + NE - 1, (NE - 1) % 2)
            all_rounds(act_e, round_)

        @block.tensor
        def _(pe):
            def bank(banks, uses, freed, k):
                n = uses[k]
                if n >= 2:
                    pe.wait_ge(*freed(n - 2))
                return banks[n % 2]

            def transposes(k, parts, done=pt_done):
                dst = bank(pt, PT, pt_freed, k)
                for src, o in parts:
                    last = pe.transpose(dst[0:src.shape[1], o:o + src.shape[0]], src, ident[0:src.shape[0], 0:src.shape[0]])
                last.then_inc(done, 1)

            pe.wait_ge(consts, 1)
            pe.wait_ge(s_rows, 16 * 12)
            transposes(('par', 0), [(rows[0:N_ROWS, :], 0)])
            for n, rb in enumerate(in_order):
                v = xs[:, n % 2, :].rearrange("q (p k) -> q k p", k=KT)
                pe.wait_ge(in_scaled, n + 1)
                for h in range(2):
                    transposes(('in', rb, h), [(v[:, 4 * h + i, :], i * P) for i in range(4)])

            def tokens(b):
                return slice(M + b * P, M + (b + 1) * P)

            def project(k):
                name = k[0]
                w = chunk(name)
                pe.wait_ge(chunk_in[CH[name]], 16)
                dst = bank(pa, PA, pa_freed, k)
                if name[:2] == 'wo':
                    c, b, half = int(name[2]), k[1], k[2]
                    y = y_t[:, NF:2 * NF, :] if c == 2 else y_t[:, 0:NF, :]
                    if c == 0:
                        pe.wait_ge(lru_ready, NF)
                    else:
                        pe.wait_ge(feat_ready, FT[('ym' if c == 2 else 'yd', TB - 1)] + 1)
                    pairs = [(y[:, i, b * P:(b + 1) * P], w[:, i, half * 512:(half + 1) * 512]) for i in range(NF)]
                elif name in ('lx', 'lg'):
                    pe.wait_ge(in_feat, 2 * TB)
                    pairs = [(w[:, i, k[1] * P:(k[1] + 1) * P], act[:, i, M:M + S]) for i in range(KT)]
                else:
                    pe.wait_ge(in_feat, 2 * (TB + MB))
                    t = slice(k[1] * P, (k[1] + 1) * P) if name in ('mk', 'mv') else tokens(k[1])
                    pairs = [(act[:, i, t], w[:, i, :]) for i in range(KT)]
                for i, (x, y) in enumerate(pairs):
                    last = pe.matmul(dst[:, :], x, y, start=(i == 0), stop=(i == len(pairs) - 1))
                last.then_inc(pa_done, 1)
            def turn(k):
                pe.wait_ge(sc_ready, NT[k] + 1)
                v = sc[:, NT[k] % 2, :]
                transposes(k, [(v[:, i * P:(i + 1) * P], i * P) for i in range(NF)])

            for k in part_a[0:2 * NF]:
                project(k)
            pe.wait_ge(s_gw, 64)
            for g, f in scores[0:2 * NF]:
                pe.wait_ge(xc_ready, f + 1)
                dst = bank(ps, PS, ps_freed, (g, f))
                pe.matmul(dst[:, :], gates_w[:, 0 if g == 'ga' else 1, f, :], xc[:, f, :], start=True, stop=True).then_inc(ps_done, 1)

            def run(part):
                before = None
                for k in part:
                    project(k)
                    if before in SM:
                        turn(before)
                    before = k

            run(part_a[2 * NF:])

            def mem_scores(u):
                b, hp = mem_units[u]
                dst = bank(ps, PS, ps_freed, ('sm', u))
                for i in range(2):
                    last = pe.matmul(dst[:, i * M:(i + 1) * M], mq_t[:, 2 * hp + i, b * P:(b + 1) * P], mk_t[:, 2 * hp + i, :],
                                     start=True, stop=True)
                last.then_inc(ps_done, 1)

            pe.wait_ge(feat_ready, FT[('mq', TB - 1)] + 1)
            pe.wait_ge(copied, MB)
            mem_scores(0)
            for u, (b, hp) in enumerate(mem_units):
                if u + 1 < len(mem_units):
                    mem_scores(u + 1)
                pe.wait_ge(mem_exp, 2 * u + 2)
                transposes(('pm', u), [(e_sb[:, u % 2, 0, i * P:(i + 1) * P], i * P) for i in range(4)])
                if hp == 0 and b >= 1:
                    turn(('ym', b - 1))
                if hp == 0 and b >= 2:
                    pe.wait_ge(sc_ready, NT[('ym', b - 2)] + 1)
                pe.wait_ge(pt_ready, u + 1)
                for i in range(2):
                    h = 2 * hp + i
                    for t in mb:
                        last = pe.matmul(po[b % 2][:, h * HD:(h + 1) * HD], p_t[:, u % 2, (2 * i + t) * P:(2 * i + t + 1) * P],
                                         mv[:, t, h * HD:(h + 1) * HD], start=(t == 0), stop=(t == MB - 1))
                last.then_inc(pv_done, 1)
            turn(('ym', TB - 1))
            run(part_b)

            def diff_scores(u):
                b, h = diff_units[u]
                for c in range(2):
                    d = slice(64 * c, 64 * c + 64)
                    dst = bank(ps, PS, ps_freed, ('sd', u, c))
                    pe.matmul(dst[:, 0:(b + 1) * P], q_t[d, h, b * P:(b + 1) * P], k_t[d, h, 0:(b + 1) * P],
                              start=True, stop=True).then_inc(ps_done, 1)

            nm = len(mem_units)
            pe.wait_ge(feat_ready, FT[('q', TB - 1)] + 1)
            pe.wait_ge(copied, MB + TB)
            diff_scores(0)
            for u, (b, h) in enumerate(diff_units):
                if u + 1 < len(diff_units):
                    diff_scores(u + 1)
                pe.wait_ge(p_ready, u + 1)
                transposes(('pd', u), [(e_sb[:, u % 2, 0, i * P:(i + 1) * P], i * P) for i in range(b + 1)])
                if h == 0 and b >= 1:
                    turn(('yd', b - 1))
                if h == 0:
                    pe.wait_ge(sc_ready, NT[('ym', TB - 2 + b) if b < 2 else ('yd', b - 2)] + 1)
                pe.wait_ge(pt_ready, nm + u + 1)
                for t in range(b + 1):
                    last = pe.matmul(po[(TB + b) % 2][:, h * HD:(h + 1) * HD], p_t[:, (nm + u) % 2, t * P:(t + 1) * P],
                                     v_sb[:, t, h * HD:(h + 1) * HD], start=(t == 0), stop=(t == b))
                last.then_inc(pv_done, 1)
            turn(('yd', TB - 1))

            for k in wo_tiles(1):
                project(k)
            pe.wait_ge(wr_ready, 1)
            for b in tb:
                pe.wait_ge(scaled2, b + 1)
                v = xs2[:, b % 2, :].rearrange("q (p k) -> q k p", k=KT)
                for h in range(2):
                    transposes(('x2', b, h), [(v[:, 4 * h + i, :], i * P) for i in range(4)])
                pe.wait_ge(x2_ready, 2 * b + 2)
                dst = bank(ps, PS, ps_freed, ('lo', b))
                for i in range(KT):
                    last = pe.matmul(dst[:, 0:NR], x2_t[:, b % 2, i, :], wr[:, i, :], start=(i == 0), stop=(i == KT - 1))
                last.then_inc(ps_done, 1)

            pe.wait_ge(sel_ready, 1)
            for b in tb:
                dst = bank(ps, PS, ps_freed, ('cum', b))
                for c in range(b + 1):
                    last = pe.matmul(dst[:, 0:NE], tri[:, :] if c == b else ones[:, :], sel[:, c, :], start=(c == 0), stop=(c == b))
                last.then_inc(ps_done, 1)
            dst = bank(ps, PS, ps_freed, ('cnt', 0))
            for c in tb:
                last = pe.matmul(dst[:, 0:NE], ones[:, :], sel[:, c, :], start=(c == 0), stop=(c == TB - 1))
            last.then_inc(ps_done, 1)

            def x_turn(r, e, j):
                n, g = r * NE + e, j % 3
                pe.wait_ge(xg_loaded[g], gathered(r, e, j))
                pe.wait_ge(xt_ready, n)
                v = xg[:, g, :].rearrange("q (p k) -> q k p", k=KT)
                pe.transpose(pt[0][:, 0:P], v[:, 0, :], ident[:, :])
                for i in range(1, KT):
                    last = pe.transpose(pt[0][:, i * CAP:(i + 1) * CAP], v[0:CAP, i, :], ident[0:CAP, 0:CAP])
                last.then_inc(xt_done, 1)

            def down(n, j, u):
                pe.wait_ge(ht_ready, n + 1)
                pe.wait_ge(y_copied0, n)
                pe.wait_ge(y_copied1, n)
                w = expert_d(j)
                for half in range(2):
                    for i in range(2):
                        last = pe.matmul(po[half][0:CAP, :], h_t[:, u, i, :], w[:, i, half * 512:(half + 1) * 512],
                                         start=(i == 0), stop=(i == 1))
                last.then_inc(y_done, 1)

            def round_(r):
                for e in range(NE):
                    t = r * NE + e
                    pe.wait_ge(oh_ready, t + 1)
                    pe.wait_ge(tab_ready, t)
                    for b in tb:
                        last = pe.matmul(ps[1][0:CAP, 0:3], onehot[:, e % 2, b, :], tab_r[:, b, e, :], start=(b == 0), stop=(b == TB - 1))
                    last.then_inc(tab_done, 1)
                x_turn(r, 0, 0)

                def expert(e, j, first, last_):
                    n = r * NE + e
                    u = j % 2
                    pe.wait_ge(xt_ready, n + 1)
                    pe.wait_ge(expert_in[j], load_count(r, e, j))
                    if not (isinstance(n, int) and n < 2):
                        pe.wait_ge(h_ready, n - 1)
                    w = expert_gu(j)
                    for i in range(KT):
                        last = pe.matmul(pa[u][0:CAP, :].rearrange("p (w f) -> p w f", w=2), xg_t[:, u, i, :], w[:, :, i, :],
                                         start=(i == 0), stop=(i == KT - 1))
                    last.then_inc(gu_done, 1)
                    if not last_:
                        x_turn(r, e + 1, (j + 1) % UN)
                    if not first:
                        down(n - 1, (j - 1) % UN, (j - 1) % 2)
                    pe.wait_ge(h_ready, n + 1)
                    pe.wait_ge(ht_ready, n)
                    v = h_sb[:, u, :].rearrange("q (p j) -> q j p", j=2)
                    pe.transpose(ps[0][:, 0:P], v[:, 0, :], ident[:, :])
                    pe.transpose(ps[0][:, CAP:P], v[0:CAP, 1, :], ident[0:CAP, 0:CAP]).then_inc(ht_done, 1)
                bodies(pe, expert)
                down(r * NE + NE - 1, (NE - 1) % UN, (NE - 1) % 2)

            def gathered(r, e, j):
                per = 16 * len([x for x in range(NE) if x % 3 == j % 3])
                if isinstance(e, int):
                    return r * per + 16 * (e // 3 + 1)
                return r * per + (e_iter[0] * (UN // 3 * 16) + 16 * ((j if j else UN) // 3 + 1))

            def load_count(r, e, j):
                per = [len([x for x in range(NE) if x % UN == jj]) for jj in range(UN)]
                if isinstance(e, int):
                    k = e // UN
                    return r * (48 * per[j]) + 48 * (k + 1)
                return r * (48 * per[j]) + (e_iter[0] + 1) * 48
            all_rounds(pe, round_)

        @block.vector
        def _(dve):
            steps = [0]

            def link(ins):
                steps[0] += 1
                ins.then_inc(dve_step, 1)
                dve.wait_ge(dve_step, steps[0])

            dve.memset(xpad[:, :, 0:CONV], 0.0).then_inc(pads_ready, 1)
            dve.wait_ge(pt_done, PT[('par', 0)] + 1)
            dve.tensor_copy(cols[:, 0:N_ROWS], pt[0][:, 0:N_ROWS]).then_inc(cols_ready, 1)

            def scale_in(n):
                rb = in_order[n]
                src = x_sb[:, rb - MB, :] if rb >= MB else mem_sb[:, rb, :]
                dve.wait_ge(in_rstd, n + 1)
                if n >= 2:
                    dve.wait_ge(pt_done, PT[('in', in_order[n - 2], 1)] + 1)
                dve.tensor_scalar(xs[:, n % 2, :], src, st_in[:, 1, n:n + 1], None, ALU.mult).then_inc(in_scaled, 1)

            def gained(dst, k, which, h):
                return dve.tensor_tensor(dst, pt[PT[k] % 2][:, :].rearrange("p (k t) -> p k t", k=4),
                                         gain_in[:, which, 4 * h:4 * h + 4].unsqueeze(2).to_broadcast([P, 4, P]), ALU.mult)

            dve.wait_ge(s_par, 16 * 11)
            scale_in(0)
            for n, rb in enumerate(in_order):
                if n + 1 < len(in_order):
                    scale_in(n + 1)
                for h in range(2):
                    k = ('in', rb, h)
                    dve.wait_ge(pt_done, PT[k] + 1)
                    o = rb * P
                    gained(act[:, 4 * h:4 * h + 4, o:o + P], k, 1 if rb >= MB else 0, h).then_inc(in_feat, 1)

            lam_c = cols[:, C_LAM:C_LAM + NF]
            dve.wait_ge(cols_ready, 1)
            link(dve.tensor_scalar(sp[:, 2, :], lam_c, -1.0, None, ALU.mult))
            dve.tensor_tensor(sp[:, 0, :], sp[:, 2, :], lam_c, ALU.max).then_inc(abs_ready, 1)
            for n in range(2):
                link(dve.tensor_tensor(lam4[:, 2 * n, :], lam4[:, 2 * n, :], lam4[:, 2 * n + 1, :], ALU.mult))
                red = dve.tensor_reduce(lam_s[:, n:n + 1], lam4[:, 2 * n, :], AX, ALU.add)
                if n == 0:
                    link(red)
            red.then_inc(lam_sum, 1)
            dve.wait_ge(sp_exp, 1)
            link(dve.tensor_scalar(sp[:, 3, :], sp[:, 1, :], 2.0, None, ALU.add))
            link(dve.reciprocal(sp[:, 4, :], sp[:, 3, :]))
            link(dve.tensor_tensor(sp[:, 5, :], sp[:, 1, :], sp[:, 4, :], ALU.mult))
            link(dve.tensor_tensor(sp[:, 6, :], sp[:, 5, :], sp[:, 5, :], ALU.mult))
            link(dve.tensor_scalar(sp[:, 7, :], sp[:, 6, :], 1.0 / 17, None, ALU.mult))
            for c in (15, 13, 11, 9, 7, 5, 3):
                link(dve.scalar_tensor_tensor(sp[:, 7, :], sp[:, 7, :], 1.0 / c, sp[:, 6, :], ALU.add, ALU.mult))
            link(dve.scalar_tensor_tensor(sp[:, 7, :], sp[:, 7, :], 1.0, sp[:, 5, :], ALU.add, ALU.mult))
            link(dve.tensor_scalar(sp[:, 2, :], sp[:, 2, :], 0.0, None, ALU.max))
            link(dve.scalar_tensor_tensor(sp[:, 7, :], sp[:, 7, :], 2.0, sp[:, 2, :], ALU.mult, ALU.add))
            link(dve.tensor_scalar(sp[:, 8, :], sp[:, 7, :], LRU_C, None, ALU.mult))
            dve.tensor_scalar(sp[:, 9, :], sp[:, 7, :], -LRU_C, None, ALU.mult).then_inc(sp_ready, 1)
            dve.wait_ge(lam_exp, 1)
            link(dve.tensor_tensor(lam_s[:, 0:1], lam_s[:, 3:4], lam_s[:, 2:3], ALU.subtract))
            link(dve.tensor_scalar(lam_s[:, 0:1], lam_s[:, 0:1], -LAM_INIT, None, ALU.add))
            link(dve.tensor_scalar(cols[:, C_DH:C_DH + 1], cols[:, C_DH:C_DH + 1], 1.0 - LAM_INIT, None, ALU.mult))
            link(dve.tensor_copy(wr[:, :, 0:NG], wr_g[:, :, :]))
            dve.tensor_copy(wr[:, :, NG:NR], wr_e[:, :, :]).then_inc(wr_ready, 1)

            for f in range(NF):
                dve.wait_ge(xpad_ready, f + 1)
                tap = [xpad[:, f % 2, j:j + S] for j in range(CONV)]
                wcol = [cols[:, C_CONV + NF * j + f:C_CONV + NF * j + f + 1] for j in range(CONV)]
                link(dve.tensor_scalar(xc[:, f, :], tap[3], wcol[3], cols[:, C_CB + f:C_CB + f + 1], ALU.mult, ALU.add))
                for j in range(CONV - 1):
                    ins = dve.scalar_tensor_tensor(xc[:, f, :], tap[j], wcol[j], xc[:, f, :], ALU.mult, ALU.add)
                    if j < CONV - 2:
                        link(ins)
                ins.then_inc(xc_ready, 1)
            dve.wait_ge(xc_ready, NF)
            for f in range(NF):
                dve.wait_ge(a_ready, f + 1)
                link(dve.tensor_tensor(xpad[:, f % 2, 0:S], ra[:, f, :], ra[:, f, :], ALU.mult))
                dve.scalar_tensor_tensor(th[:, f, :], xpad[:, f % 2, 0:S], 1.0, th[:, f, :], ALU.add, ALU.mult).then_inc(b2_ready, 1)
            for f in range(NF):
                link(dve.tensor_tensor(ix[:, f, :], ix[:, f, :], xc[:, f, :], ALU.mult))
            for f in range(NF):
                dve.wait_ge(b_ready, f + 1)
                link(dve.tensor_tensor(ix[:, f, :], ix[:, f, :], th[:, f, :], ALU.mult))
                link(dve.tensor_tensor_scan(xc[:, f, :], ra[:, f, :], ix[:, f, :], 0.0, ALU.mult, ALU.add))
                dve.wait_ge(gelu_ready, f + 1)
                dve.tensor_tensor(y_t[:, f, :], xc[:, f, :], y_t[:, f, :], ALU.mult).then_inc(lru_ready, 1)

            def scaled(k, src, scale, g):
                n = NT[k]
                if n >= 2:
                    dve.wait_ge(pt_done, PT[normed[n - 2]] + 1)
                dve.tensor_tensor(sc[:, n % 2, :].rearrange("p (g d) -> p g d", g=g), src[:, :].rearrange("p (g d) -> p g d", g=g),
                                  scale.unsqueeze(2).to_broadcast([P, g, GW // g]), ALU.mult).then_inc(sc_ready, 1)

            def norm(k, src):
                n, g = SM[k], groups_of[k[0]]
                dve.wait_ge(sq_ready, n + 1)
                dve.tensor_reduce(st[:, 0, n, 0:g], sq[:, n % 2, :].rearrange("p (g d) -> p g d", g=g), AX, ALU.add).then_inc(ss_ready, 1)
                dve.wait_ge(rstd_ready, n + 1)
                scaled(k, src, st[:, 1, n, 0:g], g)

            def project(part):
                for k in part:
                    if k in SM:
                        norm(k, pa[PA[k] % 2])
                    if k in WO:
                        name, b, half = k
                        o = slice(half * 512, half * 512 + 512)
                        dve.wait_ge(pa_done, PA[k] + 1)
                        dve.tensor_tensor(x_sb[:, b, o], pa[PA[k] % 2][:, :], x_sb[:, b, o], ALU.add).then_inc(wo_added, 1)

            project(part_a[2 * NF:])

            def mem_max(u):
                n = PS[('sm', u)]
                dve.wait_ge(ps_done, n + 1)
                link(dve.tensor_reduce(mx[:, 2 * u:2 * u + 2], ps[n % 2][:, :].rearrange("p (i m) -> p i m", i=2), AX, ALU.max))
                dve.tensor_scalar(nb[:, 2 * u:2 * u + 2], mx[:, 2 * u:2 * u + 2], -HD ** -0.5, None, ALU.mult).then_inc(mem_nb, 1)

            mem_max(0)
            for u, (b, hp) in enumerate(mem_units):
                if u + 1 < len(mem_units):
                    mem_max(u + 1)
                if hp == 1:
                    dve.wait_ge(mem_exp, 2 * u + 2)
                    link(dve.reciprocal(rr[:, 4 * b:4 * b + 4], rs[:, 4 * b:4 * b + 4]))
                    dve.wait_ge(pv_done, u + 1)
                    scaled(('ym', b), po[b % 2], rr[:, 4 * b:4 * b + 4], 4)
            project(part_b)

            def diff_max(u):
                b, h = diff_units[u]
                n = (b + 1) * P
                for c in range(2):
                    k = PS[('sd', u, c)]
                    i = 16 + 2 * (u % 16) + c
                    dve.wait_ge(ps_done, k + 1)
                    link(dve.tensor_tensor(ps[k % 2][:, b * P:n], ps[k % 2][:, b * P:n], cmask[:, :], ALU.add))
                    link(dve.tensor_reduce(mx[:, i:i + 1], ps[k % 2][:, 0:n], AX, ALU.max))
                    dve.tensor_scalar(nb[:, i:i + 1], mx[:, i:i + 1], -QK_DIM ** -0.5, None, ALU.mult).then_inc(diff_nb, 1)

            diff_max(0)
            for u, (b, h) in enumerate(diff_units):
                if u + 1 < len(diff_units):
                    diff_max(u + 1)
                n, i = (b + 1) * P, 16 + 2 * (u % 16)
                dve.wait_ge(diff_exp, 2 * u + 2)
                link(dve.reciprocal(rr[:, i:i + 2], rs[:, i:i + 2]))
                link(dve.tensor_scalar(rr[:, i + 1:i + 2], rr[:, i + 1:i + 2], lam_s[:, 0:1], None, ALU.mult))
                link(dve.tensor_scalar(e_sb[:, u % 2, 0, 0:n], e_sb[:, u % 2, 0, 0:n], rr[:, i:i + 1], None, ALU.mult))
                dve.scalar_tensor_tensor(e_sb[:, u % 2, 0, 0:n], e_sb[:, u % 2, 1, 0:n], rr[:, i + 1:i + 2],
                                         e_sb[:, u % 2, 0, 0:n], ALU.mult, ALU.add).then_inc(p_ready, 1)
                if h == 0 and b >= 1:
                    norm(('yd', b - 1), po[(TB + b - 1) % 2])
            norm(('yd', TB - 1), po[(2 * TB - 1) % 2])
            project(wo_tiles(1))

            for b in tb:
                n = TB + MB + b
                dve.wait_ge(rstd2, b + 1)
                if b >= 2:
                    dve.wait_ge(pt_done, PT[('x2', b - 2, 1)] + 1)
                    dve.wait_ge(xn_stored[b - 2], 16)
                dve.tensor_scalar(xs2[:, b % 2, :], x_sb[:, b, :], st_in[:, 1, n:n + 1], None, ALU.mult).then_inc(scaled2, 1)
                for h in range(2):
                    k = ('x2', b, h)
                    dve.wait_ge(pt_done, PT[k] + 1)
                    if b >= 2 and h == 0:
                        dve.wait_ge(ps_done, PS[('lo', b - 2)] + 1)
                    gained(x2_t[:, b % 2, 4 * h:4 * h + 4, :], k, 2, h).then_inc(x2_ready, 1)
                dve.wait_ge(ps_done, PS[('lo', b)] + 1)
                dve.tensor_tensor(lg_sb[:, b, :], ps[PS[('lo', b)] % 2][:, 0:NR], br[:, :], ALU.add).then_inc(logits_ready, 1)
            dve.wait_ge(logits_ready, TB)

            def bc(ap, n):
                return ap.unsqueeze(2).to_broadcast([P, TB, n])
            iota8 = iota_s[:, 0:8].unsqueeze(1).to_broadcast([P, TB, 8])
            link(dve.memset(rt[:, 0, :, :], NEG))
            link(dve.tensor_copy(rt[:, 0, :, 0:NG], lg_sb[:, :, 0:NG]))
            for b in tb:
                link(dve.max(out=rt[:, 2, b, :], in_=rt[:, 0, b, :]))
                link(dve.max_index(out=rti[:, 0, b, :], in_max=rt[:, 2, b, :], in_values=rt[:, 0, b, :]))
            dve.tensor_tensor(rt[:, 1, :, 0:NG], lg_sb[:, :, 0:NG], bc(rt[:, 2, :, 0], NG), ALU.subtract).then_inc(r_exp_in, 1)
            link(dve.tensor_copy(rt[:, 3, :, 0:2], rti[:, 0, :, 0:2]))
            link(dve.tensor_tensor(rt[:, 4, :, 0:8], iota8, bc(rt[:, 3, :, 0], 8), ALU.is_equal))
            for b in tb:
                pr = rprod[:, b, :].rearrange("p (e g) -> p e g", g=NG)
                link(dve.tensor_tensor(pr, lg_sb[:, b, NG:NR].rearrange("p (g e) -> p e g", g=NG),
                                       rt[:, 4, b, 0:NG].unsqueeze(1).to_broadcast([P, NE_G, NG]), ALU.mult))
                link(dve.tensor_reduce(rt[:, 6, b, :], pr, AX, ALU.add))
                link(dve.max(out=rt[:, 7, b, :], in_=rt[:, 6, b, :]))
                link(dve.max_index(out=rti[:, 1, b, :], in_max=rt[:, 7, b, :], in_values=rt[:, 6, b, :]))
            dve.tensor_tensor(rt[:, 5, :, 0], rt[:, 7, :, 1], rt[:, 7, :, 0], ALU.subtract).then_inc(r_exp_in, 1)
            link(dve.tensor_copy(rt[:, 3, :, 2:4], rti[:, 1, :, 0:2]))
            link(dve.tensor_tensor(rt[:, 8, :, :], iota8, bc(rt[:, 3, :, 2], 8), ALU.is_equal))
            link(dve.tensor_tensor(rt[:, 9, :, :], iota8, bc(rt[:, 3, :, 3], 8), ALU.is_equal))
            dve.wait_ge(r_exp_out, 2)
            link(dve.tensor_reduce(rt[:, 3, :, 4], rt[:, 1, :, 0:NG], AX, ALU.add))
            link(dve.reciprocal(rt[:, 3, :, 4], rt[:, 3, :, 4]))
            link(dve.tensor_scalar(rt[:, 3, :, 5], rt[:, 5, :, 0], 1.0, None, ALU.add))
            link(dve.reciprocal(rt[:, 3, :, 5], rt[:, 3, :, 5]))
            link(dve.tensor_tensor(rt[:, 3, :, 5], rt[:, 3, :, 5], rt[:, 3, :, 4], ALU.mult))
            link(dve.tensor_tensor(rt[:, 3, :, 6], rt[:, 3, :, 5], rt[:, 5, :, 0], ALU.mult))
            link(dve.tensor_tensor(rt[:, 10, :, :], rt[:, 8, :, :], bc(rt[:, 3, :, 5], 8), ALU.mult))
            link(dve.tensor_tensor(rt[:, 11, :, :], rt[:, 9, :, :], bc(rt[:, 3, :, 6], 8), ALU.mult))
            link(dve.tensor_tensor(rt[:, 10, :, :], rt[:, 10, :, :], rt[:, 11, :, :], ALU.add))
            link(dve.tensor_tensor(rt[:, 8, :, :], rt[:, 8, :, :], rt[:, 9, :, :], ALU.add))
            for b in tb:
                gsel = rt[:, 4, b, 0:NG].unsqueeze(2).to_broadcast([P, NG, NE_G])
                link(dve.tensor_tensor(comb[:, b, :].rearrange("p (g e) -> p g e", g=NG), gsel,
                                       rt[:, 10, b, :].unsqueeze(1).to_broadcast([P, NG, NE_G]), ALU.mult))
                link(dve.scalar_tensor_tensor(tab_r[:, b, :, 2].rearrange("p (g e) -> p g e", g=NG), gsel, float(S),
                                              rt[:, 9, b, :].unsqueeze(1).to_broadcast([P, NG, NE_G]), ALU.mult, ALU.mult))
                ins = dve.tensor_tensor(sel[:, b, :].rearrange("p (g e) -> p g e", g=NG), gsel,
                                        rt[:, 8, b, :].unsqueeze(1).to_broadcast([P, NG, NE_G]), ALU.mult)
                if b < TB - 1:
                    link(ins)
            ins.then_inc(sel_ready, 1)
            dve.wait_ge(sel_ready, 1)
            link(dve.tensor_copy(tab_r[:, :, :, 0], bc(tok[:, :], NE)))
            link(dve.tensor_copy(tab_r[:, :, :, 1], comb[:, :, :]))
            link(dve.tensor_tensor(tab_r[:, :, :, 2], tab_r[:, :, :, 2], bc(tok[:, :], NE), ALU.add))
            for b in tb:
                n = PS[('cum', b)]
                dve.wait_ge(ps_done, n + 1)
                dve.scalar_tensor_tensor(posm[:, b, :], ps[n % 2][:, 0:NE], 1.0, sel[:, b, :], ALU.add, ALU.mult).then_inc(cum_read, 1)
            dve.wait_ge(cum_read, TB)
            link(dve.tensor_scalar(posm[:, :, :], posm[:, :, :], -1.0, None, ALU.add))
            n = PS[('cnt', 0)]
            dve.wait_ge(ps_done, n + 1)
            link(dve.tensor_reduce(cnt[:, 0:1], ps[n % 2][:, 0:NE], AX, ALU.max))
            link(dve.tensor_scalar(cnt[:, 1:9], iota_s[:, 0:8], float(CAP), cnt[:, 0:1], ALU.mult, ALU.is_lt))
            link(dve.tensor_reduce(cnt[:, 9:10], cnt[:, 1:9], AX, ALU.add))
            dve.tensor_copy(nr_i[:, :], cnt[:, 9:10]).then_inc(nr_ready, 1)
            dve.wait_ge(pa_done, PA[('v', TB - 1)] + 1)
            link(dve.memset(h_sb, 0.0))
            dve.memset(xg, 0.0).then_inc(xt_done, 3)

            def indices(n, e, j):
                dve.tensor_scalar(idx[0:CAP, j, :], tab[0:CAP, e, 0:1], BIG, None, ALU.add)
                dve.tensor_scalar(idy[0:CAP, j, :], tab[0:CAP, e, 2:3], BIG, None, ALU.add)
                dve.tensor_copy(gw[0:CAP, j, :], tab[0:CAP, e, 1:2]).then_inc(idx_ready, 1)

            def x_features(n, u):
                dve.wait_ge(xt_done, n + 4)
                dve.tensor_tensor(xg_t[:, u, :, :], pt[0][:, :].rearrange("p (k s) -> p k s", k=KT),
                                  gain_in[:, 2, :].unsqueeze(2).to_broadcast([P, KT, CAP]), ALU.mult).then_inc(xt_ready, 1)

            def y_half(n, u):
                dve.wait_ge(y_done, n + 1)
                dve.wait_ge(scattered[u], n * 8 - 8 * u)
                dve.tensor_copy(y_sb[:, u, 512:1024], po[1][0:CAP, :]).then_inc(y_copied1, 1)

            def round_(r):
                if not isinstance(r, int):
                    dve.wait_ge(tab_done, r * NE)
                    dve.tensor_scalar(posm[:, :, :], posm[:, :, :], -float(CAP), None, ALU.add).then_inc(round_done, 1)
                    dve.wait_ge(round_done, r)
                for e in range(NE + 1):
                    if e < NE:
                        t = r * NE + e
                        if e >= 2:
                            dve.wait_ge(tab_done, t - 1)
                        dve.tensor_tensor(onehot[:, e % 2, :, :], iota_s[:, :].unsqueeze(1).to_broadcast([P, TB, CAP]),
                                          posm[:, :, e].unsqueeze(2).to_broadcast([P, TB, CAP]), ALU.is_equal).then_inc(oh_ready, 1)
                    if e >= 1:
                        t = r * NE + e - 1
                        dve.wait_ge(tab_done, t + 1)
                        dve.tensor_copy(tab[0:CAP, e - 1, :], ps[1][0:CAP, 0:3]).then_inc(tab_ready, 1)
                dve.wait_ge(tab_ready, r * NE + NE)
                if not isinstance(r, int):
                    for u in range(2):
                        dve.wait_ge(scattered[u], r * (8 * NE))
                for e in range(3):
                    indices(r * NE + e, e, e)
                x_features(r * NE, 0)

                def expert(e, j, first, last):
                    n = r * NE + e
                    u = j % 2
                    if not last:
                        x_features(n + 1, (j + 1) % 2)
                    dve.wait_ge(silu_ready, n + 1)
                    dve.scalar_tensor_tensor(h_sb[0:CAP, u, :], silu[:, u, :], gw[0:CAP, j, :], pa[u][0:CAP, FE:2 * FE],
                                             ALU.mult, ALU.mult).then_inc(h_ready, 1)
                    if not first:
                        y_half(n - 1, (j - 1) % 2)
                    if isinstance(e, int) and e + 3 >= NE:
                        return
                    if not isinstance(e, int) or e + 3 >= UN:
                        dve.wait_ge(scattered[1 - u], n * 8 - 8 - 8 * (1 - u))
                    indices(n + 3, e + 3, (j + 3) % UN)
                bodies(dve, expert)
                y_half(r * NE + NE - 1, (NE - 1) % 2)
            all_rounds(dve, round_)

            for b in tb:
                for c in range(2):
                    dve.wait_ge(res_in[b][c], 16)
                    ins = dve.tensor_tensor(x_sb[:, b, :], x_sb[:, b, :], res[:, b, c, :], ALU.add)
                    if c == 0:
                        link(ins)
                ins.then_inc(res_added, 1)


def kernel(**inputs):
    import numpy as _np
    import concourse.bacc as _bacc
    from concourse import mybir as _mybir
    from concourse.bass_utils import run_bass_kernel_spmd as _run

    nc = _bacc.Bacc("TRN2", target_bir_lowering=False, num_devices=1)
    arrays, args = {}, {}
    for name in INS:
        arr = _np.ascontiguousarray(inputs[name])
        arrays[f"in_{name}"] = arr
        args[name] = nc.dram_tensor(f"in_{name}", arr.shape, _mybir.dt.from_np(arr.dtype), kind="ExternalInput").ap()
    out = nc.dram_tensor("out_0", (1, S, D), _mybir.dt.float32, kind="ExternalOutput").ap()
    build(nc, args, out)
    r = _run(nc, [arrays], core_ids=[0])
    return r.results[0]["out_0"]
```

```python
from contextlib import ExitStack

import concourse.bass as bass
from concourse import mybir

P = 128
D = 1024
KT = D // P
S = 512
TB = S // P
M = 256
MB = M // P
GW = 512
NF = GW // P
CONV = 4
LRU_BLOCK = 64
LRU_C = 8.0
QK_DIM = 64
HD = 128
NG, NE_G = 4, 8
NE = NG * NE_G
FE = 256
EPS = 1e-6
LAM_INIT = 0.2
CAP = 64
ROUNDS = S // CAP
NR = NG + NE
BIG = 2048.0
NEG = -1e30

RING = 3
SLOT = KT * 2 * FE + 2 * D
UN = 2 * RING

F32 = mybir.dt.float32
I32 = mybir.dt.int32
U32 = mybir.dt.uint32
ALU = mybir.AluOpType
ACT = mybir.ActivationFunctionType
AX = mybir.AxisListType.X

INS = ['x', 'mem', 'norm1_g', 'w_in', 'conv_w', 'conv_b', 'rg_wa', 'rg_ba', 'rg_wx', 'rg_bx', 'rg_lambda',
       'dq_norm_g', 'dk_norm_g', 'lambda_q1', 'lambda_k1', 'lambda_q2', 'lambda_k2', 'diff_head_norm_g',
       'mem_norm_g', 'w_mem_kv', 'mq_norm_g', 'mk_norm_g', 'w_out', 'norm2_g',
       'w_router_group', 'b_router_group', 'w_router_expert', 'b_router_expert',
       'w_expert_gate', 'w_expert_up', 'w_expert_down']


def build(nc, a, out):
    tb, mb = range(TB), range(MB)

    mem_units = [(b, hp) for b in tb for hp in range(2)]
    diff_units = [(b, h) for b in tb for h in range(NF)]
    in_order = (2, 3, 4, 5, 0, 1)
    per_head = ('mk', 'mq', 'k', 'q')

    def order_of_work():
        plan = [('rs', 0)]
        for n in range(TB):
            plan += [('rs', n + 1), ('rt', n)]
        plan += [('par', 0), ('tile', 'lx', 0), ('rs', TB + 1), ('tile', 'lx', 1), ('rt', TB), ('tile', 'lx', 2),
                 ('rt', TB + 1), ('tile', 'lx', 3)]
        plan += [('tile', 'lg', f) for f in range(NF)]
        pending = []

        def tile(name, i):
            plan.append(('tile', name, i))
            while pending:
                plan.append(('turn', *pending.pop()))
            if name in per_head:
                plan.append(('scale', name, i))
                pending.append((name, i))

        early = [('mk', 0), ('mk', 1), ('mq', 0), ('mq', 1), ('mq', 2), ('mq', 3), ('mv', 0), ('mv', 1)]
        for n, k in enumerate(early):
            if n < NF:
                plan += [('gate', 'ga', n), ('gate', 'gx', n)]
            if n == NF:
                plan.append(('lru_a',))
            if n == NF + 2:
                plan.append(('lru_b',))
            tile(*k)
        fill = [(name, b) for name in ('k', 'q', 'v') for b in tb]
        plan += [('ms', 0), ('me', 0)]
        for u, (b, hp) in enumerate(mem_units):
            name, i = fill.pop(0)
            plan.append(('tile', name, i))
            for k in pending:
                plan.append(('turn', *k))
            pending.clear()
            plan.append(('mt', u))
            if u + 1 < len(mem_units):
                plan += [('ms', u + 1), ('me', u + 1)]
            plan.append(('mv', u))
            if name in per_head:
                plan.append(('scale', name, i))
                pending.append((name, i))
            if hp == 1:
                plan.append(('scale', 'ym', b))
                pending.append(('ym', b))
        while fill:
            tile(*fill.pop(0))
        plan.extend(('turn', *k) for k in pending)
        pending.clear()
        two = lambda c, b: [('tile', f'wo{c}', (b, h)) for h in range(2)]
        fill = {0: two(0, 0), 1: two(0, 1), 2: two(0, 2), 3: two(0, 3), 4: two(2, 0), 5: two(2, 1),
                6: two(1, 0) + [('xs', 0)], 7: [('x2', 0)] + two(2, 2), 8: [('lo', 0)], 9: two(2, 3),
                10: two(1, 1) + [('xs', 1)], 11: [('x2', 1)], 12: [('lo', 1)], 14: two(1, 2) + [('xs', 2)],
                15: [('x2', 2)]}
        plan += [('ds', 0), ('de', 0)]
        for u, (b, h) in enumerate(diff_units):
            f = fill.get(u, [])
            plan += f[0:1]
            plan.append(('dc', u))
            plan += f[1:]
            if h == 0 and b >= 1:
                plan.append(('scale', 'yd', b - 1))
            plan.append(('dt', u))
            if u + 1 < len(diff_units):
                plan += [('ds', u + 1), ('de', u + 1)]
            plan.append(('dv', u))
            if h == 0 and b >= 1:
                plan.append(('turn', 'yd', b - 1))
        plan += [('lo', 2), ('scale', 'yd', TB - 1), ('turn', 'yd', TB - 1)] + two(1, 3) + [('xs', 3), ('x2', 3), ('lo', 3)]
        return plan

    plan = order_of_work()

    def number(keys):
        return {k: n for n, k in enumerate(keys)}

    tiles = [k[1:] for k in plan if k[0] == 'tile']
    chunks = list(dict.fromkeys(k[0] for k in tiles))
    NCH = len(chunks)
    CH = number(chunks)
    PA = number(tiles)
    normed = [k[1:] for k in plan if k[0] == 'scale']
    NT = number(normed)
    sums = [k[1:] for k in plan if (k[0] == 'tile' and k[1] in per_head) or (k[0] == 'dv' and k[1] % NF == NF - 1)]
    sums = [k if len(k) == 2 else ('yd', k[0] // NF) for k in sums]
    SM = number(sums)
    CP = number([k for k in tiles if k[0] in ('mv', 'v')])
    scores, turns = [], []
    for k in plan:
        if k[0] == 'gate':
            scores.append(k[1:])
        if k[0] == 'ms':
            scores.append(('sm', k[1]))
        if k[0] == 'ds':
            scores += [('sd', k[1], 0), ('sd', k[1], 1)]
        if k[0] == 'lo':
            scores.append(k)
        if k[0] == 'rt':
            turns += [('in', k[1], 0), ('in', k[1], 1)]
        if k[0] == 'x2':
            turns += [('x2', k[1], 0), ('x2', k[1], 1)]
        if k[0] == 'turn':
            turns.append(k[1:])
        if k[0] in ('par', 'mt', 'dt'):
            turns.append(k)
    scores += [('cum', b) for b in tb] + [('cnt', 0)]
    PS = number(scores)
    PT = number(turns)
    FT = number([k for k in turns if k in NT])
    PB = number([k for k in turns if k[0] in ('mt', 'dt')])
    IN = number([k for k in turns if k[0] == 'in'])
    X2 = number([k for k in turns if k[0] == 'x2'])
    WO = number([k for k in tiles if k[0][:2] == 'wo'])
    nm = len(mem_units)

    with ExitStack() as ctx:
        def sb(name, shape, dt=F32):
            return ctx.enter_context(nc.sbuf_tensor(name, shape, dt))

        def sem(name):
            return ctx.enter_context(nc.semaphore(name))

        pa = [ctx.enter_context(nc.psum_tensor(f"pa{i}", [P, 512], F32)) for i in range(2)]
        pt = [ctx.enter_context(nc.psum_tensor(f"pt{i}", [P, 512], F32)) for i in range(2)]
        ps = [ctx.enter_context(nc.psum_tensor(f"ps{i}", [P, 512], F32)) for i in range(2)]
        po = [ctx.enter_context(nc.psum_tensor(f"po{i}", [P, 512], F32)) for i in range(2)]

        xn_dram = nc.dram_tensor("xn_scratch", (S, D), F32, kind="Internal").ap()
        y_dram = nc.dram_tensor("y_scratch", (2 * S, D), F32, kind="Internal").ap()

        ring = sb("ring", [P, RING, SLOT])
        x_sb = sb("x_sb", [P, TB, D])
        act_t = sb("act_t", [P, KT * (M + S)])
        act = act_t[:, :].rearrange("p (k n) -> p k n", k=KT)
        sq = sb("sq", [P, 2, GW])
        sc = sb("sc", [P, 2, GW])
        y_t = sb("y_t", [P, 2 * NF, S])
        p_t = sb("p_t", [P, 2, S])
        memq = sb("memq", [P, 4096])
        mk_t = memq[:, 0:1024].rearrange("p (h m) -> p h m", h=NF)
        mv = memq[:, 1024:2048].rearrange("p (t v) -> p t v", t=MB)
        mq_t = memq[:, 2048:4096].rearrange("p (h s) -> p h s", h=NF)
        xpad = sb("xpad", [P, 2, S + CONV])
        area = sb("area", [P, 4, NF * S])
        lru = area[:, :, :].rearrange("p w (f s) -> p w f s", f=NF)
        xc, ra, ix, th = lru[:, 0], lru[:, 1], lru[:, 2], lru[:, 3]
        mem_sb = area[:, 3, :].rearrange("p (t d) -> p t d", t=2)
        xs = area[:, 2, :].rearrange("p (t d) -> p t d", t=2)
        k_t, q_t, v_sb = lru[:, 0], lru[:, 1], lru[:, 2]
        e_sb = area[:, 3, :].rearrange("p (u c n) -> p u c n", u=2, c=2)
        flat = area[:, :, :].rearrange("p w n -> p (w n)")
        xg = flat[:, 0:3 * D].rearrange("p (u d) -> p u d", u=3)
        xg_t = flat[:, 3072:4096].rearrange("p (u k s) -> p u k s", u=2, k=KT)
        silu = flat[0:CAP, 4096:4608].rearrange("p (u f) -> p u f", u=2)
        h_sb = flat[:, 4608:5120].rearrange("p (u f) -> p u f", u=2)
        h_t = flat[:, 5120:5376].rearrange("p (u j s) -> p u j s", u=2, j=2)
        y_sb = flat[0:CAP, 5376:7424].rearrange("p (u d) -> p u d", u=2)
        xs2 = act_t[:, 0:2048].rearrange("p (u d) -> p u d", u=2)
        x2_t = act_t[:, 2048:4096].rearrange("p (u k n) -> p u k n", u=2, k=KT)
        squares = act_t[:, 4096:6144].rearrange("p (u d) -> p u d", u=2)

        res = ring[:, 0:2, :].rearrange("p r n -> p (r n)")[:, 0:TB * 2 * D].rearrange("p (b c d) -> p b c d", b=TB, c=2)

        ident = sb("ident", [P, P])
        ones = sb("ones", [P, P])
        tri = sb("tri", [P, P])
        cmask = sb("cmask", [P, P])
        gates_w = sb("gates_w", [P, 2, NF, P])
        rows = sb("rows", [P, P])
        cols = sb("cols", [P, P])
        gain_in = sb("gain_in", [P, 3, KT])
        lam4 = sb("lam4", [P, 4, QK_DIM])
        lam_s = sb("lam_s", [P, 4])
        wr = sb("wr", [P, KT, NR])
        wr_g = sb("wr_g", [P, KT, NG])
        wr_e = sb("wr_e", [P, KT, NE])
        br = sb("br", [P, NR])
        sp = sb("sp", [P, 10, NF])
        half_neg = sb("half_neg", [P, 8])
        st_in = sb("st_in", [P, 2, 12])
        st = sb("st", [P, 2, len(sums), 8])
        mx = sb("mx", [P, 64])
        nb = sb("nb", [P, 64])
        rs = sb("rs", [P, 64])
        rr = sb("rr", [P, 64])
        idx_i = sb("idx_i", [P, CAP], I32)
        iota_s = sb("iota_s", [P, CAP])
        tok_i = sb("tok_i", [P, TB], I32)
        tok = sb("tok", [P, TB])
        lg_sb = sb("lg_sb", [P, TB, NR])
        spare = [0]

        def table(*shape):
            n = 1
            for x in shape:
                n *= x
            o = spare[0]
            spare[0] += n
            names = "abcd"[0:len(shape)]
            return memq[:, o:o + n].rearrange(f"p ({' '.join(names)}) -> p {' '.join(names)}",
                                              **{c: x for c, x in zip(names, shape)})
        rt = table(12, TB, 8)
        rprod = table(TB, NE)
        sel, comb, posm = table(TB, NE), table(TB, NE), table(TB, NE)
        tab_r = table(TB, NE, 3)
        onehot = table(2, TB, CAP)
        rti = sb("rti", [P, 2, TB, 8], U32)
        tab = sb("tab", [P, NE, 3])
        carrier = sb("carrier", [1, 4])
        idx = sb("idx", [P, UN, 1], U32)
        idy = sb("idy", [P, UN, 1], U32)
        gw = sb("gw", [P, UN, 1])
        nr_i = sb("nr_i", [P, 1], I32)
        cnt = sb("cnt", [P, 16])

        C_CONV, C_CB, C_BA, C_BX, C_LAM, C_DQ, C_DK, C_DH, C_MQ, C_MK, N_ROWS = 0, 16, 20, 24, 28, 32, 33, 34, 35, 36, 37
        gain_of = {'q': C_DQ, 'k': C_DK, 'yd': C_DH, 'mq': C_MQ, 'mk': C_MK}
        groups_of = {'q': 8, 'k': 8, 'yd': 4, 'mq': 4, 'mk': 4, 'ym': 4}

        s_mem = sem("s_mem")
        s_x = [sem(f"s_x{b}") for b in tb]
        s_par = sem("s_par")
        s_g1 = sem("s_g1")
        s_rows = sem("s_rows")
        s_gw = sem("s_gw")
        chunk_in = [sem(f"chunk_in{c}") for c in range(NCH)]
        expert_in = [sem(f"expert_in{j}") for j in range(UN)]
        consts, more_consts = sem("consts"), sem("more_consts")
        pool_step, act_step, dve_step = sem("pool_step"), sem("act_step"), sem("dve_step")
        pads_ready = sem("pads_ready")
        pa_done, pt_done, ps_done = sem("pa_done"), sem("pt_done"), sem("ps_done")
        cols_ready = sem("cols_ready")
        in_sum, in_rstd, in_scaled, in_feat = sem("in_sum"), sem("in_rstd"), sem("in_scaled"), sem("in_feat")
        abs_ready, sp_exp, sp_ready, lam_sum, lam_exp, lam_ready = (
            sem(n) for n in ("abs_ready", "sp_exp", "sp_ready", "lam_sum", "lam_exp", "lam_ready"))
        xpad_ready, xc_ready, gelu_ready, sig_ready, a_ready = (
            sem(n) for n in ("xpad_ready", "xc_ready", "gelu_ready", "sig_ready", "a_ready"))
        b2_ready, b_ready, lru_ready = sem("b2_ready"), sem("b_ready"), sem("lru_ready")
        sq_ready, ss_ready, rstd_ready, sc_ready, feat_ready = (
            sem(n) for n in ("sq_ready", "ss_ready", "rstd_ready", "sc_ready", "feat_ready"))
        copied = sem("copied")
        mem_nb, mem_exp, diff_nb, diff_exp, p_ready, pt_ready, pv_done = (
            sem(n) for n in ("mem_nb", "mem_exp", "diff_nb", "diff_exp", "p_ready", "pt_ready", "pv_done"))
        wo_added, x1_stored, sum2, rstd2, scaled2, x2_ready, logits_ready = (
            sem(n) for n in ("wo_added", "x1_stored", "sum2", "rstd2", "scaled2", "x2_ready", "logits_ready"))
        wr_ready, r_exp_in, r_exp_out, sel_ready, cum_read, nr_ready = (
            sem(n) for n in ("wr_ready", "r_exp_in", "r_exp_out", "sel_ready", "cum_read", "nr_ready"))
        xg_loaded = [sem(f"xg_loaded{g}") for g in range(3)]
        res_in = [[sem(f"res_in{b}_{c}") for c in range(2)] for b in tb]
        res_added, out_stored, all_scattered = sem("res_added"), sem("out_stored"), sem("all_scattered")
        carried = [sem("gather_carried"), sem("scatter_carried")]
        xn_stored = [sem(f"xn_stored{b}") for b in tb]
        oh_ready, tab_done, tab_ready = sem("oh_ready"), sem("tab_done"), sem("tab_ready")
        idx_ready, xt_done, xt_ready = (
            sem(n) for n in ("idx_ready", "xt_done", "xt_ready"))
        scattered = [sem("scattered0"), sem("scattered1")]
        gu_done, silu_ready, h_ready, ht_done, ht_ready, y_done, y_copied0, y_copied1, round_done = (
            sem(n) for n in ("gu_done", "silu_ready", "h_ready", "ht_done", "ht_ready", "y_done", "y_copied0",
                             "y_copied1", "round_done"))

        def pa_freed(n):
            k = tiles[n]
            if k[0] == 'lx':
                return xpad_ready, k[1] + 1
            if k[0] == 'lg':
                return gelu_ready, k[1] + 1
            if k in CP:
                return copied, CP[k] + 1
            if k in WO:
                return wo_added, WO[k] + 1
            return sc_ready, NT[k] + 1

        def pt_freed(n):
            k = turns[n]
            if k[0] == 'par':
                return cols_ready, 1
            if k[0] == 'in':
                return in_feat, IN[k] + 1
            if k in PB:
                return pt_ready, PB[k] + 1
            if k in X2:
                return x2_ready, X2[k] + 1
            return feat_ready, FT[k] + 1

        def ps_freed(n):
            k = scores[n]
            if k[0] in ('ga', 'gx'):
                return sig_ready, n + 1
            if k[0] == 'sm':
                return mem_exp, 2 * (k[1] + 1)
            if k[0] == 'sd':
                return diff_exp, 2 * k[1] + k[2] + 1
            if k[0] == 'lo':
                return logits_ready, k[1] + 1
            return cum_read, (k[1] if k[0] == 'cum' else TB) + 1

        w_in_v = a['w_in'][0].rearrange("(p k) n -> p k n", k=KT)
        w_kv_v = a['w_mem_kv'][0].rearrange("(p k) n -> p k n", k=KT)
        w_out_v = a['w_out'][0].rearrange("(c k p) n -> c p k n", p=P, k=NF)
        col_of = {'lx': 0, 'lg': 512, 'q': 1024, 'k': 1536, 'v': 2048, 'mq': 2560}
        wg_v = a['w_expert_gate'][0].rearrange("e (p k) f -> e p (k f)", k=KT)
        wu_v = a['w_expert_up'][0].rearrange("e (p k) f -> e p (k f)", k=KT)
        wd_v = a['w_expert_down'][0].rearrange("e (p j) n -> e p (j n)", j=2)

        def chunk(name):
            k = NF if name[:2] == 'wo' else KT
            return ring[:, CH[name] % RING, 0:KT * 512].rearrange("p (k n) -> p k n", k=k)

        def chunk_end(c):
            return max(i for i, k in enumerate(tiles) if k[0] == chunks[c]) + 1

        def slot_of(j):
            return (NCH + j) % RING

        def expert_gu(j):
            return ring[:, slot_of(j), 0:2 * KT * FE].rearrange("p (w k f) -> p w k f", w=2, k=KT)

        def expert_d(j):
            return ring[:, slot_of(j), 2 * KT * FE:SLOT].rearrange("p (j n) -> p j n", j=2)

        full = (NE - 3) // UN
        left = NE - full * UN

        def bodies(eng, body):
            for j in range(UN):
                body(j, j, j == 0, False)
            with eng.Fori(1, full) as i:
                e_iter[0] = i
                for j in range(UN):
                    body(i * UN + j, j, False, False)
            for j in range(left):
                body(full * UN + j, j % UN, False, j == left - 1)
        e_iter = [0]

        def all_rounds(eng, round_):
            round_(0)
            eng.wait_ge(nr_ready, 1)
            rounds = eng.value_load(nr_i[0:1, 0:1], min_val=0, max_val=ROUNDS)
            with eng.Fori(1, ROUNDS) as r:
                with eng.If(r < rounds):
                    round_(r)

        block = ctx.enter_context(nc.Block())

        @block.sync
        def _(sync):
            x_v = a['x'][0].rearrange("(t p) d -> t p d", p=P)
            for b in tb:
                sync.dma_start(x_sb[:, b, :], x_v[b]).then_inc(s_x[b], 16)
                if b == 0:
                    sync.dma_start(gain_in[:, 1, :], a['norm1_g'][0].rearrange("(p k) -> p k", k=KT)).then_inc(s_g1, 16)
            sync.dma_start(chunk('lx'), w_in_v[:, :, 0:512]).then_inc(chunk_in[0], 16)
            o = 0
            for src in (a['conv_w'][0].rearrange("j (f p) -> (j f) p", p=P),
                        a['conv_b'].rearrange("o (f p) -> (o f) p", p=P), a['rg_ba'].rearrange("o (f p) -> (o f) p", p=P),
                        a['rg_bx'].rearrange("o (f p) -> (o f) p", p=P), a['rg_lambda'].rearrange("o (f p) -> (o f) p", p=P)):
                n = src.shape[0]
                sync.dma_start(rows[o:o + n, :], src).then_inc(s_rows, 16)
                o += n
            for c, src in ((C_DQ, a['dq_norm_g']), (C_DK, a['dk_norm_g'])):
                for h in range(2):
                    sync.dma_start(rows[c:c + 1, 64 * h:64 * h + 64], src).then_inc(s_rows, 16)
            for c, src in ((C_DH, a['diff_head_norm_g']), (C_MQ, a['mq_norm_g']), (C_MK, a['mk_norm_g'])):
                sync.dma_start(rows[c:c + 1, :], src).then_inc(s_rows, 16)
            sync.dma_start(mem_sb, a['mem'][0].rearrange("(t p) d -> p t d", p=P)).then_inc(s_mem, 16)
            sync.dma_start(gain_in[:, 0, :], a['mem_norm_g'].rearrange("(p k) -> p k", k=KT)).then_inc(s_par, 16)
            sync.dma_start(gain_in[:, 2, :], a['norm2_g'][0].rearrange("(p k) -> p k", k=KT)).then_inc(s_par, 16)
            sync.dma_start(wr_g[:, :, :], a['w_router_group'][0].rearrange("(p k) g -> p k g", k=KT)).then_inc(s_par, 16)
            sync.dma_start(wr_e[:, :, :], a['w_router_expert'][0].rearrange("(p k) g -> p k g", k=KT)).then_inc(s_par, 16)
            sync.dma_start(br[:, 0:NG], a['b_router_group'].to_broadcast([P, NG])).then_inc(s_par, 16)
            sync.dma_start(br[:, NG:NR], a['b_router_expert'].to_broadcast([P, NE])).then_inc(s_par, 16)
            for n, w in enumerate(('lambda_q1', 'lambda_k1', 'lambda_q2', 'lambda_k2')):
                sync.dma_start(lam4[:, n, :], a[w].to_broadcast([P, QK_DIM])).then_inc(s_par, 16)
            for c, name in enumerate(chunks):
                if c == 0:
                    continue
                if c >= RING:
                    sync.wait_ge(pa_done, chunk_end(c - RING))
                if name in col_of:
                    src = w_in_v[:, :, col_of[name]:col_of[name] + 512]
                elif name in ('mk', 'mv'):
                    o = 0 if name == 'mk' else 512
                    src = w_kv_v[:, :, o:o + 512]
                else:
                    src = w_out_v[int(name[2])]
                sync.dma_start(chunk(name), src).then_inc(chunk_in[c], 16)

            def load(n, e, j):
                if isinstance(n, int) and n < RING:
                    sync.wait_ge(pa_done, chunk_end(NCH - RING + n))
                else:
                    sync.wait_ge(y_done, n - RING + 1)
                w = KT * FE
                slot = ring[:, slot_of(j), :]
                for m, src in enumerate((wg_v, wu_v, wd_v)):
                    row = src[e] if isinstance(e, int) else src[bass.ds(e, 1)].rearrange("o p n -> (o p) n")
                    sync.dma_start(slot[:, m * w:(m + 1) * w], row).then_inc(expert_in[j], 16)

            all_rounds(sync, lambda r: bodies(sync, lambda e, j, first, last: load(r * NE + e, e, j)))

            sync.wait_ge(all_scattered, 2)
            y_v = y_dram.rearrange("(c t p) d -> c t p d", c=2, p=P)
            for b in tb:
                for c in range(2):
                    sync.dma_start(res[:, b, c, :], y_v[c, b]).then_inc(res_in[b][c], 16)
            o_v = out[0].rearrange("(t p) d -> t p d", p=P)
            for b in tb:
                sync.wait_ge(res_added, b + 1)
                sync.dma_start(o_v[b], x_sb[:, b, :]).then_inc(out_stored, 16)
            sync.wait_ge(out_stored, 16 * TB)

        @block.gpsimd
        def _(pool):
            steps = [0]

            def link(ins):
                steps[0] += 1
                ins.then_inc(pool_step, 1)
                pool.wait_ge(pool_step, steps[0])

            link(pool.memset(half_neg[:, :], -0.5))
            link(pool.memset(ident[:, :], 0.0))
            pool.affine_select(out=ident[:, :], in_=ident[:, :], compare_op=ALU.not_equal, fill=1.0,
                               base=0, pattern=[[-1, P]], channel_multiplier=1).then_inc(consts, 1)

            def rsqrt(src, dst, div, const, done):
                link(pool.tensor_scalar(dst, src, div, EPS, ALU.mult, ALU.add))
                pool.tensor_tensor(dst, dst, const, ALU.pow).then_inc(done, 1)

            def more_constants():
                link(pool.memset(gates_w[:, :, :, :], 0.0))
                for g, w in enumerate((a['rg_wa'], a['rg_wx'])):
                    v = w[0].rearrange("(f h) i j -> h i f j", h=2)
                    for h in range(2):
                        pool.dma_start(gates_w[64 * h:64 * h + 64, g, :, 64 * h:64 * h + 64], v[h]).then_inc(s_gw, 16)
                link(pool.memset(ones[:, :], 1.0))
                link(pool.memset(cmask[:, :], 0.0))
                link(pool.affine_select(out=cmask[:, :], in_=cmask[:, :], compare_op=ALU.is_ge, fill=NEG,
                                        base=0, pattern=[[-1, P]], channel_multiplier=1))
                link(pool.affine_select(out=tri[:, :], in_=ones[:, :], compare_op=ALU.is_gt, fill=0.0,
                                        base=0, pattern=[[1, P]], channel_multiplier=-1))
                link(pool.iota(idx_i[:, :], pattern=[[1, CAP]], base=0, channel_multiplier=0))
                link(pool.iota(tok_i[:, :], pattern=[[P, TB]], base=-int(BIG), channel_multiplier=1))
                link(pool.tensor_copy(iota_s[:, :], idx_i[:, :]))
                pool.tensor_copy(tok[:, :], tok_i[:, :]).then_inc(more_consts, 1)

            def head_rsqrt(k):
                n, g = SM[k], groups_of[k[0]]
                pool.wait_ge(ss_ready, n + 1)
                rsqrt(st[:, 0, n, 0:g], st[:, 1, n, 0:g], g / GW, half_neg[:, 0:g], rstd_ready)

            for k in plan:
                if k[0] == 'rs':
                    n = k[1]
                    if n == TB:
                        more_constants()
                    pool.wait_ge(in_sum, n + 1)
                    rsqrt(st_in[:, 0, n:n + 1], st_in[:, 1, n:n + 1], 1.0 / D, half_neg[:, 0:1], in_rstd)
                if k[0] == 'tile' and k[1:] in SM:
                    head_rsqrt(k[1:])
                if k[0] == 'dv' and diff_units[k[1]][1] == NF - 1:
                    head_rsqrt(('yd', diff_units[k[1]][0]))
                if k[0] == 'xs':
                    n = TB + MB + k[1]
                    pool.wait_ge(sum2, k[1] + 1)
                    rsqrt(st_in[:, 0, n:n + 1], st_in[:, 1, n:n + 1], 1.0 / D, half_neg[:, 0:1], rstd2)

            for b in tb:
                pool.wait_ge(xn_stored[b], 16)

            def carry_waits(n, i):
                pool.wait_ge(carried[i], n)
                pool.tensor_tensor(carrier[0:1, i:i + 1], half_neg[0:1, 0:1], half_neg[0:1, 0:1], ALU.mult).then_inc(carried[i], 1)

            def gather(n, j):
                g = j % 3
                pool.wait_ge(idx_ready, n + 1)
                pool.wait_ge(xt_done, n + 1)
                carry_waits(n, 0)
                pool.indirect_dma_start(
                    out=xg[0:CAP, g, :], out_offset=None, in_=xn_dram,
                    in_offset=bass.IndirectOffsetOnAxis(ap=idx[0:CAP, j, :], axis=0),
                    bounds_check=S - 1, oob_is_err=False).then_inc(xg_loaded[g], 16)

            def scatter(n, j, u):
                pool.wait_ge(y_copied0, n + 1)
                pool.wait_ge(y_copied1, n + 1)
                carry_waits(n, 1)
                pool.indirect_dma_start(
                    out=y_dram, out_offset=bass.IndirectOffsetOnAxis(ap=idy[0:CAP, j, :], axis=0),
                    in_=y_sb[:, u, :], in_offset=None,
                    bounds_check=2 * S - 1, oob_is_err=False).then_inc(scattered[u], 16)

            def round_(r):
                pool.wait_ge(xt_done, r * NE + 3)
                gather(r * NE, 0)
                gather(r * NE + 1, 1)

                def expert(e, j, first, last):
                    if not isinstance(e, int) or e + 2 < NE:
                        gather(r * NE + e + 2, (j + 2) % UN)
                    if not first:
                        scatter(r * NE + e - 1, (j - 1) % UN, (j - 1) % 2)
                bodies(pool, expert)
                scatter(r * NE + NE - 1, (NE - 1) % UN, (NE - 1) % 2)
            all_rounds(pool, round_)
            rounds = pool.value_load(nr_i[0:1, 0:1], min_val=0, max_val=ROUNDS)
            for u in range(2):
                pool.wait_ge(scattered[u], rounds * (8 * NE))
                pool.tensor_tensor(carrier[0:1, 2 + u:3 + u], half_neg[0:1, 0:1], half_neg[0:1, 0:1], ALU.mult).then_inc(all_scattered, 1)

        @block.scalar
        def _(act_e):
            steps = [0]

            def link(ins):
                steps[0] += 1
                ins.then_inc(act_step, 1)
                act_e.wait_ge(act_step, steps[0])

            def row_squares(n):
                rb = in_order[n]
                if rb >= MB:
                    act_e.wait_ge(s_x[rb - MB], 16)
                    src = x_sb[:, rb - MB, :]
                else:
                    act_e.wait_ge(s_mem, 16)
                    src = mem_sb[:, rb, :]
                link(act_e.activation(y_t[:, 2 * (n % 2):2 * (n % 2) + 2, :].rearrange("p a b -> p (a b)"), src, ACT.Square,
                                      accum_out=st_in[:, 0, n:n + 1]))
                act_e.activation(cnt[:, 15:16], st_in[:, 0, n:n + 1], ACT.Copy).then_inc(in_sum, 1)

            def square(k, src, wait):
                n = SM[k]
                act_e.wait_ge(*wait)
                if n >= 2:
                    act_e.wait_ge(ss_ready, n - 1)
                act_e.activation(sq[:, n % 2, :], src, ACT.Square).then_inc(sq_ready, 1)

            def features(k):
                kind, b = k
                dst = {'mk': mk_t, 'mq': mq_t, 'k': k_t, 'q': q_t, 'yd': y_t[:, 0:NF, :], 'ym': y_t[:, NF:2 * NF, :]}[kind]
                act_e.wait_ge(pt_done, PT[k] + 1)
                if k in (('k', 0), ('q', 0)):
                    act_e.wait_ge(lru_ready, NF)
                if k == ('yd', 0):
                    act_e.wait_ge(pa_done, PA[('wo0', (TB - 1, 1))] + 1)
                src = pt[PT[k] % 2][:, :].rearrange("p (h t) -> p h t", h=NF)
                sc_ = 1.0 if kind == 'ym' else cols[:, gain_of[kind]:gain_of[kind] + 1]
                act_e.activation(dst[:, :, b * P:(b + 1) * P], src, ACT.Copy, scale=sc_).then_inc(feat_ready, 1)

            def probs(k, n):
                i = PB[k]
                act_e.wait_ge(pt_done, PT[k] + 1)
                if i >= 2:
                    act_e.wait_ge(pv_done, i - 1)
                act_e.activation(p_t[:, i % 2, 0:n], pt[PT[k] % 2][:, 0:n], ACT.Copy).then_inc(pt_ready, 1)

            def tile(k):
                act_e.wait_ge(pa_done, PA[k] + 1)
                src = pa[PA[k] % 2][:, :]
                if k[0] == 'lx':
                    f = k[1]
                    if f >= 2:
                        act_e.wait_ge(xc_ready, f - 1)
                    act_e.activation(xpad[:, f % 2, CONV - 1:CONV - 1 + S], src, ACT.Copy).then_inc(xpad_ready, 1)
                elif k[0] == 'lg':
                    act_e.activation(y_t[:, k[1], :], src, ACT.Gelu_apprx_tanh).then_inc(gelu_ready, 1)
                elif k in SM:
                    square(k, src, (pa_done, PA[k] + 1))
                elif k in CP:
                    dst = (mv if k[0] == 'mv' else v_sb)[:, k[1], :]
                    act_e.activation(dst, src, ACT.Copy).then_inc(copied, 1)

            def gate(g, f):
                n = PS[(g, f)]
                act_e.wait_ge(ps_done, n + 1)
                c = (C_BA if g == 'ga' else C_BX) + f
                dst = ra[:, f, :] if g == 'ga' else ix[:, f, :]
                act_e.activation(dst, ps[n % 2][:, :], ACT.Sigmoid, bias=cols[:, c:c + 1]).then_inc(sig_ready, 1)

            def decay():
                act_e.wait_ge(sp_ready, 1)
                act_e.wait_ge(sig_ready, 2 * NF)
                for f in range(NF):
                    act_e.activation(th[:, f, :], ra[:, f, :], ACT.Tanh, scale=sp[:, 8, f:f + 1]).then_inc(act_step, 1)
                    steps[0] += 1
                act_e.wait_ge(act_step, steps[0])
                for f in range(NF):
                    act_e.activation(ra[:, f, :], ra[:, f, :], ACT.Exp, scale=sp[:, 9, f:f + 1]).then_inc(a_ready, 1)

            def mem_exps(u):
                act_e.wait_ge(mem_nb, u + 1)
                if u == 0:
                    act_e.wait_ge(lru_ready, NF)
                if u >= 2:
                    act_e.wait_ge(pt_done, PT[('mt', u - 2)] + 1)
                for i in range(2):
                    act_e.activation(e_sb[:, u % 2, 0, i * M:(i + 1) * M], ps[PS[('sm', u)] % 2][:, i * M:(i + 1) * M],
                                     ACT.Exp, bias=nb[:, 2 * u + i:2 * u + i + 1], scale=HD ** -0.5,
                                     accum_out=rs[:, 2 * u + i:2 * u + i + 1]).then_inc(mem_exp, 1)

            def diff_exps(u):
                b, h = diff_units[u]
                n = (b + 1) * P
                for c in range(2):
                    act_e.wait_ge(diff_nb, 2 * u + c + 1)
                    if c == 0:
                        act_e.wait_ge(pt_done, PT[('dt', u - 2) if u >= 2 else ('mt', nm - 2 + u)] + 1)
                    i = 16 + 2 * (u % 16) + c
                    act_e.activation(e_sb[:, u % 2, c, 0:n], ps[PS[('sd', u, c)] % 2][:, 0:n], ACT.Exp,
                                     bias=nb[:, i:i + 1], scale=QK_DIM ** -0.5, accum_out=rs[:, i:i + 1]).then_inc(diff_exp, 1)

            n_v = xn_dram.rearrange("(t p) d -> t p d", p=P)

            def row_squares2(b):
                n = TB + MB + b
                act_e.wait_ge(wo_added, WO[('wo1', (b, 1))] + 1)
                link(act_e.activation(squares[:, b % 2, :], x_sb[:, b, :], ACT.Square, accum_out=st_in[:, 0, n:n + 1]))
                act_e.activation(cnt[:, 15:16], st_in[:, 0, n:n + 1], ACT.Copy).then_inc(sum2, 1)

            act_e.wait_ge(pads_ready, 1)
            for k in plan:
                if k[0] == 'rs':
                    row_squares(k[1])
                if k[0] == 'tile':
                    tile(k[1:])
                if k[0] == 'gate':
                    gate(*k[1:])
                if k == ('tile', 'lx', 1):
                    act_e.wait_ge(abs_ready, 1)
                    act_e.activation(sp[:, 1, :], sp[:, 0, :], ACT.Exp, scale=-1.0).then_inc(sp_exp, 1)
                    act_e.wait_ge(lam_sum, 1)
                    act_e.activation(lam_s[:, 2:4], lam_s[:, 0:2], ACT.Exp).then_inc(lam_exp, 1)
                if k[0] == 'lru_a':
                    decay()
                if k[0] == 'lru_b':
                    for f in range(NF):
                        act_e.wait_ge(b2_ready, f + 1)
                        act_e.activation(th[:, f, :], th[:, f, :], ACT.Sqrt).then_inc(b_ready, 1)
                if k[0] == 'turn':
                    features(k[1:])
                if k[0] == 'me':
                    mem_exps(k[1])
                if k[0] == 'mt':
                    probs(k, 512)
                if k[0] == 'de':
                    diff_exps(k[1])
                if k[0] == 'dt':
                    probs(k, (diff_units[k[1]][0] + 1) * P)
                if k[0] == 'dv':
                    b, h = diff_units[k[1]]
                    if h == NF - 1:
                        square(('yd', b), po[(TB + b) % 2][:, :], (pv_done, nm + k[1] + 1))
                if k[0] == 'xs':
                    row_squares2(k[1])
                if k[0] == 'x2':
                    act_e.wait_ge(scaled2, k[1] + 1)
                    act_e.dma_start(n_v[k[1]], xs2[:, k[1] % 2, :]).then_inc(xn_stored[k[1]], 16)
            act_e.wait_ge(r_exp_in, 1)
            act_e.activation(rt[:, 1, :, 0:NG], rt[:, 1, :, 0:NG], ACT.Exp).then_inc(r_exp_out, 1)
            act_e.wait_ge(r_exp_in, 2)
            act_e.activation(rt[:, 5, :, 0:1], rt[:, 5, :, 0:1], ACT.Exp).then_inc(r_exp_out, 1)

            def expert(r, e, j, first, last):
                n = r * NE + e
                u = j % 2
                act_e.wait_ge(gu_done, n + 1)
                act_e.activation(silu[:, u, :], pa[u][0:CAP, 0:FE], ACT.Silu).then_inc(silu_ready, 1)
                if not first:
                    y_half(n - 1, (j - 1) % 2)
                act_e.wait_ge(ht_done, n + 1)
                act_e.activation(h_t[:, u, :, :], ps[0][:, 0:2 * CAP].rearrange("p (j s) -> p j s", j=2), ACT.Copy).then_inc(ht_ready, 1)

            def y_half(n, u):
                act_e.wait_ge(y_done, n + 1)
                act_e.wait_ge(scattered[u], n * 8 - 8 * u)
                act_e.activation(y_sb[:, u, 0:512], po[0][0:CAP, :], ACT.Copy).then_inc(y_copied0, 1)

            def round_(r):
                bodies(act_e, lambda e, j, first, last: expert(r, e, j, first, last))
                y_half(r * NE + NE - 1, (NE - 1) % 2)
            all_rounds(act_e, round_)

        @block.tensor
        def _(pe):
            def bank(banks, uses, freed, k):
                n = uses[k]
                if n >= 2:
                    pe.wait_ge(*freed(n - 2))
                return banks[n % 2]

            def transposes(k, parts, done=pt_done):
                dst = bank(pt, PT, pt_freed, k)
                for src, o in parts:
                    last = pe.transpose(dst[0:src.shape[1], o:o + src.shape[0]], src, ident[0:src.shape[0], 0:src.shape[0]])
                last.then_inc(done, 1)

            def row_turn(n):
                v = xs[:, n % 2, :].rearrange("q (p k) -> q k p", k=KT)
                pe.wait_ge(in_scaled, n + 1)
                for h in range(2):
                    transposes(('in', n, h), [(v[:, 4 * h + i, :], i * P) for i in range(4)])

            def tokens(b):
                return slice(M + b * P, M + (b + 1) * P)

            def project(k):
                name = k[0]
                w = chunk(name)
                pe.wait_ge(chunk_in[CH[name]], 16)
                dst = bank(pa, PA, pa_freed, k)
                if name[:2] == 'wo':
                    c, (b, half) = int(name[2]), k[1]
                    y = y_t[:, NF:2 * NF, :] if c == 2 else y_t[:, 0:NF, :]
                    if c == 0:
                        pe.wait_ge(lru_ready, NF)
                    else:
                        pe.wait_ge(feat_ready, FT[('ym' if c == 2 else 'yd', b)] + 1)
                    pairs = [(y[:, i, b * P:(b + 1) * P], w[:, i, half * 512:(half + 1) * 512]) for i in range(NF)]
                elif name in ('lx', 'lg'):
                    pe.wait_ge(in_feat, 2 * TB)
                    pairs = [(w[:, i, k[1] * P:(k[1] + 1) * P], act[:, i, M:M + S]) for i in range(KT)]
                else:
                    pe.wait_ge(in_feat, 2 * (TB + MB))
                    t = slice(k[1] * P, (k[1] + 1) * P) if name in ('mk', 'mv') else tokens(k[1])
                    pairs = [(act[:, i, t], w[:, i, :]) for i in range(KT)]
                for i, (x, y) in enumerate(pairs):
                    last = pe.matmul(dst[:, :], x, y, start=(i == 0), stop=(i == len(pairs) - 1))
                last.then_inc(pa_done, 1)
            def turn(k):
                pe.wait_ge(sc_ready, NT[k] + 1)
                v = sc[:, NT[k] % 2, :]
                transposes(k, [(v[:, i * P:(i + 1) * P], i * P) for i in range(NF)])

            def gate(g, f):
                pe.wait_ge(xc_ready, f + 1)
                dst = bank(ps, PS, ps_freed, (g, f))
                pe.matmul(dst[:, :], gates_w[:, 0 if g == 'ga' else 1, f, :], xc[:, f, :], start=True, stop=True).then_inc(ps_done, 1)

            def mem_scores(u):
                b, hp = mem_units[u]
                if hp == 0:
                    pe.wait_ge(feat_ready, FT[('mq', b)] + 1)
                dst = bank(ps, PS, ps_freed, ('sm', u))
                for i in range(2):
                    last = pe.matmul(dst[:, i * M:(i + 1) * M], mq_t[:, 2 * hp + i, b * P:(b + 1) * P], mk_t[:, 2 * hp + i, :],
                                     start=True, stop=True)
                last.then_inc(ps_done, 1)

            def mem_values(u):
                b, hp = mem_units[u]
                if u == 0:
                    pe.wait_ge(copied, CP[('mv', MB - 1)] + 1)
                if hp == 0 and b >= 2:
                    pe.wait_ge(sc_ready, NT[('ym', b - 2)] + 1)
                pe.wait_ge(pt_ready, u + 1)
                for i in range(2):
                    h = 2 * hp + i
                    for t in mb:
                        last = pe.matmul(po[b % 2][:, h * HD:(h + 1) * HD], p_t[:, u % 2, (2 * i + t) * P:(2 * i + t + 1) * P],
                                         mv[:, t, h * HD:(h + 1) * HD], start=(t == 0), stop=(t == MB - 1))
                last.then_inc(pv_done, 1)

            def diff_scores(u):
                b, h = diff_units[u]
                if u == 0:
                    pe.wait_ge(feat_ready, FT[('q', TB - 1)] + 1)
                for c in range(2):
                    d = slice(64 * c, 64 * c + 64)
                    dst = bank(ps, PS, ps_freed, ('sd', u, c))
                    pe.matmul(dst[:, 0:(b + 1) * P], q_t[d, h, b * P:(b + 1) * P], k_t[d, h, 0:(b + 1) * P],
                              start=True, stop=True).then_inc(ps_done, 1)

            def diff_values(u):
                b, h = diff_units[u]
                if u == 0:
                    pe.wait_ge(copied, CP[('v', TB - 1)] + 1)
                if h == 0:
                    pe.wait_ge(sc_ready, NT[('ym', TB - 2 + b) if b < 2 else ('yd', b - 2)] + 1)
                pe.wait_ge(pt_ready, nm + u + 1)
                for t in range(b + 1):
                    last = pe.matmul(po[(TB + b) % 2][:, h * HD:(h + 1) * HD], p_t[:, (nm + u) % 2, t * P:(t + 1) * P],
                                     v_sb[:, t, h * HD:(h + 1) * HD], start=(t == 0), stop=(t == b))
                last.then_inc(pv_done, 1)

            def x2_turn(b):
                v = xs2[:, b % 2, :].rearrange("q (p k) -> q k p", k=KT)
                pe.wait_ge(scaled2, b + 1)
                for h in range(2):
                    transposes(('x2', b, h), [(v[:, 4 * h + i, :], i * P) for i in range(4)])

            def logits(b):
                pe.wait_ge(x2_ready, 2 * b + 2)
                dst = bank(ps, PS, ps_freed, ('lo', b))
                for i in range(KT):
                    last = pe.matmul(dst[:, 0:NR], x2_t[:, b % 2, i, :], wr[:, i, :], start=(i == 0), stop=(i == KT - 1))
                last.then_inc(ps_done, 1)

            pe.wait_ge(consts, 1)
            for k in plan:
                if k[0] == 'rt':
                    row_turn(k[1])
                if k[0] == 'par':
                    pe.wait_ge(s_rows, 16 * 12)
                    transposes(k, [(rows[0:N_ROWS, :], 0)])
                if k[0] == 'tile':
                    project(k[1:])
                if k[0] == 'turn':
                    turn(k[1:])
                if k[0] == 'gate':
                    if k[1:] == ('ga', 0):
                        pe.wait_ge(s_gw, 64)
                    gate(*k[1:])
                if k[0] == 'ms':
                    mem_scores(k[1])
                if k[0] == 'mt':
                    pe.wait_ge(mem_exp, 2 * k[1] + 2)
                    transposes(k, [(e_sb[:, k[1] % 2, 0, i * P:(i + 1) * P], i * P) for i in range(4)])
                if k[0] == 'mv':
                    mem_values(k[1])
                if k[0] == 'ds':
                    diff_scores(k[1])
                if k[0] == 'dt':
                    pe.wait_ge(p_ready, k[1] + 1)
                    transposes(k, [(e_sb[:, k[1] % 2, 0, i * P:(i + 1) * P], i * P) for i in range(diff_units[k[1]][0] + 1)])
                if k[0] == 'dv':
                    diff_values(k[1])
                if k[0] == 'x2':
                    x2_turn(k[1])
                if k[0] == 'lo':
                    if k[1] == 0:
                        pe.wait_ge(wr_ready, 1)
                    logits(k[1])

            pe.wait_ge(sel_ready, 1)
            for b in tb:
                dst = bank(ps, PS, ps_freed, ('cum', b))
                for c in range(b + 1):
                    last = pe.matmul(dst[:, 0:NE], tri[:, :] if c == b else ones[:, :], sel[:, c, :], start=(c == 0), stop=(c == b))
                last.then_inc(ps_done, 1)
            dst = bank(ps, PS, ps_freed, ('cnt', 0))
            for c in tb:
                last = pe.matmul(dst[:, 0:NE], ones[:, :], sel[:, c, :], start=(c == 0), stop=(c == TB - 1))
            last.then_inc(ps_done, 1)

            def x_turn(r, e, j):
                n, g = r * NE + e, j % 3
                pe.wait_ge(xg_loaded[g], gathered(r, e, j))
                pe.wait_ge(xt_ready, n)
                v = xg[:, g, :].rearrange("q (p k) -> q k p", k=KT)
                pe.transpose(pt[0][:, 0:P], v[:, 0, :], ident[:, :])
                for i in range(1, KT):
                    last = pe.transpose(pt[0][:, i * CAP:(i + 1) * CAP], v[0:CAP, i, :], ident[0:CAP, 0:CAP])
                last.then_inc(xt_done, 1)

            def down(n, j, u):
                pe.wait_ge(ht_ready, n + 1)
                pe.wait_ge(y_copied0, n)
                pe.wait_ge(y_copied1, n)
                w = expert_d(j)
                for half in range(2):
                    for i in range(2):
                        last = pe.matmul(po[half][0:CAP, :], h_t[:, u, i, :], w[:, i, half * 512:(half + 1) * 512],
                                         start=(i == 0), stop=(i == 1))
                last.then_inc(y_done, 1)

            def round_(r):
                for e in range(NE):
                    t = r * NE + e
                    pe.wait_ge(oh_ready, t + 1)
                    pe.wait_ge(tab_ready, t)
                    for b in tb:
                        last = pe.matmul(ps[1][0:CAP, 0:3], onehot[:, e % 2, b, :], tab_r[:, b, e, :], start=(b == 0), stop=(b == TB - 1))
                    last.then_inc(tab_done, 1)
                x_turn(r, 0, 0)

                def expert(e, j, first, last_):
                    n = r * NE + e
                    u = j % 2
                    pe.wait_ge(xt_ready, n + 1)
                    pe.wait_ge(expert_in[j], load_count(r, e, j))
                    if not (isinstance(n, int) and n < 2):
                        pe.wait_ge(h_ready, n - 1)
                    w = expert_gu(j)
                    for i in range(KT):
                        last = pe.matmul(pa[u][0:CAP, :].rearrange("p (w f) -> p w f", w=2), xg_t[:, u, i, :], w[:, :, i, :],
                                         start=(i == 0), stop=(i == KT - 1))
                    last.then_inc(gu_done, 1)
                    if not last_:
                        x_turn(r, e + 1, (j + 1) % UN)
                    if not first:
                        down(n - 1, (j - 1) % UN, (j - 1) % 2)
                    pe.wait_ge(h_ready, n + 1)
                    pe.wait_ge(ht_ready, n)
                    v = h_sb[:, u, :].rearrange("q (p j) -> q j p", j=2)
                    pe.transpose(ps[0][:, 0:P], v[:, 0, :], ident[:, :])
                    pe.transpose(ps[0][:, CAP:P], v[0:CAP, 1, :], ident[0:CAP, 0:CAP]).then_inc(ht_done, 1)
                bodies(pe, expert)
                down(r * NE + NE - 1, (NE - 1) % UN, (NE - 1) % 2)

            def gathered(r, e, j):
                per = 16 * len([x for x in range(NE) if x % 3 == j % 3])
                if isinstance(e, int):
                    return r * per + 16 * (e // 3 + 1)
                return r * per + (e_iter[0] * (UN // 3 * 16) + 16 * ((j if j else UN) // 3 + 1))

            def load_count(r, e, j):
                per = [len([x for x in range(NE) if x % UN == jj]) for jj in range(UN)]
                if isinstance(e, int):
                    k = e // UN
                    return r * (48 * per[j]) + 48 * (k + 1)
                return r * (48 * per[j]) + (e_iter[0] + 1) * 48
            all_rounds(pe, round_)

        @block.vector
        def _(dve):
            steps = [0]

            def link(ins):
                steps[0] += 1
                ins.then_inc(dve_step, 1)
                dve.wait_ge(dve_step, steps[0])

            dve.memset(xpad[:, :, 0:CONV], 0.0).then_inc(pads_ready, 1)

            def scale_in(n):
                rb = in_order[n]
                src = x_sb[:, rb - MB, :] if rb >= MB else mem_sb[:, rb, :]
                dve.wait_ge(in_rstd, n + 1)
                if n >= 2:
                    dve.wait_ge(pt_done, PT[('in', n - 2, 1)] + 1)
                dve.tensor_scalar(xs[:, n % 2, :], src, st_in[:, 1, n:n + 1], None, ALU.mult).then_inc(in_scaled, 1)

            def gained(dst, k, which, h):
                return dve.tensor_tensor(dst, pt[PT[k] % 2][:, :].rearrange("p (k t) -> p k t", k=4),
                                         gain_in[:, which, 4 * h:4 * h + 4].unsqueeze(2).to_broadcast([P, 4, P]), ALU.mult)

            def row_features(n):
                rb = in_order[n]
                if n == 0:
                    dve.wait_ge(s_g1, 16)
                if n == TB:
                    dve.wait_ge(s_par, 16 * 10)
                for h in range(2):
                    k = ('in', n, h)
                    dve.wait_ge(pt_done, PT[k] + 1)
                    gained(act[:, 4 * h:4 * h + 4, rb * P:(rb + 1) * P], k, 1 if rb >= MB else 0, h).then_inc(in_feat, 1)

            def parameters_1():
                lam_c = cols[:, C_LAM:C_LAM + NF]
                dve.wait_ge(pt_done, PT[('par', 0)] + 1)
                dve.tensor_copy(cols[:, 0:N_ROWS], pt[PT[('par', 0)] % 2][:, 0:N_ROWS]).then_inc(cols_ready, 1)
                dve.wait_ge(cols_ready, 1)
                link(dve.tensor_scalar(sp[:, 2, :], lam_c, -1.0, None, ALU.mult))
                dve.tensor_tensor(sp[:, 0, :], sp[:, 2, :], lam_c, ALU.max).then_inc(abs_ready, 1)
                dve.wait_ge(s_par, 16 * 10)
                for n in range(2):
                    link(dve.tensor_tensor(lam4[:, 2 * n, :], lam4[:, 2 * n, :], lam4[:, 2 * n + 1, :], ALU.mult))
                    red = dve.tensor_reduce(lam_s[:, n:n + 1], lam4[:, 2 * n, :], AX, ALU.add)
                    if n == 0:
                        link(red)
                red.then_inc(lam_sum, 1)

            def parameters_2():
                dve.wait_ge(sp_exp, 1)
                link(dve.tensor_scalar(sp[:, 3, :], sp[:, 1, :], 2.0, None, ALU.add))
                link(dve.reciprocal(sp[:, 4, :], sp[:, 3, :]))
                link(dve.tensor_tensor(sp[:, 5, :], sp[:, 1, :], sp[:, 4, :], ALU.mult))
                link(dve.tensor_tensor(sp[:, 6, :], sp[:, 5, :], sp[:, 5, :], ALU.mult))
                link(dve.tensor_scalar(sp[:, 7, :], sp[:, 6, :], 1.0 / 17, None, ALU.mult))
                for c in (15, 13, 11, 9, 7, 5, 3):
                    link(dve.scalar_tensor_tensor(sp[:, 7, :], sp[:, 7, :], 1.0 / c, sp[:, 6, :], ALU.add, ALU.mult))
                link(dve.scalar_tensor_tensor(sp[:, 7, :], sp[:, 7, :], 1.0, sp[:, 5, :], ALU.add, ALU.mult))
                link(dve.tensor_scalar(sp[:, 2, :], sp[:, 2, :], 0.0, None, ALU.max))
                link(dve.scalar_tensor_tensor(sp[:, 7, :], sp[:, 7, :], 2.0, sp[:, 2, :], ALU.mult, ALU.add))
                link(dve.tensor_scalar(sp[:, 8, :], sp[:, 7, :], LRU_C, None, ALU.mult))
                dve.tensor_scalar(sp[:, 9, :], sp[:, 7, :], -LRU_C, None, ALU.mult).then_inc(sp_ready, 1)
                dve.wait_ge(lam_exp, 1)
                link(dve.tensor_tensor(lam_s[:, 0:1], lam_s[:, 3:4], lam_s[:, 2:3], ALU.subtract))
                link(dve.tensor_scalar(lam_s[:, 0:1], lam_s[:, 0:1], -LAM_INIT, None, ALU.add))
                link(dve.tensor_scalar(cols[:, C_DH:C_DH + 1], cols[:, C_DH:C_DH + 1], 1.0 - LAM_INIT, None, ALU.mult))
                link(dve.tensor_copy(wr[:, :, 0:NG], wr_g[:, :, :]))
                dve.tensor_copy(wr[:, :, NG:NR], wr_e[:, :, :]).then_inc(wr_ready, 1)

            def convolve(f):
                dve.wait_ge(xpad_ready, f + 1)
                tap = [xpad[:, f % 2, j:j + S] for j in range(CONV)]
                wcol = [cols[:, C_CONV + NF * j + f:C_CONV + NF * j + f + 1] for j in range(CONV)]
                link(dve.tensor_scalar(xc[:, f, :], tap[3], wcol[3], cols[:, C_CB + f:C_CB + f + 1], ALU.mult, ALU.add))
                for j in range(CONV - 1):
                    ins = dve.scalar_tensor_tensor(xc[:, f, :], tap[j], wcol[j], xc[:, f, :], ALU.mult, ALU.add)
                    if j < CONV - 2:
                        link(ins)
                ins.then_inc(xc_ready, 1)

            def inputs():
                dve.wait_ge(xc_ready, NF)
                dve.wait_ge(sig_ready, 2 * NF)
                for f in range(NF):
                    link(dve.tensor_tensor(ix[:, f, :], ix[:, f, :], xc[:, f, :], ALU.mult))
                for f in range(NF):
                    dve.wait_ge(a_ready, f + 1)
                    link(dve.tensor_tensor(xpad[:, f % 2, 0:S], ra[:, f, :], ra[:, f, :], ALU.mult))
                    dve.scalar_tensor_tensor(th[:, f, :], xpad[:, f % 2, 0:S], 1.0, th[:, f, :], ALU.add, ALU.mult).then_inc(b2_ready, 1)

            def recurrence():
                for f in range(NF):
                    dve.wait_ge(b_ready, f + 1)
                    link(dve.tensor_tensor(ix[:, f, :], ix[:, f, :], th[:, f, :], ALU.mult))
                    link(dve.tensor_tensor_scan(xc[:, f, :], ra[:, f, :], ix[:, f, :], 0.0, ALU.mult, ALU.add))
                    dve.wait_ge(gelu_ready, f + 1)
                    dve.tensor_tensor(y_t[:, f, :], xc[:, f, :], y_t[:, f, :], ALU.mult).then_inc(lru_ready, 1)

            def scaled(k, src, scale, g):
                n = NT[k]
                if n >= 2:
                    dve.wait_ge(pt_done, PT[normed[n - 2]] + 1)
                dve.tensor_tensor(sc[:, n % 2, :].rearrange("p (g d) -> p g d", g=g), src[:, :].rearrange("p (g d) -> p g d", g=g),
                                  scale.unsqueeze(2).to_broadcast([P, g, GW // g]), ALU.mult).then_inc(sc_ready, 1)

            def sum_squares(k):
                n, g = SM[k], groups_of[k[0]]
                dve.wait_ge(sq_ready, n + 1)
                dve.tensor_reduce(st[:, 0, n, 0:g], sq[:, n % 2, :].rearrange("p (g d) -> p g d", g=g), AX, ALU.add).then_inc(ss_ready, 1)

            def scale(k):
                kind, b = k
                if kind == 'ym':
                    dve.wait_ge(mem_exp, 4 * b + 4)
                    link(dve.reciprocal(rr[:, 4 * b:4 * b + 4], rs[:, 4 * b:4 * b + 4]))
                    dve.wait_ge(pv_done, 2 * b + 2)
                    scaled(k, po[b % 2], rr[:, 4 * b:4 * b + 4], 4)
                else:
                    n, g = SM[k], groups_of[kind]
                    dve.wait_ge(rstd_ready, n + 1)
                    scaled(k, po[(TB + b) % 2] if kind == 'yd' else pa[PA[k] % 2], st[:, 1, n, 0:g], g)

            def tile(k):
                if k[0] == 'lx':
                    convolve(k[1])
                elif k in SM:
                    sum_squares(k)
                elif k in WO:
                    b, half = k[1]
                    o = slice(half * 512, half * 512 + 512)
                    dve.wait_ge(pa_done, PA[k] + 1)
                    dve.tensor_tensor(x_sb[:, b, o], pa[PA[k] % 2][:, :], x_sb[:, b, o], ALU.add).then_inc(wo_added, 1)

            def mem_max(u):
                n = PS[('sm', u)]
                dve.wait_ge(ps_done, n + 1)
                link(dve.tensor_reduce(mx[:, 2 * u:2 * u + 2], ps[n % 2][:, :].rearrange("p (i m) -> p i m", i=2), AX, ALU.max))
                dve.tensor_scalar(nb[:, 2 * u:2 * u + 2], mx[:, 2 * u:2 * u + 2], -HD ** -0.5, None, ALU.mult).then_inc(mem_nb, 1)

            def diff_max(u):
                b, h = diff_units[u]
                n = (b + 1) * P
                for c in range(2):
                    k = PS[('sd', u, c)]
                    i = 16 + 2 * (u % 16) + c
                    dve.wait_ge(ps_done, k + 1)
                    link(dve.tensor_tensor(ps[k % 2][:, b * P:n], ps[k % 2][:, b * P:n], cmask[:, :], ALU.add))
                    link(dve.tensor_reduce(mx[:, i:i + 1], ps[k % 2][:, 0:n], AX, ALU.max))
                    dve.tensor_scalar(nb[:, i:i + 1], mx[:, i:i + 1], -QK_DIM ** -0.5, None, ALU.mult).then_inc(diff_nb, 1)

            def difference(u):
                n, i = (diff_units[u][0] + 1) * P, 16 + 2 * (u % 16)
                dve.wait_ge(diff_exp, 2 * u + 2)
                link(dve.reciprocal(rr[:, i:i + 2], rs[:, i:i + 2]))
                link(dve.tensor_scalar(rr[:, i + 1:i + 2], rr[:, i + 1:i + 2], lam_s[:, 0:1], None, ALU.mult))
                link(dve.tensor_scalar(e_sb[:, u % 2, 0, 0:n], e_sb[:, u % 2, 0, 0:n], rr[:, i:i + 1], None, ALU.mult))
                dve.scalar_tensor_tensor(e_sb[:, u % 2, 0, 0:n], e_sb[:, u % 2, 1, 0:n], rr[:, i + 1:i + 2],
                                         e_sb[:, u % 2, 0, 0:n], ALU.mult, ALU.add).then_inc(p_ready, 1)

            def scale2(b):
                n = TB + MB + b
                dve.wait_ge(rstd2, b + 1)
                if b == 0:
                    dve.wait_ge(pa_done, PA[('v', TB - 1)] + 1)
                if b >= 2:
                    dve.wait_ge(pt_done, PT[('x2', b - 2, 1)] + 1)
                    dve.wait_ge(xn_stored[b - 2], 16)
                dve.tensor_scalar(xs2[:, b % 2, :], x_sb[:, b, :], st_in[:, 1, n:n + 1], None, ALU.mult).then_inc(scaled2, 1)

            def x2_features(b):
                if b >= 2:
                    dve.wait_ge(ps_done, PS[('lo', b - 2)] + 1)
                for h in range(2):
                    k = ('x2', b, h)
                    dve.wait_ge(pt_done, PT[k] + 1)
                    gained(x2_t[:, b % 2, 4 * h:4 * h + 4, :], k, 2, h).then_inc(x2_ready, 1)

            for k in plan:
                if k[0] == 'rs':
                    scale_in(k[1])
                if k[0] == 'rt':
                    row_features(k[1])
                if k[0] == 'par':
                    parameters_1()
                if k == ('tile', 'lx', 2):
                    parameters_2()
                if k[0] == 'tile':
                    tile(k[1:])
                if k[0] == 'lru_a':
                    inputs()
                if k[0] == 'lru_b':
                    recurrence()
                if k[0] == 'ms':
                    mem_max(k[1])
                if k[0] == 'scale':
                    scale(k[1:])
                if k[0] == 'ds':
                    diff_max(k[1])
                if k[0] == 'dc':
                    difference(k[1])
                if k[0] == 'dv' and diff_units[k[1]][1] == NF - 1:
                    sum_squares(('yd', diff_units[k[1]][0]))
                if k[0] == 'xs':
                    scale2(k[1])
                if k[0] == 'x2':
                    x2_features(k[1])
                if k[0] == 'lo':
                    b = k[1]
                    dve.wait_ge(ps_done, PS[k] + 1)
                    if b == 0:
                        dve.wait_ge(more_consts, 1)
                    dve.tensor_tensor(lg_sb[:, b, :], ps[PS[k] % 2][:, 0:NR], br[:, :], ALU.add).then_inc(logits_ready, 1)
            dve.wait_ge(logits_ready, TB)

            def bc(ap, n):
                return ap.unsqueeze(2).to_broadcast([P, TB, n])
            iota8 = iota_s[:, 0:8].unsqueeze(1).to_broadcast([P, TB, 8])
            link(dve.memset(rt[:, 0, :, :], NEG))
            link(dve.tensor_copy(rt[:, 0, :, 0:NG], lg_sb[:, :, 0:NG]))
            for b in tb:
                link(dve.max(out=rt[:, 2, b, :], in_=rt[:, 0, b, :]))
                link(dve.max_index(out=rti[:, 0, b, :], in_max=rt[:, 2, b, :], in_values=rt[:, 0, b, :]))
            dve.tensor_tensor(rt[:, 1, :, 0:NG], lg_sb[:, :, 0:NG], bc(rt[:, 2, :, 0], NG), ALU.subtract).then_inc(r_exp_in, 1)
            link(dve.tensor_copy(rt[:, 3, :, 0:2], rti[:, 0, :, 0:2]))
            link(dve.tensor_tensor(rt[:, 4, :, 0:8], iota8, bc(rt[:, 3, :, 0], 8), ALU.is_equal))
            for b in tb:
                pr = rprod[:, b, :].rearrange("p (e g) -> p e g", g=NG)
                link(dve.tensor_tensor(pr, lg_sb[:, b, NG:NR].rearrange("p (g e) -> p e g", g=NG),
                                       rt[:, 4, b, 0:NG].unsqueeze(1).to_broadcast([P, NE_G, NG]), ALU.mult))
                link(dve.tensor_reduce(rt[:, 6, b, :], pr, AX, ALU.add))
                link(dve.max(out=rt[:, 7, b, :], in_=rt[:, 6, b, :]))
                link(dve.max_index(out=rti[:, 1, b, :], in_max=rt[:, 7, b, :], in_values=rt[:, 6, b, :]))
            dve.tensor_tensor(rt[:, 5, :, 0], rt[:, 7, :, 1], rt[:, 7, :, 0], ALU.subtract).then_inc(r_exp_in, 1)
            link(dve.tensor_copy(rt[:, 3, :, 2:4], rti[:, 1, :, 0:2]))
            link(dve.tensor_tensor(rt[:, 8, :, :], iota8, bc(rt[:, 3, :, 2], 8), ALU.is_equal))
            link(dve.tensor_tensor(rt[:, 9, :, :], iota8, bc(rt[:, 3, :, 3], 8), ALU.is_equal))
            dve.wait_ge(r_exp_out, 2)
            link(dve.tensor_reduce(rt[:, 3, :, 4], rt[:, 1, :, 0:NG], AX, ALU.add))
            link(dve.reciprocal(rt[:, 3, :, 4], rt[:, 3, :, 4]))
            link(dve.tensor_scalar(rt[:, 3, :, 5], rt[:, 5, :, 0], 1.0, None, ALU.add))
            link(dve.reciprocal(rt[:, 3, :, 5], rt[:, 3, :, 5]))
            link(dve.tensor_tensor(rt[:, 3, :, 5], rt[:, 3, :, 5], rt[:, 3, :, 4], ALU.mult))
            link(dve.tensor_tensor(rt[:, 3, :, 6], rt[:, 3, :, 5], rt[:, 5, :, 0], ALU.mult))
            link(dve.tensor_tensor(rt[:, 10, :, :], rt[:, 8, :, :], bc(rt[:, 3, :, 5], 8), ALU.mult))
            link(dve.tensor_tensor(rt[:, 11, :, :], rt[:, 9, :, :], bc(rt[:, 3, :, 6], 8), ALU.mult))
            link(dve.tensor_tensor(rt[:, 10, :, :], rt[:, 10, :, :], rt[:, 11, :, :], ALU.add))
            link(dve.tensor_tensor(rt[:, 8, :, :], rt[:, 8, :, :], rt[:, 9, :, :], ALU.add))
            for b in tb:
                gsel = rt[:, 4, b, 0:NG].unsqueeze(2).to_broadcast([P, NG, NE_G])
                link(dve.tensor_tensor(comb[:, b, :].rearrange("p (g e) -> p g e", g=NG), gsel,
                                       rt[:, 10, b, :].unsqueeze(1).to_broadcast([P, NG, NE_G]), ALU.mult))
                link(dve.scalar_tensor_tensor(tab_r[:, b, :, 2].rearrange("p (g e) -> p g e", g=NG), gsel, float(S),
                                              rt[:, 9, b, :].unsqueeze(1).to_broadcast([P, NG, NE_G]), ALU.mult, ALU.mult))
                ins = dve.tensor_tensor(sel[:, b, :].rearrange("p (g e) -> p g e", g=NG), gsel,
                                        rt[:, 8, b, :].unsqueeze(1).to_broadcast([P, NG, NE_G]), ALU.mult)
                if b < TB - 1:
                    link(ins)
            ins.then_inc(sel_ready, 1)
            dve.wait_ge(sel_ready, 1)
            link(dve.tensor_copy(tab_r[:, :, :, 0], bc(tok[:, :], NE)))
            link(dve.tensor_copy(tab_r[:, :, :, 1], comb[:, :, :]))
            link(dve.tensor_tensor(tab_r[:, :, :, 2], tab_r[:, :, :, 2], bc(tok[:, :], NE), ALU.add))
            for b in tb:
                n = PS[('cum', b)]
                dve.wait_ge(ps_done, n + 1)
                dve.scalar_tensor_tensor(posm[:, b, :], ps[n % 2][:, 0:NE], 1.0, sel[:, b, :], ALU.add, ALU.mult).then_inc(cum_read, 1)
            dve.wait_ge(cum_read, TB)
            link(dve.tensor_scalar(posm[:, :, :], posm[:, :, :], -1.0, None, ALU.add))
            n = PS[('cnt', 0)]
            dve.wait_ge(ps_done, n + 1)
            link(dve.tensor_reduce(cnt[:, 0:1], ps[n % 2][:, 0:NE], AX, ALU.max))
            link(dve.tensor_scalar(cnt[:, 1:9], iota_s[:, 0:8], float(CAP), cnt[:, 0:1], ALU.mult, ALU.is_lt))
            link(dve.tensor_reduce(cnt[:, 9:10], cnt[:, 1:9], AX, ALU.add))
            dve.tensor_copy(nr_i[:, :], cnt[:, 9:10]).then_inc(nr_ready, 1)
            dve.wait_ge(pa_done, PA[('v', TB - 1)] + 1)
            link(dve.memset(h_sb, 0.0))
            dve.memset(xg, 0.0).then_inc(xt_done, 3)

            def indices(n, e, j):
                dve.tensor_scalar(idx[0:CAP, j, :], tab[0:CAP, e, 0:1], BIG, None, ALU.add)
                dve.tensor_scalar(idy[0:CAP, j, :], tab[0:CAP, e, 2:3], BIG, None, ALU.add)
                dve.tensor_copy(gw[0:CAP, j, :], tab[0:CAP, e, 1:2]).then_inc(idx_ready, 1)

            def x_features(n, u):
                dve.wait_ge(xt_done, n + 4)
                dve.tensor_tensor(xg_t[:, u, :, :], pt[0][:, :].rearrange("p (k s) -> p k s", k=KT),
                                  gain_in[:, 2, :].unsqueeze(2).to_broadcast([P, KT, CAP]), ALU.mult).then_inc(xt_ready, 1)

            def y_half(n, u):
                dve.wait_ge(y_done, n + 1)
                dve.wait_ge(scattered[u], n * 8 - 8 * u)
                dve.tensor_copy(y_sb[:, u, 512:1024], po[1][0:CAP, :]).then_inc(y_copied1, 1)

            def round_(r):
                if not isinstance(r, int):
                    dve.wait_ge(tab_done, r * NE)
                    dve.tensor_scalar(posm[:, :, :], posm[:, :, :], -float(CAP), None, ALU.add).then_inc(round_done, 1)
                    dve.wait_ge(round_done, r)
                for e in range(NE + 1):
                    if e < NE:
                        t = r * NE + e
                        if e >= 2:
                            dve.wait_ge(tab_done, t - 1)
                        dve.tensor_tensor(onehot[:, e % 2, :, :], iota_s[:, :].unsqueeze(1).to_broadcast([P, TB, CAP]),
                                          posm[:, :, e].unsqueeze(2).to_broadcast([P, TB, CAP]), ALU.is_equal).then_inc(oh_ready, 1)
                    if e >= 1:
                        t = r * NE + e - 1
                        dve.wait_ge(tab_done, t + 1)
                        dve.tensor_copy(tab[0:CAP, e - 1, :], ps[1][0:CAP, 0:3]).then_inc(tab_ready, 1)
                dve.wait_ge(tab_ready, r * NE + NE)
                if not isinstance(r, int):
                    for u in range(2):
                        dve.wait_ge(scattered[u], r * (8 * NE))
                for e in range(3):
                    indices(r * NE + e, e, e)
                x_features(r * NE, 0)

                def expert(e, j, first, last):
                    n = r * NE + e
                    u = j % 2
                    if not last:
                        x_features(n + 1, (j + 1) % 2)
                    dve.wait_ge(silu_ready, n + 1)
                    dve.scalar_tensor_tensor(h_sb[0:CAP, u, :], silu[:, u, :], gw[0:CAP, j, :], pa[u][0:CAP, FE:2 * FE],
                                             ALU.mult, ALU.mult).then_inc(h_ready, 1)
                    if not first:
                        y_half(n - 1, (j - 1) % 2)
                    if isinstance(e, int) and e + 3 >= NE:
                        return
                    if not isinstance(e, int) or e + 3 >= UN:
                        dve.wait_ge(scattered[1 - u], n * 8 - 8 - 8 * (1 - u))
                    indices(n + 3, e + 3, (j + 3) % UN)
                bodies(dve, expert)
                y_half(r * NE + NE - 1, (NE - 1) % 2)
            all_rounds(dve, round_)

            for b in tb:
                for c in range(2):
                    dve.wait_ge(res_in[b][c], 16)
                    ins = dve.tensor_tensor(x_sb[:, b, :], x_sb[:, b, :], res[:, b, c, :], ALU.add)
                    if c == 0:
                        link(ins)
                ins.then_inc(res_added, 1)


def kernel(**inputs):
    import numpy as _np
    import concourse.bacc as _bacc
    from concourse import mybir as _mybir
    from concourse.bass_utils import run_bass_kernel_spmd as _run

    nc = _bacc.Bacc("TRN2", target_bir_lowering=False, num_devices=1)
    arrays, args = {}, {}
    for name in INS:
        arr = _np.ascontiguousarray(inputs[name])
        arrays[f"in_{name}"] = arr
        args[name] = nc.dram_tensor(f"in_{name}", arr.shape, _mybir.dt.from_np(arr.dtype), kind="ExternalInput").ap()
    out = nc.dram_tensor("out_0", (1, S, D), _mybir.dt.float32, kind="ExternalOutput").ap()
    build(nc, args, out)
    r = _run(nc, [arrays], core_ids=[0])
    return r.results[0]["out_0"]
```

```python
from contextlib import ExitStack

import concourse.bass as bass
from concourse import mybir

P = 128
D = 1024
KT = D // P
S = 512
TB = S // P
M = 256
MB = M // P
GW = 512
NF = GW // P
CONV = 4
LRU_BLOCK = 64
LRU_C = 8.0
QK_DIM = 64
HD = 128
NG, NE_G = 4, 8
NE = NG * NE_G
FE = 256
EPS = 1e-6
LAM_INIT = 0.2
CAP = 64
ROUNDS = S // CAP
NR = NG + NE
BIG = 2048.0
NEG = -1e30

RING = 3
SLOT = KT * 2 * FE + 2 * D
UN = 2 * RING

QUARTERS = 4
PIECES = 3

F32 = mybir.dt.float32
F32R = mybir.dt.float32r
I32 = mybir.dt.int32
U32 = mybir.dt.uint32
ALU = mybir.AluOpType
ACT = mybir.ActivationFunctionType
AX = mybir.AxisListType.X

INS = ['x', 'mem', 'norm1_g', 'w_in', 'conv_w', 'conv_b', 'rg_wa', 'rg_ba', 'rg_wx', 'rg_bx', 'rg_lambda',
       'dq_norm_g', 'dk_norm_g', 'lambda_q1', 'lambda_k1', 'lambda_q2', 'lambda_k2', 'diff_head_norm_g',
       'mem_norm_g', 'w_mem_kv', 'mq_norm_g', 'mk_norm_g', 'w_out', 'norm2_g',
       'w_router_group', 'b_router_group', 'w_router_expert', 'b_router_expert',
       'w_expert_gate', 'w_expert_up', 'w_expert_down']


def build(nc, a, out):
    tb, mb = range(TB), range(MB)

    mem_units = [(b, hp) for b in tb for hp in range(2)]
    diff_units = [(b, h) for b in tb for h in range(NF)]
    in_order = (2, 3, 4, 5, 0, 1)
    per_head = ('mk', 'mq', 'k', 'q')
    dense = ('mk', 'mq', 'mv', 'k', 'q', 'v')

    def order_of_work():
        plan = [('rs', 0), ('rs', 1), ('rt', 0), ('rs', 2), ('rt', 1), ('rs', 3), ('split_x', 0), ('rt', 2), ('split_x', 1),
                ('rt', 3), ('split_x', 2), ('split_w', 0), ('split_x', 3), ('split_w', 1),
                ('tile', 'lx', 0), ('split_w', 2), ('par', 0), ('rs', TB), ('tile', 'lx', 1), ('split_w', 3), ('conv', 0),
                ('rs', TB + 1), ('rt', TB), ('tile', 'lx', 2), ('split_w', 4), ('conv', 1), ('split_x', TB),
                ('rt', TB + 1), ('tile', 'lx', 3), ('split_w', 5), ('conv', 2), ('split_x', TB + 1),
                ('tile', 'lg', 0), ('split_w', 6), ('conv', 3), ('tile', 'lg', 1), ('split_w', 7), ('tile', 'lg', 2)]
        plan += [('split_c', 'mk', q) for q in range(QUARTERS)]
        plan.append(('tile', 'lg', 3))
        pending = []
        def last_tile(name, i):
            if name in dense[:-2] and i == (MB if name in ('mk', 'mv') else TB) - 1:
                plan.extend(('split_c', dense[dense.index(name) + 1], q) for q in range(QUARTERS))

        def tile(name, i):
            last_tile(name, i)
            plan.append(('tile', name, i))
            while pending:
                plan.append(('turn', *pending.pop()))
            if name in per_head:
                plan.append(('scale', name, i))
                pending.append((name, i))

        early = [('mk', 0), ('mk', 1), ('mq', 0), ('mq', 1), ('mq', 2), ('mq', 3), ('mv', 0), ('mv', 1)]
        for n, k in enumerate(early):
            if n < NF:
                plan += [('gate', 'ga', n), ('gate', 'gx', n)]
            if n == NF:
                plan.append(('lru_a',))
            if n == NF + 2:
                plan.append(('lru_b',))
            tile(*k)
        two = lambda c, b: [('tile', f'wo{c}', (b, h)) for h in range(2)]
        fill = [[('tile', name, b)] for name in ('k', 'q', 'v') for b in tb]
        q_last = fill.pop(2 * TB - 1)[0]
        fill.insert(7, [])
        wo = lambda c, b, h: ('tile', f'wo{c}', (b, h))
        fill += [two(0, 0), two(0, 1), two(2, 0), two(1, 0) + [('xs', 0)],
                 [wo(0, 2, 0), ('x2', 0)], [wo(0, 2, 1), wo(2, 1, 0), ('lo', 0), ('route', 0)],
                 [wo(2, 1, 1), wo(1, 1, 0), ('weigh', 0)], [wo(1, 1, 1), wo(0, 3, 0), ('xs', 1)],
                 [wo(0, 3, 1), ('x2', 1)], [wo(2, 2, 0), ('lo', 1), ('route', 1)],
                 [wo(2, 2, 1), wo(1, 2, 0), ('weigh', 1)], [wo(1, 2, 1), ('xs', 2)]]
        units = [('m', u) for u in range(len(mem_units))] + [('d', u) for u in range(len(diff_units))]
        plan += [('ms', 0), ('me', 0)]
        for n, (kind, u) in enumerate(units):
            f = fill[n]
            if kind == 'd':
                plan.append(('dc', u))
            if f:
                last_tile(*f[0][1:])
            plan += f[0:1]
            plan.extend(('turn', *k) for k in pending)
            pending.clear()
            if kind == 'd' and u % NF == 0 and u > 0:
                plan.append(('scale', 'yd', u // NF - 1))
                pending.append(('yd', u // NF - 1))
            plan.append((kind + 't', u))
            if n + 1 < len(units):
                k, v = units[n + 1]
                plan += [(k + 's', v), (k + 'e', v)]
            plan += f[1:]
            plan.append((kind + 'v', u))
            if f and f[0][1] in per_head:
                plan.append(('scale', *f[0][1:]))
                pending.append(f[0][1:])
            if kind == 'm' and u % 2 == 1:
                plan.append(('scale', 'ym', u // 2))
                pending.append(('ym', u // 2))
            if (kind, u) == ('m', len(mem_units) - 1):
                plan += [('split_c', 'v', q) for q in range(QUARTERS)]
                tile(*q_last[1:])
        plan += [wo(2, 3, 0), ('x2', 2), ('scale', 'yd', TB - 1), ('turn', 'yd', TB - 1), wo(2, 3, 1), ('lo', 2)]
        plan += [('route', 2), ('weigh', 2)] + two(1, 3) + [('xs', 3), ('first',), ('x2', 3), ('lo', 3), ('route', 3), ('weigh', 3)]
        return plan

    plan = order_of_work()
    lru_tiles = [('lx', f) for f in range(NF)] + [('lg', f) for f in range(NF)]

    def number(keys):
        return {k: n for n, k in enumerate(keys)}

    tiles = [k[1:] for k in plan if k[0] == 'tile']
    chunks = list(dict.fromkeys(k[0] for k in tiles))
    NCH = len(chunks)
    CH = number(chunks)
    PA = number(tiles)
    normed = [k[1:] for k in plan if k[0] == 'scale']
    NT = number(normed)
    sums = [k[1:] for k in plan if (k[0] == 'tile' and k[1] in per_head) or (k[0] == 'dv' and k[1] % NF == NF - 1)]
    sums = [k if len(k) == 2 else ('yd', k[0] // NF) for k in sums]
    SM = number(sums)
    CP = number([k for k in tiles if k[0] in ('mv', 'v')])
    scores, turns = [], []
    for k in plan:
        if k[0] == 'gate':
            scores.append(k[1:])
        if k[0] == 'ms':
            scores.append(('sm', k[1]))
        if k[0] == 'ds':
            scores += [('sd', k[1], 0), ('sd', k[1], 1)]
        if k[0] == 'lo':
            scores.append(k)
        if k[0] == 'rt':
            turns += [('in', k[1], 0), ('in', k[1], 1)]
        if k[0] == 'x2':
            turns += [('x2', k[1], 0), ('x2', k[1], 1)]
        if k[0] == 'turn':
            turns.append(k[1:])
        if k[0] in ('par', 'mt', 'dt'):
            turns.append(k)
    scores += [('cum', 0), ('cnt', 0)]
    PS = number(scores)
    PT = number(turns)
    FT = number([k for k in turns if k in NT])
    PB = number([k for k in turns if k[0] in ('mt', 'dt')])
    IN = number([k for k in turns if k[0] == 'in'])
    X2 = number([k for k in turns if k[0] == 'x2'])
    WO = number([k for k in tiles if k[0][:2] == 'wo'])
    nm = len(mem_units)

    with ExitStack() as ctx:
        def sb(name, shape, dt=F32):
            return ctx.enter_context(nc.sbuf_tensor(name, shape, dt))

        def sem(name):
            return ctx.enter_context(nc.semaphore(name))

        pa = [ctx.enter_context(nc.psum_tensor(f"pa{i}", [P, 512], F32)) for i in range(2)]
        pt = [ctx.enter_context(nc.psum_tensor(f"pt{i}", [P, 512], F32)) for i in range(2)]
        ps = [ctx.enter_context(nc.psum_tensor(f"ps{i}", [P, 512], F32)) for i in range(2)]
        po = [ctx.enter_context(nc.psum_tensor(f"po{i}", [P, 512], F32)) for i in range(2)]

        xn_dram = nc.dram_tensor("xn_scratch", (S, D), F32, kind="Internal").ap()
        y_dram = nc.dram_tensor("y_scratch", (2 * S, D), F32, kind="Internal").ap()

        def twice(name, shape):
            with ExitStack() as first:
                t = first.enter_context(nc.sbuf_tensor(name, shape, F32))
            return t, sb(name + "_r", shape, F32R)

        ring, ring_r = twice("ring", [P, RING, SLOT])
        x_sb, x_sb_r = twice("x_sb", [P, TB, D])
        memq, memq_r = twice("memq", [P, 4096])
        mk_t = memq[:, 0:1024].rearrange("p (h m) -> p h m", h=NF)
        mv = memq[:, 1024:2048].rearrange("p (t v) -> p t v", t=MB)
        mq_t = memq[:, 2048:4096].rearrange("p (h s) -> p h s", h=NF)
        area = sb("area", [P, 4, NF * S])
        lru = area[:, :, :].rearrange("p w (f s) -> p w f s", f=NF)
        xc, ra, ix, th = lru[:, 0], lru[:, 1], lru[:, 2], lru[:, 3]
        mem_sb = area[:, 3, :].rearrange("p (t d) -> p t d", t=2)
        xs = area[:, 2, :].rearrange("p (t d) -> p t d", t=2)
        k_t, q_t, v_sb = lru[:, 0], lru[:, 1], lru[:, 2]
        e_sb = area[:, 3, :].rearrange("p (u c n) -> p u c n", u=2, c=2)
        flat = area[:, :, :].rearrange("p w n -> p (w n)")
        xg = flat[:, 0:3 * D].rearrange("p (u d) -> p u d", u=3)
        xg_t = flat[:, 3072:4096].rearrange("p (u k s) -> p u k s", u=2, k=KT)
        silu = flat[0:CAP, 4096:4352]
        h_sb = flat[:, 4352:4864].rearrange("p (u f) -> p u f", u=2)
        h_t = flat[:, 4864:5120].rearrange("p (u j s) -> p u j s", u=2, j=2)
        y_sb = flat[0:CAP, 5120:7168].rearrange("p (u d) -> p u d", u=2)
        gu_sum = flat[0:CAP, 7168:7680]
        gu_low = flat[0:CAP, 7680:8192]

        res = ring[:, 0:2, :].rearrange("p r n -> p (r n)")[:, 0:TB * 2 * D].rearrange("p (b c d) -> p b c d", b=TB, c=2)

        ident = sb("ident", [P, P])
        ones = sb("ones", [P, P])
        tri = sb("tri", [P, P])
        cmask = sb("cmask", [P, P])
        gates_w = sb("gates_w", [P, 2, NF, P])
        rows = sb("rows", [P, P])
        cols = sb("cols", [P, P])
        gain_in = sb("gain_in", [P, 3, KT])
        lam4 = sb("lam4", [P, 4, QK_DIM])
        lam_s = sb("lam_s", [P, 4])
        wr = sb("wr", [P, KT, NR])
        wr_g = sb("wr_g", [P, KT, NG])
        wr_e = sb("wr_e", [P, KT, NE])
        br = sb("br", [P, NR])
        sp = sb("sp", [P, 10, NF])
        half_neg = sb("half_neg", [P, 8])
        st_in = sb("st_in", [P, 2, 12])
        st = sb("st", [P, 2, len(sums), 8])
        mx = sb("mx", [P, 64])
        nb = sb("nb", [P, 64])
        rs = sb("rs", [P, 64])
        rr = sb("rr", [P, 64])
        idx_i = sb("idx_i", [P, CAP], I32)
        iota_s = sb("iota_s", [P, CAP])
        tok_i = sb("tok_i", [P, TB], I32)
        tok = sb("tok", [P, TB])
        lg_sb = sb("lg_sb", [P, TB, NR])
        spare = [0]

        def table(*shape):
            n = 1
            for x in shape:
                n *= x
            o = spare[0]
            spare[0] += n
            names = "abcd"[0:len(shape)]
            return memq[:, o:o + n].rearrange(f"p ({' '.join(names)}) -> p {' '.join(names)}",
                                              **{c: x for c, x in zip(names, shape)})
        rt = table(12, TB, 8)
        rprod = table(TB, NE)
        sel, posm = table(TB, NE), table(TB, NE)
        tab_r = table(TB, NE, 3)
        onehot = table(2, TB, CAP)
        tab_e = table(2, TB, 3)
        rti = sb("rti", [P, 2, TB, 8], U32)
        carrier = sb("carrier", [1, 4])
        idx = sb("idx", [P, UN, 1], U32)
        idy = sb("idy", [P, UN, 1], U32)
        gw = sb("gw", [P, UN, 1])
        nr_i = sb("nr_i", [P, 1], I32)
        cnt = sb("cnt", [P, 16])

        with ExitStack() as early:
            def sb_early(name, shape):
                return early.enter_context(nc.sbuf_tensor(name, shape, F32))
            act_t = sb_early("act_t", [P, KT * (M + S)])
            y_t = sb_early("y_t", [P, 2 * NF, S])
            sq = sb_early("sq", [P, 2, GW])
            sc = sb_early("sc", [P, 2, GW])
            p_t = sb_early("p_t", [P, 2, S])
            xpad = sb_early("xpad", [P, 2, S + CONV])
        act = act_t[:, :].rearrange("p (k n) -> p k n", k=KT)
        third = act_t[:, :].rearrange("p (c n) -> p c n", c=3)
        xs2 = [third[:, c, 0:D] for c in (0, 2)]
        x2_t = [third[:, c, D:2 * D].rearrange("p (k n) -> p k n", k=KT) for c in (0, 2)]
        squares = third[:, 1, :].rearrange("p (u d) -> p u d", u=2)
        w_hi = sb("w_hi", [P, PIECES, 2, KT // 2, FE], F32R)
        w_lo = sb("w_lo", [P, PIECES, 2, KT // 2, FE], F32R)
        x_hl = sb("x_hl", [P, 2, KT, 2 * CAP], F32R)
        tails = [ring_r[:, c, 2 * KT * FE:SLOT] for c in range(RING)]
        tok_hi = [t.rearrange("p (k s) -> p k s", k=KT // 2) for t in tails[0:2]]
        mem_hi = tails[2].rearrange("p (k m) -> p k m", k=KT)
        act_lo = w_hi[:, :, :, :, :].rearrange("p c w k f -> p (c w k f)").rearrange("p (k n) -> p k n", k=KT)
        in_hi = x_sb_r[:, :, :].rearrange("p b d -> p (b d)").rearrange("p (k n) -> p k n", k=KT)
        v_hi = memq_r[:, :].rearrange("p (k n) -> p k n", k=KT)
        lw = memq_r[:, :].rearrange("p (c u k f) -> p c u k f", c=2, u=2, k=KT)

        C_CONV, C_CB, C_BA, C_BX, C_LAM, C_DQ, C_DK, C_DH, C_MQ, C_MK, N_ROWS = 0, 16, 20, 24, 28, 32, 33, 34, 35, 36, 37
        gain_of = {'q': C_DQ, 'k': C_DK, 'yd': C_DH, 'mq': C_MQ, 'mk': C_MK}
        groups_of = {'q': 8, 'k': 8, 'yd': 4, 'mq': 4, 'mk': 4, 'ym': 4}

        s_mem = sem("s_mem")
        s_x = [sem(f"s_x{b}") for b in tb]
        s_par = sem("s_par")
        s_g1 = sem("s_g1")
        s_rows = sem("s_rows")
        s_gw = sem("s_gw")
        chunk_in = [sem(f"chunk_in{c}") for c in range(NCH)]
        gate_up_in = [sem(f"gate_up_in{j}") for j in range(UN)]
        down_in = [sem(f"down_in{j}") for j in range(UN)]
        xh_ready, xl_ready, lw_hi_ready, lw_lo_ready = (sem(n) for n in ("xh_ready", "xl_ready", "lw_hi_ready", "lw_lo_ready"))
        chunk_hi_ready, chunk_lo_ready, quarter_used = sem("chunk_hi_ready"), sem("chunk_lo_ready"), sem("quarter_used")
        s_x_again = [sem(f"s_x_again{b}") for b in tb]
        hi_ready, lo_ready, piece_used = sem("hi_ready"), sem("lo_ready"), sem("piece_used")
        x_hi_ready, x_lo_ready, low_ready, sum_ready = (
            sem(n) for n in ("x_hi_ready", "x_lo_ready", "low_ready", "sum_ready"))
        consts, more_consts = sem("consts"), sem("more_consts")
        pool_step, act_step, dve_step = sem("pool_step"), sem("act_step"), sem("dve_step")
        pads_ready = sem("pads_ready")
        pa_done, pt_done, ps_done = sem("pa_done"), sem("pt_done"), sem("ps_done")
        cols_ready = sem("cols_ready")
        in_sum, in_rstd, in_scaled, in_feat = sem("in_sum"), sem("in_rstd"), sem("in_scaled"), sem("in_feat")
        abs_ready, sp_exp, sp_ready, lam_sum, lam_exp = (
            sem(n) for n in ("abs_ready", "sp_exp", "sp_ready", "lam_sum", "lam_exp"))
        xpad_ready, xc_ready, gelu_ready, sig_ready, a_ready = (
            sem(n) for n in ("xpad_ready", "xc_ready", "gelu_ready", "sig_ready", "a_ready"))
        gated, scanned = sem("gated"), sem("scanned")
        b2_ready, b_ready, lru_ready = sem("b2_ready"), sem("b_ready"), sem("lru_ready")
        sq_ready, ss_ready, rstd_ready, sc_ready, feat_ready = (
            sem(n) for n in ("sq_ready", "ss_ready", "rstd_ready", "sc_ready", "feat_ready"))
        copied = sem("copied")
        mem_nb, mem_exp, diff_nb, diff_exp, p_ready, pt_ready, pv_done = (
            sem(n) for n in ("mem_nb", "mem_exp", "diff_nb", "diff_exp", "p_ready", "pt_ready", "pv_done"))
        wo_added, sum2, rstd2, scaled2, x2_ready, logits_ready = (
            sem(n) for n in ("wo_added", "sum2", "rstd2", "scaled2", "x2_ready", "logits_ready"))
        wr_ready, r_exp_in, r_exp_out, sel_ready, cum_read, nr_ready = (
            sem(n) for n in ("wr_ready", "r_exp_in", "r_exp_out", "sel_ready", "cum_read", "nr_ready"))
        xg_loaded = [sem(f"xg_loaded{g}") for g in range(3)]
        res_in = [[sem(f"res_in{b}_{c}") for c in range(2)] for b in tb]
        res_added, out_stored, all_scattered = sem("res_added"), sem("out_stored"), sem("all_scattered")
        carried = [sem("gather_carried"), sem("scatter_carried")]
        xn_stored = [sem(f"xn_stored{b}") for b in tb]
        oh_ready, tab_done = sem("oh_ready"), sem("tab_done")
        idx_ready, xt_done, xt_ready = (
            sem(n) for n in ("idx_ready", "xt_done", "xt_ready"))
        scattered = [sem("scattered0"), sem("scattered1")]
        silu_ready, h_ready, ht_done, ht_ready, y_done, y_copied0, y_copied1, round_done = (
            sem(n) for n in ("silu_ready", "h_ready", "ht_done", "ht_ready", "y_done", "y_copied0",
                             "y_copied1", "round_done"))

        count_bank = PS[('cnt', 0)] % 2
        h_bank, tab_bank = ps[count_bank], ps[1 - count_bank]

        def pa_freed(n):
            k = tiles[n]
            if k[0] == 'lx':
                return xpad_ready, k[1] + 1
            if k[0] == 'lg':
                return gelu_ready, k[1] + 1
            if k in CP:
                return copied, CP[k] + 1
            if k in WO:
                return wo_added, WO[k] + 1
            return sc_ready, NT[k] + 1

        def pt_freed(n):
            k = turns[n]
            if k[0] == 'par':
                return cols_ready, 1
            if k[0] == 'in':
                return in_feat, IN[k] + 1
            if k in PB:
                return pt_ready, PB[k] + 1
            if k in X2:
                return x2_ready, X2[k] + 1
            return feat_ready, FT[k] + 1

        def ps_freed(n):
            k = scores[n]
            if k[0] in ('ga', 'gx'):
                return sig_ready, n + 1
            if k[0] == 'sm':
                return mem_exp, 2 * (k[1] + 1)
            if k[0] == 'sd':
                return diff_exp, 2 * k[1] + k[2] + 1
            if k[0] == 'lo':
                return logits_ready, k[1] + 1
            return cum_read, 1

        w_in_v = a['w_in'][0].rearrange("(p k) n -> p k n", k=KT)
        w_kv_v = a['w_mem_kv'][0].rearrange("(p k) n -> p k n", k=KT)
        w_out_v = a['w_out'][0].rearrange("(c k p) n -> c p k n", p=P, k=NF)
        col_of = {'lx': 0, 'lg': 512, 'q': 1024, 'k': 1536, 'v': 2048, 'mq': 2560}
        wg_v = a['w_expert_gate'][0].rearrange("e (p k) f -> e p (k f)", k=KT)
        wu_v = a['w_expert_up'][0].rearrange("e (p k) f -> e p (k f)", k=KT)
        wd_v = a['w_expert_down'][0].rearrange("e (p j) n -> e p (j n)", j=2)

        def chunk(name):
            k = NF if name[:2] == 'wo' else KT
            return ring[:, CH[name] % RING, 0:KT * 512].rearrange("p (k n) -> p k n", k=k)

        def chunk_end(c):
            return max(i for i, k in enumerate(tiles) if k[0] == chunks[c]) + 1

        def chunk_lo(name):
            return ring_r[:, CH[name] % RING, 0:KT * 512].rearrange("p (k n) -> p k n", k=KT)

        def chunk_hi(name):
            return v_hi if name == 'v' else in_hi

        def input_high(n):
            rb = in_order[n]
            if rb < MB:
                return [(mem_hi[:, :, rb * P:(rb + 1) * P], 0, KT)]
            o = (rb - MB) * P
            return [(tok_hi[h][:, :, o:o + P], h * KT // 2, KT // 2) for h in range(2)]

        def lru_weights(i):
            name, f = lru_tiles[i]
            return chunk(name)[:, :, f * P:(f + 1) * P], i % 2

        def slot_of(j):
            return (NCH + j) % RING

        def expert_gu(j):
            return ring[:, slot_of(j), 0:2 * KT * FE].rearrange("p (w k f) -> p w k f", w=2, k=KT)

        def expert_d(j):
            return ring[:, slot_of(j), 2 * KT * FE:SLOT].rearrange("p (j n) -> p j n", j=2)

        full = (NE - 3) // UN
        left = NE - full * UN

        def bodies(eng, body):
            for j in range(UN):
                body(j, j, j == 0, False)
            with eng.Fori(1, full) as i:
                e_iter[0] = i
                for j in range(UN):
                    body(i * UN + j, j, False, False)
            for j in range(left):
                body(full * UN + j, j % UN, False, j == left - 1)
        e_iter = [0]

        def all_rounds(eng, round_):
            round_(0)
            eng.wait_ge(nr_ready, 1)
            rounds = eng.value_load(nr_i[0:1, 0:1], min_val=0, max_val=ROUNDS)
            with eng.Fori(1, ROUNDS) as r:
                with eng.If(r < rounds):
                    round_(r)

        def arrived(r, e, j, d, buffers, per_expert):
            b = (j + d) % buffers
            per_round = per_expert * len([x for x in range(NE) if x % buffers == b])
            if isinstance(e, int):
                return r * per_round + per_expert * ((e + d) // buffers + 1)
            return r * per_round + (e_iter[0] * (UN // buffers * per_expert) + per_expert * ((j + d) // buffers + 1))

        def exists(e, d):
            return not isinstance(e, int) or e + d < NE

        def gate_up_raw(j, half):
            k = KT // 2
            return expert_gu(j)[:, :, half * k:(half + 1) * k, :]

        def split(eng, r, e, j, d, half, write):
            if not exists(e, d):
                return
            if half == 0:
                eng.wait_ge(gate_up_in[(j + d) % UN], arrived(r, e, j, d, UN, 32))
            if not isinstance(e, int) or 2 * (e + d) + half >= PIECES:
                eng.wait_ge(piece_used, 2 * (r * NE + e) + (2 * d + half - PIECES + 1))
            write((2 * (j + d) + half) % PIECES, gate_up_raw((j + d) % UN, half))

        block = ctx.enter_context(nc.Block())

        @block.sync
        def _(sync):
            x_v = a['x'][0].rearrange("(t p) d -> t p d", p=P)
            for b in tb:
                sync.dma_start(x_sb[:, b, :], x_v[b]).then_inc(s_x[b], 16)
                if b == 0:
                    sync.dma_start(gain_in[:, 1, :], a['norm1_g'][0].rearrange("(p k) -> p k", k=KT)).then_inc(s_g1, 16)
            sync.dma_start(chunk('lx'), w_in_v[:, :, 0:512]).then_inc(chunk_in[0], 16)
            o = 0
            for src in (a['conv_w'][0].rearrange("j (f p) -> (j f) p", p=P),
                        a['conv_b'].rearrange("o (f p) -> (o f) p", p=P), a['rg_ba'].rearrange("o (f p) -> (o f) p", p=P),
                        a['rg_bx'].rearrange("o (f p) -> (o f) p", p=P), a['rg_lambda'].rearrange("o (f p) -> (o f) p", p=P)):
                n = src.shape[0]
                sync.dma_start(rows[o:o + n, :], src).then_inc(s_rows, 16)
                o += n
            for c, src in ((C_DQ, a['dq_norm_g']), (C_DK, a['dk_norm_g'])):
                for h in range(2):
                    sync.dma_start(rows[c:c + 1, 64 * h:64 * h + 64], src).then_inc(s_rows, 16)
            for c, src in ((C_DH, a['diff_head_norm_g']), (C_MQ, a['mq_norm_g']), (C_MK, a['mk_norm_g'])):
                sync.dma_start(rows[c:c + 1, :], src).then_inc(s_rows, 16)
            sync.dma_start(mem_sb, a['mem'][0].rearrange("(t p) d -> p t d", p=P)).then_inc(s_mem, 16)
            sync.dma_start(gain_in[:, 0, :], a['mem_norm_g'].rearrange("(p k) -> p k", k=KT)).then_inc(s_par, 16)
            sync.dma_start(gain_in[:, 2, :], a['norm2_g'][0].rearrange("(p k) -> p k", k=KT)).then_inc(s_par, 16)
            sync.dma_start(wr_g[:, :, :], a['w_router_group'][0].rearrange("(p k) g -> p k g", k=KT)).then_inc(s_par, 16)
            sync.dma_start(wr_e[:, :, :], a['w_router_expert'][0].rearrange("(p k) g -> p k g", k=KT)).then_inc(s_par, 16)
            sync.dma_start(br[:, 0:NG], a['b_router_group'].to_broadcast([P, NG])).then_inc(s_par, 16)
            sync.dma_start(br[:, NG:NR], a['b_router_expert'].to_broadcast([P, NE])).then_inc(s_par, 16)
            for n, w in enumerate(('lambda_q1', 'lambda_k1', 'lambda_q2', 'lambda_k2')):
                sync.dma_start(lam4[:, n, :], a[w].to_broadcast([P, QK_DIM])).then_inc(s_par, 16)
            def row_of(v, e):
                return v[e] if isinstance(e, int) else v[bass.ds(e, 1)].rearrange("o p n -> (o p) n")
            w = KT * FE

            for c, name in enumerate(chunks):
                if c == 0:
                    continue
                if c >= RING:
                    sync.wait_ge(pa_done, chunk_end(c - RING))
                if name in col_of:
                    src = w_in_v[:, :, col_of[name]:col_of[name] + 512]
                elif name in ('mk', 'mv'):
                    o = 0 if name == 'mk' else 512
                    src = w_kv_v[:, :, o:o + 512]
                else:
                    src = w_out_v[int(name[2])]
                if c == CH['q'] + RING:
                    for b in tb:
                        sync.dma_start(x_sb[:, b, :], x_v[b]).then_inc(s_x_again[b], 16)
                sync.dma_start(chunk(name), src).then_inc(chunk_in[c], 16)
                if c == CH['v'] + RING:
                    for e in range(RING):
                        sync.dma_start(ring[:, slot_of(e), 2 * w:3 * w], row_of(wd_v, e)).then_inc(down_in[e], 16)

            def load_gate_up(r, e, j, d):
                if not exists(e, d):
                    return
                n = e + d
                if isinstance(r, int) and isinstance(n, int) and n < RING:
                    sync.wait_ge(pa_done, chunk_end(NCH - RING + n))
                elif not isinstance(n, int) or n >= RING:
                    sync.wait_ge(hi_ready, r * (2 * NE) + n * 2 - (2 * RING - 2))
                    sync.wait_ge(lo_ready, r * (2 * NE) + n * 2 - (2 * RING - 2))
                slot = ring[:, slot_of((j + d) % UN), :]
                for m, v in enumerate((wg_v, wu_v)):
                    sync.dma_start(slot[:, m * w:(m + 1) * w], row_of(v, n)).then_inc(gate_up_in[(j + d) % UN], 16)

            def load_down(r, e, j):
                if isinstance(r, int) and isinstance(e, int) and e < RING:
                    return
                if not isinstance(e, int) or e >= RING:
                    sync.wait_ge(y_done, r * NE + e - (RING - 1))
                sync.dma_start(ring[:, slot_of(j), 2 * w:3 * w], row_of(wd_v, e)).then_inc(down_in[j], 16)

            def weights(r):
                if not isinstance(r, int):
                    sync.wait_ge(y_done, r * NE)
                load_gate_up(r, 0, 0, 0)

                def expert(e, j, first, last):
                    load_gate_up(r, e, j, 1)
                    load_down(r, e, j)
                bodies(sync, expert)
            all_rounds(sync, weights)

            sync.wait_ge(all_scattered, 2)
            y_v = y_dram.rearrange("(c t p) d -> c t p d", c=2, p=P)
            for b in tb:
                for c in range(2):
                    sync.dma_start(res[:, b, c, :], y_v[c, b]).then_inc(res_in[b][c], 16)
            o_v = out[0].rearrange("(t p) d -> t p d", p=P)
            for b in tb:
                sync.wait_ge(res_added, b + 1)
                sync.dma_start(o_v[b], x_sb[:, b, :]).then_inc(out_stored, 16)
            sync.wait_ge(out_stored, 16 * TB)

        @block.gpsimd
        def _(pool):
            steps = [0]

            def link(ins):
                steps[0] += 1
                ins.then_inc(pool_step, 1)
                pool.wait_ge(pool_step, steps[0])

            link(pool.memset(half_neg[:, :], -0.5))
            link(pool.memset(ident[:, :], 0.0))
            pool.affine_select(out=ident[:, :], in_=ident[:, :], compare_op=ALU.not_equal, fill=1.0,
                               base=0, pattern=[[-1, P]], channel_multiplier=1).then_inc(consts, 1)

            def rsqrt(src, dst, div, const, done):
                link(pool.tensor_scalar(dst, src, div, EPS, ALU.mult, ALU.add))
                pool.tensor_tensor(dst, dst, const, ALU.pow).then_inc(done, 1)

            def more_constants():
                link(pool.memset(gates_w[:, :, :, :], 0.0))
                for g, w in enumerate((a['rg_wa'], a['rg_wx'])):
                    v = w[0].rearrange("(f h) i j -> h i f j", h=2)
                    for h in range(2):
                        pool.dma_start(gates_w[64 * h:64 * h + 64, g, :, 64 * h:64 * h + 64], v[h]).then_inc(s_gw, 16)
                link(pool.memset(ones[:, :], 1.0))
                link(pool.memset(cmask[:, :], 0.0))
                link(pool.affine_select(out=cmask[:, :], in_=cmask[:, :], compare_op=ALU.is_ge, fill=NEG,
                                        base=0, pattern=[[-1, P]], channel_multiplier=1))
                link(pool.affine_select(out=tri[:, :], in_=ones[:, :], compare_op=ALU.is_gt, fill=0.0,
                                        base=0, pattern=[[1, P]], channel_multiplier=-1))
                link(pool.iota(idx_i[:, :], pattern=[[1, CAP]], base=0, channel_multiplier=0))
                link(pool.iota(tok_i[:, :], pattern=[[P, TB]], base=-int(BIG), channel_multiplier=1))
                link(pool.tensor_copy(iota_s[:, :], idx_i[:, :]))
                pool.tensor_copy(tok[:, :], tok_i[:, :]).then_inc(more_consts, 1)

            def head_rsqrt(k):
                n, g = SM[k], groups_of[k[0]]
                pool.wait_ge(ss_ready, n + 1)
                rsqrt(st[:, 0, n, 0:g], st[:, 1, n, 0:g], g / GW, half_neg[:, 0:g], rstd_ready)

            for k in plan:
                if k[0] == 'rs':
                    n = k[1]
                    if n == TB:
                        more_constants()
                    pool.wait_ge(in_sum, n + 1)
                    rsqrt(st_in[:, 0, n:n + 1], st_in[:, 1, n:n + 1], 1.0 / D, half_neg[:, 0:1], in_rstd)
                if k[0] == 'split_w' and k[1] < 2:
                    raw, u = lru_weights(k[1])
                    pool.wait_ge(lw_hi_ready, k[1] + 1)
                    pool.tensor_tensor(lw[:, 1, u, :, :], raw, lw[:, 0, u, :, :], ALU.subtract).then_inc(lw_lo_ready, 1)
                if k[0] == 'gate' and k[1] == 'gx':
                    f = k[2]
                    pool.wait_ge(sig_ready, PS[('gx', f)] + 1)
                    pool.wait_ge(xc_ready, f + 1)
                    pool.tensor_tensor(ix[:, f, :], ix[:, f, :], xc[:, f, :], ALU.mult).then_inc(gated, 1)
                if k[0] == 'lru_b':
                    for f in range(NF):
                        pool.wait_ge(scanned, f + 1)
                        pool.wait_ge(gelu_ready, f + 1)
                        pool.tensor_tensor(y_t[:, f, :], xc[:, f, :], y_t[:, f, :], ALU.mult).then_inc(lru_ready, 1)
                if k[0] == 'tile' and k[1:] in SM:
                    head_rsqrt(k[1:])
                if k[0] == 'dv' and diff_units[k[1]][1] == NF - 1:
                    head_rsqrt(('yd', diff_units[k[1]][0]))
                if k[0] == 'xs':
                    n = TB + MB + k[1]
                    pool.wait_ge(sum2, k[1] + 1)
                    rsqrt(st_in[:, 0, n:n + 1], st_in[:, 1, n:n + 1], 1.0 / D, half_neg[:, 0:1], rstd2)

            def low_bits(i, raw):
                pool.tensor_tensor(w_lo[:, i, :, :, :], raw, w_hi[:, i, :, :, :], ALU.subtract).then_inc(lo_ready, 1)
            for half in range(2):
                pool.wait_ge(hi_ready, half + 1)
                split(pool, 0, 0, 0, 0, half, low_bits)
            pool.wait_ge(pv_done, nm + len(diff_units))
            link(pool.memset(h_sb, 0.0))
            pool.memset(xg, 0.0).then_inc(xt_done, 3)

            for b in tb:
                pool.wait_ge(xn_stored[b], 16)

            def carry_waits(n, i):
                pool.wait_ge(carried[i], n)
                pool.tensor_tensor(carrier[0:1, i:i + 1], half_neg[0:1, 0:1], half_neg[0:1, 0:1], ALU.mult).then_inc(carried[i], 1)

            def gather(n, j):
                g = j % 3
                pool.wait_ge(idx_ready, n + 1)
                pool.wait_ge(xt_done, n + 1)
                carry_waits(n, 0)
                pool.indirect_dma_start(
                    out=xg[0:CAP, g, :], out_offset=None, in_=xn_dram,
                    in_offset=bass.IndirectOffsetOnAxis(ap=idx[0:CAP, j, :], axis=0),
                    bounds_check=S - 1, oob_is_err=False).then_inc(xg_loaded[g], 16)

            def scatter(n, j, u):
                pool.wait_ge(y_copied0, n + 1)
                pool.wait_ge(y_copied1, n + 1)
                carry_waits(n, 1)
                pool.indirect_dma_start(
                    out=y_dram, out_offset=bass.IndirectOffsetOnAxis(ap=idy[0:CAP, j, :], axis=0),
                    in_=y_sb[:, u, :], in_offset=None,
                    bounds_check=2 * S - 1, oob_is_err=False).then_inc(scattered[u], 16)

            def round_(r):
                pool.wait_ge(xt_done, r * NE + 3)
                gather(r * NE, 0)
                gather(r * NE + 1, 1)
                if isinstance(r, int):
                    pool.wait_ge(hi_ready, PIECES)
                    split(pool, r, 0, 0, 1, 0, low_bits)

                def expert(e, j, first, last):
                    if not isinstance(e, int) or e + 2 < NE:
                        gather(r * NE + e + 2, (j + 2) % UN)
                    if not first:
                        scatter(r * NE + e - 1, (j - 1) % UN, (j - 1) % 2)
                bodies(pool, expert)
                scatter(r * NE + NE - 1, (NE - 1) % UN, (NE - 1) % 2)
            all_rounds(pool, round_)
            rounds = pool.value_load(nr_i[0:1, 0:1], min_val=0, max_val=ROUNDS)
            for u in range(2):
                pool.wait_ge(scattered[u], rounds * (8 * NE))
                pool.tensor_tensor(carrier[0:1, 2 + u:3 + u], half_neg[0:1, 0:1], half_neg[0:1, 0:1], ALU.mult).then_inc(all_scattered, 1)

        @block.scalar
        def _(act_e):
            steps = [0]

            def link(ins):
                steps[0] += 1
                ins.then_inc(act_step, 1)
                act_e.wait_ge(act_step, steps[0])

            def row_squares(n):
                rb = in_order[n]
                if rb >= MB:
                    act_e.wait_ge(s_x[rb - MB], 16)
                    src = x_sb[:, rb - MB, :]
                else:
                    act_e.wait_ge(s_mem, 16)
                    src = mem_sb[:, rb, :]
                link(act_e.activation(y_t[:, 2 * (n % 2):2 * (n % 2) + 2, :].rearrange("p a b -> p (a b)"), src, ACT.Square,
                                      accum_out=st_in[:, 0, n:n + 1]))
                act_e.activation(cnt[:, 15:16], st_in[:, 0, n:n + 1], ACT.Copy).then_inc(in_sum, 1)

            def square(k, src, wait):
                n = SM[k]
                act_e.wait_ge(*wait)
                if n >= 2:
                    act_e.wait_ge(ss_ready, n - 1)
                act_e.activation(sq[:, n % 2, :], src, ACT.Square).then_inc(sq_ready, 1)

            def features(k):
                kind, b = k
                dst = {'mk': mk_t, 'mq': mq_t, 'k': k_t, 'q': q_t, 'yd': y_t[:, 0:NF, :], 'ym': y_t[:, NF:2 * NF, :]}[kind]
                act_e.wait_ge(pt_done, PT[k] + 1)
                if kind in ('k', 'q'):
                    act_e.wait_ge(lru_ready, NF)
                if kind == 'yd':
                    act_e.wait_ge(pa_done, PA[('wo0', (b, 1))] + 1)
                src = pt[PT[k] % 2][:, :].rearrange("p (h t) -> p h t", h=NF)
                sc_ = 1.0 if kind == 'ym' else cols[:, gain_of[kind]:gain_of[kind] + 1]
                act_e.activation(dst[:, :, b * P:(b + 1) * P], src, ACT.Copy, scale=sc_).then_inc(feat_ready, 1)

            def probs(k, n):
                i = PB[k]
                act_e.wait_ge(pt_done, PT[k] + 1)
                if i >= 2:
                    act_e.wait_ge(pv_done, i - 1)
                act_e.activation(p_t[:, i % 2, 0:n], pt[PT[k] % 2][:, 0:n], ACT.Copy).then_inc(pt_ready, 1)

            def tile(k):
                act_e.wait_ge(pa_done, PA[k] + 1)
                src = pa[PA[k] % 2][:, :]
                if k[0] == 'lx':
                    f = k[1]
                    if f >= 2:
                        act_e.wait_ge(xc_ready, f - 1)
                    act_e.activation(xpad[:, f % 2, CONV - 1:CONV - 1 + S], src, ACT.Copy).then_inc(xpad_ready, 1)
                elif k[0] == 'lg':
                    act_e.activation(y_t[:, k[1], :], src, ACT.Gelu_apprx_tanh).then_inc(gelu_ready, 1)
                elif k in SM:
                    square(k, src, (pa_done, PA[k] + 1))
                elif k in CP:
                    dst = (mv if k[0] == 'mv' else v_sb)[:, k[1], :]
                    act_e.activation(dst, src, ACT.Copy).then_inc(copied, 1)

            def gate(g, f):
                n = PS[(g, f)]
                act_e.wait_ge(ps_done, n + 1)
                c = (C_BA if g == 'ga' else C_BX) + f
                dst = ra[:, f, :] if g == 'ga' else ix[:, f, :]
                act_e.activation(dst, ps[n % 2][:, :], ACT.Sigmoid, bias=cols[:, c:c + 1]).then_inc(sig_ready, 1)

            def decay():
                act_e.wait_ge(sp_ready, 1)
                act_e.wait_ge(sig_ready, 2 * NF)
                for f in range(NF):
                    act_e.activation(th[:, f, :], ra[:, f, :], ACT.Tanh, scale=sp[:, 8, f:f + 1]).then_inc(act_step, 1)
                    steps[0] += 1
                act_e.wait_ge(act_step, steps[0])
                for f in range(NF):
                    act_e.activation(ra[:, f, :], ra[:, f, :], ACT.Exp, scale=sp[:, 9, f:f + 1]).then_inc(a_ready, 1)

            def mem_exps(u):
                act_e.wait_ge(mem_nb, u + 1)
                if u == 0:
                    act_e.wait_ge(lru_ready, NF)
                if u >= 2:
                    act_e.wait_ge(pt_done, PT[('mt', u - 2)] + 1)
                for i in range(2):
                    act_e.activation(e_sb[:, u % 2, 0, i * M:(i + 1) * M], ps[PS[('sm', u)] % 2][:, i * M:(i + 1) * M],
                                     ACT.Exp, bias=nb[:, 2 * u + i:2 * u + i + 1], scale=HD ** -0.5,
                                     accum_out=rs[:, 2 * u + i:2 * u + i + 1]).then_inc(mem_exp, 1)

            def diff_exps(u):
                b, h = diff_units[u]
                n = (b + 1) * P
                for c in range(2):
                    act_e.wait_ge(diff_nb, 2 * u + c + 1)
                    if c == 0:
                        act_e.wait_ge(pt_done, PT[('dt', u - 2) if u >= 2 else ('mt', nm - 2 + u)] + 1)
                    i = 16 + 2 * (u % 16) + c
                    act_e.activation(e_sb[:, u % 2, c, 0:n], ps[PS[('sd', u, c)] % 2][:, 0:n], ACT.Exp,
                                     bias=nb[:, i:i + 1], scale=QK_DIM ** -0.5, accum_out=rs[:, i:i + 1]).then_inc(diff_exp, 1)

            n_v = xn_dram.rearrange("(t p) d -> t p d", p=P)

            def row_squares2(b):
                n = TB + MB + b
                act_e.wait_ge(wo_added, WO[('wo1', (b, 1))] + 1)
                link(act_e.activation(squares[:, b % 2, :], x_sb[:, b, :], ACT.Square, accum_out=st_in[:, 0, n:n + 1]))
                act_e.activation(cnt[:, 15:16], st_in[:, 0, n:n + 1], ACT.Copy).then_inc(sum2, 1)

            def high_bits(i, raw):
                act_e.activation(w_hi[:, i, :, :, :], raw, ACT.Copy).then_inc(hi_ready, 1)

            act_e.wait_ge(pads_ready, 1)
            for k in plan:
                if k[0] == 'first':
                    act_e.wait_ge(logits_ready, TB - 1)
                    for b in (0, TB - 2):
                        act_e.wait_ge(xn_stored[b], 16)
                    for half in range(2):
                        split(act_e, 0, 0, 0, 0, half, high_bits)
                if k[0] == 'rs':
                    row_squares(k[1])
                if k[0] == 'split_x':
                    n = k[1]
                    o = in_order[n] * P
                    act_e.wait_ge(in_feat, 2 * (n + 1))
                    for dst, k0, nk in input_high(n):
                        ins = act_e.activation(dst, act[:, k0:k0 + nk, o:o + P], ACT.Copy)
                    ins.then_inc(xh_ready, 1)
                if k[0] == 'split_c':
                    name, quarter = k[1:]
                    ci = dense.index(name)
                    act_e.wait_ge(chunk_in[CH[name]], 16)
                    if name == 'mk':
                        act_e.wait_ge(in_scaled, TB)
                    elif name == 'v':
                        act_e.wait_ge(pv_done, nm)
                    elif quarter < QUARTERS - 1:
                        act_e.wait_ge(quarter_used, (QUARTERS - 1) * (ci - 1) + quarter + 1)
                    else:
                        act_e.wait_ge(pa_done, chunk_end(CH[name] - 1))
                    h = slice(quarter * KT // QUARTERS, (quarter + 1) * KT // QUARTERS)
                    act_e.activation(chunk_hi(name)[:, h, :], chunk(name)[:, h, :], ACT.Copy).then_inc(chunk_hi_ready, 1)
                if k[0] == 'split_w':
                    i = k[1]
                    raw, u = lru_weights(i)
                    act_e.wait_ge(chunk_in[CH[lru_tiles[i][0]]], 16)
                    if i >= 2:
                        act_e.wait_ge(pa_done, PA[lru_tiles[i - 2]] + 1)
                    act_e.activation(lw[:, 0, u, :, :], raw, ACT.Copy).then_inc(lw_hi_ready, 1)
                if k[0] == 'tile':
                    tile(k[1:])
                if k[0] == 'gate':
                    gate(*k[1:])
                if k == ('tile', 'lx', 3):
                    act_e.wait_ge(abs_ready, 1)
                    act_e.activation(sp[:, 1, :], sp[:, 0, :], ACT.Exp, scale=-1.0).then_inc(sp_exp, 1)
                    act_e.wait_ge(lam_sum, 1)
                    act_e.activation(lam_s[:, 2:4], lam_s[:, 0:2], ACT.Exp).then_inc(lam_exp, 1)
                if k[0] == 'lru_a':
                    decay()
                if k[0] == 'lru_b':
                    for f in range(NF):
                        act_e.wait_ge(b2_ready, f + 1)
                        act_e.activation(th[:, f, :], th[:, f, :], ACT.Sqrt).then_inc(b_ready, 1)
                if k[0] == 'turn':
                    features(k[1:])
                if k[0] == 'me':
                    mem_exps(k[1])
                if k[0] == 'mt':
                    probs(k, 512)
                if k[0] == 'de':
                    diff_exps(k[1])
                if k[0] == 'dt':
                    probs(k, (diff_units[k[1]][0] + 1) * P)
                if k[0] == 'dv':
                    b, h = diff_units[k[1]]
                    if h == NF - 1:
                        square(('yd', b), po[(TB + b) % 2][:, :], (pv_done, nm + k[1] + 1))
                if k[0] == 'xs':
                    row_squares2(k[1])
                if k[0] == 'route':
                    b = k[1]
                    act_e.wait_ge(r_exp_in, b + 1)
                    act_e.activation(rt[:, 1, b, 0:8], rt[:, 1, b, 0:8], ACT.Exp).then_inc(r_exp_out, 1)
                if k[0] == 'x2':
                    act_e.wait_ge(scaled2, k[1] + 1)
                    act_e.dma_start(n_v[k[1]], xs2[k[1] % 2]).then_inc(xn_stored[k[1]], 16)
            act_e.wait_ge(logits_ready, TB)
            act_e.wait_ge(pv_done, nm + len(diff_units))
            for b in tb:
                act_e.wait_ge(xn_stored[b], 16)

            def x_high(n, u):
                act_e.wait_ge(xt_ready, n + 1)
                act_e.activation(x_hl[:, u, :, 0:CAP], xg_t[:, u, :, :], ACT.Copy).then_inc(x_hi_ready, 1)

            def h_features(n, u):
                act_e.wait_ge(ht_done, n + 1)
                act_e.activation(h_t[:, u, :, :], h_bank[:, 0:2 * CAP].rearrange("p (j s) -> p j s", j=2), ACT.Copy).then_inc(ht_ready, 1)

            def y_half(n, u):
                act_e.wait_ge(y_done, n + 1)
                act_e.wait_ge(scattered[u], n * 8 - 8 * u)
                act_e.activation(y_sb[:, u, 0:512], po[0][0:CAP, :], ACT.Copy).then_inc(y_copied0, 1)

            def round_(r):
                if not isinstance(r, int):
                    act_e.wait_ge(piece_used, r * (2 * NE))
                for p in range(2 * isinstance(r, int), PIECES):
                    split(act_e, r, 0, 0, p // 2, p % 2, high_bits)
                x_high(r * NE, 0)

                def expert(e, j, first, last):
                    n, u = r * NE + e, j % 2
                    split(act_e, r, e, j, 1, 1, high_bits)
                    if not first:
                        h_features(n - 1, 1 - u)
                    act_e.wait_ge(piece_used, n * 2 + 2)
                    act_e.activation(gu_low, pa[u][CAP:2 * CAP, :], ACT.Copy).then_inc(low_ready, 1)
                    if not last:
                        x_high(n + 1, 1 - u)
                    act_e.wait_ge(sum_ready, n + 1)
                    act_e.activation(silu, gu_sum[:, 0:FE], ACT.Silu).then_inc(silu_ready, 1)
                    split(act_e, r, e, j, 2, 0, high_bits)
                    if not first:
                        y_half(n - 1, 1 - u)
                bodies(act_e, expert)
                h_features(r * NE + NE - 1, (NE - 1) % 2)
                y_half(r * NE + NE - 1, (NE - 1) % 2)
            all_rounds(act_e, round_)

        @block.tensor
        def _(pe):
            def bank(banks, uses, freed, k):
                n = uses[k]
                if n >= 2:
                    pe.wait_ge(*freed(n - 2))
                return banks[n % 2]

            def transposes(k, parts, done=pt_done):
                dst = bank(pt, PT, pt_freed, k)
                for src, o in parts:
                    last = pe.transpose(dst[0:src.shape[1], o:o + src.shape[0]], src, ident[0:src.shape[0], 0:src.shape[0]])
                last.then_inc(done, 1)

            def row_turn(n):
                v = xs[:, n % 2, :].rearrange("q (p k) -> q k p", k=KT)
                pe.wait_ge(in_scaled, n + 1)
                for h in range(2):
                    transposes(('in', n, h), [(v[:, 4 * h + i, :], i * P) for i in range(4)])

            def tokens(b):
                return slice(M + b * P, M + (b + 1) * P)

            def project(k):
                name = k[0]
                w = chunk(name)
                pe.wait_ge(chunk_in[CH[name]], 16)
                dst = bank(pa, PA, pa_freed, k)
                if name[:2] == 'wo':
                    c, (b, half) = int(name[2]), k[1]
                    y = y_t[:, NF:2 * NF, :] if c == 2 else y_t[:, 0:NF, :]
                    if c == 0:
                        pe.wait_ge(lru_ready, NF)
                    else:
                        pe.wait_ge(feat_ready, FT[('ym' if c == 2 else 'yd', b)] + 1)
                    pairs = [(y[:, i, b * P:(b + 1) * P], w[:, i, half * 512:(half + 1) * 512]) for i in range(NF)]
                elif k in lru_tiles:
                    pe.wait_ge(xl_ready, TB)
                    pe.wait_ge(lw_lo_ready, lru_tiles.index(k) + 1)
                    u = lru_tiles.index(k) % 2
                    pairs = []
                    for i in range(KT):
                        xh, xl = tok_hi[i // (KT // 2)][:, i % (KT // 2), :], act_lo[:, i, M:M + S]
                        wh, wl = lw[:, 0, u, i, :], lw[:, 1, u, i, :]
                        pairs += [(wh, xh), (wh, xl), (wl, xh)]
                else:
                    pe.wait_ge(xl_ready, TB + MB)
                    t = slice(k[1] * P, (k[1] + 1) * P)
                    hi, lo = chunk_hi(name), chunk_lo(name)
                    pairs = []
                    for i in range(KT):
                        if name in ('mk', 'mv'):
                            xh, xl = mem_hi[:, i, t], act_lo[:, i, t]
                        else:
                            xh, xl = tok_hi[i // (KT // 2)][:, i % (KT // 2), t], act_lo[:, i, tokens(k[1])]
                        pairs += [(xh, hi[:, i, :]), (xh, lo[:, i, :]), (xl, hi[:, i, :])]
                each = len(pairs) // QUARTERS
                for i, (x, y) in enumerate(pairs):
                    if name in dense and i % each == 0:
                        pe.wait_ge(chunk_lo_ready, QUARTERS * dense.index(name) + i // each + 1)
                    last = pe.matmul(dst[:, :], x, y, start=(i == 0), stop=(i == len(pairs) - 1))
                    if name in dense and i % each == each - 1 and i < len(pairs) - 1 and PA[k] + 1 == chunk_end(CH[name]):
                        last.then_inc(quarter_used, 1)
                last.then_inc(pa_done, 1)
            def turn(k):
                pe.wait_ge(sc_ready, NT[k] + 1)
                v = sc[:, NT[k] % 2, :]
                transposes(k, [(v[:, i * P:(i + 1) * P], i * P) for i in range(NF)])

            def gate(g, f):
                pe.wait_ge(xc_ready, f + 1)
                dst = bank(ps, PS, ps_freed, (g, f))
                pe.matmul(dst[:, :], gates_w[:, 0 if g == 'ga' else 1, f, :], xc[:, f, :], start=True, stop=True).then_inc(ps_done, 1)

            def mem_scores(u):
                b, hp = mem_units[u]
                if hp == 0:
                    pe.wait_ge(feat_ready, FT[('mq', b)] + 1)
                dst = bank(ps, PS, ps_freed, ('sm', u))
                for i in range(2):
                    last = pe.matmul(dst[:, i * M:(i + 1) * M], mq_t[:, 2 * hp + i, b * P:(b + 1) * P], mk_t[:, 2 * hp + i, :],
                                     start=True, stop=True)
                last.then_inc(ps_done, 1)

            def mem_values(u):
                b, hp = mem_units[u]
                if u == 0:
                    pe.wait_ge(copied, CP[('mv', MB - 1)] + 1)
                if hp == 0 and b >= 2:
                    pe.wait_ge(sc_ready, NT[('ym', b - 2)] + 1)
                pe.wait_ge(pt_ready, u + 1)
                for i in range(2):
                    h = 2 * hp + i
                    for t in mb:
                        last = pe.matmul(po[b % 2][:, h * HD:(h + 1) * HD], p_t[:, u % 2, (2 * i + t) * P:(2 * i + t + 1) * P],
                                         mv[:, t, h * HD:(h + 1) * HD], start=(t == 0), stop=(t == MB - 1))
                last.then_inc(pv_done, 1)

            def diff_scores(u):
                b, h = diff_units[u]
                if h == 0:
                    pe.wait_ge(feat_ready, max(FT[('k', b)], FT[('q', b)]) + 1)
                for c in range(2):
                    d = slice(64 * c, 64 * c + 64)
                    dst = bank(ps, PS, ps_freed, ('sd', u, c))
                    pe.matmul(dst[:, 0:(b + 1) * P], q_t[d, h, b * P:(b + 1) * P], k_t[d, h, 0:(b + 1) * P],
                              start=True, stop=True).then_inc(ps_done, 1)

            def diff_values(u):
                b, h = diff_units[u]
                if h == 0:
                    pe.wait_ge(copied, CP[('v', b)] + 1)
                if h == 0:
                    pe.wait_ge(sc_ready, NT[('ym', TB - 2 + b) if b < 2 else ('yd', b - 2)] + 1)
                pe.wait_ge(pt_ready, nm + u + 1)
                for t in range(b + 1):
                    last = pe.matmul(po[(TB + b) % 2][:, h * HD:(h + 1) * HD], p_t[:, (nm + u) % 2, t * P:(t + 1) * P],
                                     v_sb[:, t, h * HD:(h + 1) * HD], start=(t == 0), stop=(t == b))
                last.then_inc(pv_done, 1)

            def x2_turn(b):
                v = xs2[b % 2].rearrange("q (p k) -> q k p", k=KT)
                pe.wait_ge(scaled2, b + 1)
                for h in range(2):
                    transposes(('x2', b, h), [(v[:, 4 * h + i, :], i * P) for i in range(4)])

            def logits(b):
                pe.wait_ge(x2_ready, 2 * b + 2)
                dst = bank(ps, PS, ps_freed, ('lo', b))
                for i in range(KT):
                    last = pe.matmul(dst[:, 0:NR], x2_t[b % 2][:, i, :], wr[:, i, :], start=(i == 0), stop=(i == KT - 1))
                last.then_inc(ps_done, 1)

            pe.wait_ge(consts, 1)
            for k in plan:
                if k[0] == 'rt':
                    row_turn(k[1])
                if k[0] == 'par':
                    pe.wait_ge(s_rows, 16 * 12)
                    transposes(k, [(rows[0:N_ROWS, :], 0)])
                if k[0] == 'tile':
                    project(k[1:])
                if k[0] == 'turn':
                    turn(k[1:])
                if k[0] == 'gate':
                    if k[1:] == ('ga', 0):
                        pe.wait_ge(s_gw, 64)
                    gate(*k[1:])
                if k[0] == 'ms':
                    mem_scores(k[1])
                if k[0] == 'mt':
                    pe.wait_ge(mem_exp, 2 * k[1] + 2)
                    transposes(k, [(e_sb[:, k[1] % 2, 0, i * P:(i + 1) * P], i * P) for i in range(4)])
                if k[0] == 'mv':
                    mem_values(k[1])
                if k[0] == 'ds':
                    diff_scores(k[1])
                if k[0] == 'dt':
                    pe.wait_ge(p_ready, k[1] + 1)
                    transposes(k, [(e_sb[:, k[1] % 2, 0, i * P:(i + 1) * P], i * P) for i in range(diff_units[k[1]][0] + 1)])
                if k[0] == 'dv':
                    diff_values(k[1])
                if k[0] == 'x2':
                    x2_turn(k[1])
                if k[0] == 'lo':
                    if k[1] == 0:
                        pe.wait_ge(wr_ready, 1)
                    logits(k[1])

            pe.wait_ge(sel_ready, TB)
            dst = bank(ps, PS, ps_freed, ('cum', 0))
            v = sel[:, :, :].rearrange("p b e -> p (b e)")
            pe.matmul(dst[:, 0:TB * NE], tri[:, :], v, start=True, stop=False)
            for c in range(1, TB):
                last = pe.matmul(dst[:, c * NE:TB * NE], ones[:, :], v[:, 0:(TB - c) * NE], start=False, stop=(c == TB - 1))
            last.then_inc(ps_done, 1)
            dst = bank(ps, PS, ps_freed, ('cnt', 0))
            for c in tb:
                last = pe.matmul(dst[:, 0:NE], ones[:, :], sel[:, c, :], start=(c == 0), stop=(c == TB - 1))
            last.then_inc(ps_done, 1)

            def slot_table(r, e, j, d):
                n, u = r * NE + e + d, (j + d) % 2
                pe.wait_ge(oh_ready, n + 1)
                if not (isinstance(n, int) and n == 0):
                    pe.wait_ge(idx_ready, n)
                for b in tb:
                    last = pe.matmul(tab_bank[0:CAP, 0:3], onehot[:, u, b, :], tab_e[:, u, b, :], start=(b == 0), stop=(b == TB - 1))
                last.then_inc(tab_done, 1)

            def x_turn(r, e, j, d):
                n, g = r * NE + e + d, (j + d) % 3
                pe.wait_ge(xg_loaded[g], arrived(r, e, j, d, 3, 16))
                pe.wait_ge(xt_ready, n)
                v = xg[:, g, :].rearrange("q (p k) -> q k p", k=KT)
                pe.transpose(pt[0][:, 0:P], v[:, 0, :], ident[:, :])
                for i in range(1, KT):
                    last = pe.transpose(pt[0][:, i * CAP:(i + 1) * CAP], v[0:CAP, i, :], ident[0:CAP, 0:CAP])
                last.then_inc(xt_done, 1)

            def h_turn(n, u):
                pe.wait_ge(h_ready, n + 1)
                pe.wait_ge(ht_ready, n)
                v = h_sb[:, u, :].rearrange("q (p j) -> q j p", j=2)
                pe.transpose(h_bank[:, 0:P], v[:, 0, :], ident[:, :])
                pe.transpose(h_bank[:, CAP:P], v[0:CAP, 1, :], ident[0:CAP, 0:CAP]).then_inc(ht_done, 1)

            def down(r, e, j, d):
                n, j_, u = r * NE + e + d, (j + d) % UN, (j + d) % 2
                pe.wait_ge(ht_ready, n + 1)
                pe.wait_ge(y_copied0, n)
                pe.wait_ge(y_copied1, n)
                pe.wait_ge(down_in[j_], arrived(r, e, j, d, UN, 16))
                w = expert_d(j_)
                for half in range(2):
                    for i in range(2):
                        last = pe.matmul(po[half][0:CAP, :], h_t[:, u, i, :], w[:, i, half * 512:(half + 1) * 512],
                                         start=(i == 0), stop=(i == 1))
                last.then_inc(y_done, 1)

            def round_(r):
                for e in range(3):
                    slot_table(r, 0, 0, e)
                x_turn(r, 0, 0, 0)

                def expert(e, j, first, last_):
                    n, u = r * NE + e, j % 2
                    pe.wait_ge(x_hi_ready, n + 1)
                    pe.wait_ge(x_lo_ready, n + 1)
                    if not (isinstance(n, int) and n < 2):
                        pe.wait_ge(sum_ready, n - 1)
                    out_ = pa[u][:, :].rearrange("p (w f) -> p w f", w=2)
                    for half in range(2):
                        pe.wait_ge(hi_ready, n * 2 + half + 1)
                        pe.wait_ge(lo_ready, n * 2 + half + 1)
                        piece = (2 * j + half) % PIECES
                        for i in range(KT // 2):
                            k = half * (KT // 2) + i
                            for w in (w_hi, w_lo):
                                last = pe.matmul(out_, x_hl[:, u, k, :], w[:, piece, :, i, :],
                                                 start=(k == 0 and w is w_hi), stop=(k == KT - 1 and w is w_lo))
                        last.then_inc(piece_used, 1)
                    if not first:
                        h_turn(n - 1, 1 - u)
                    if exists(e, 3):
                        slot_table(r, e, j, 3)
                    if not last_:
                        x_turn(r, e, j, 1)
                    if not first:
                        down(r, e, j, -1)
                bodies(pe, expert)
                h_turn(r * NE + NE - 1, (NE - 1) % 2)
                down(r, NE - 1, (NE - 1) % UN, 0)
            all_rounds(pe, round_)

        @block.vector
        def _(dve):
            steps = [0]

            def link(ins):
                steps[0] += 1
                ins.then_inc(dve_step, 1)
                dve.wait_ge(dve_step, steps[0])

            dve.memset(xpad[:, :, 0:CONV], 0.0).then_inc(pads_ready, 1)

            def scale_in(n):
                rb = in_order[n]
                src = x_sb[:, rb - MB, :] if rb >= MB else mem_sb[:, rb, :]
                dve.wait_ge(in_rstd, n + 1)
                if n >= 2:
                    dve.wait_ge(pt_done, PT[('in', n - 2, 1)] + 1)
                dve.tensor_scalar(xs[:, n % 2, :], src, st_in[:, 1, n:n + 1], None, ALU.mult).then_inc(in_scaled, 1)

            def gained(dst, k, which, h):
                return dve.tensor_tensor(dst, pt[PT[k] % 2][:, :].rearrange("p (k t) -> p k t", k=4),
                                         gain_in[:, which, 4 * h:4 * h + 4].unsqueeze(2).to_broadcast([P, 4, P]), ALU.mult)

            def row_features(n):
                rb = in_order[n]
                if n == 0:
                    dve.wait_ge(s_g1, 16)
                if n == TB:
                    dve.wait_ge(s_par, 16 * 10)
                for h in range(2):
                    k = ('in', n, h)
                    dve.wait_ge(pt_done, PT[k] + 1)
                    gained(act[:, 4 * h:4 * h + 4, rb * P:(rb + 1) * P], k, 1 if rb >= MB else 0, h).then_inc(in_feat, 1)

            def parameters_1():
                lam_c = cols[:, C_LAM:C_LAM + NF]
                dve.wait_ge(pt_done, PT[('par', 0)] + 1)
                dve.tensor_copy(cols[:, 0:N_ROWS], pt[PT[('par', 0)] % 2][:, 0:N_ROWS]).then_inc(cols_ready, 1)
                dve.wait_ge(cols_ready, 1)
                link(dve.tensor_scalar(sp[:, 2, :], lam_c, -1.0, None, ALU.mult))
                dve.tensor_tensor(sp[:, 0, :], sp[:, 2, :], lam_c, ALU.max).then_inc(abs_ready, 1)
                dve.wait_ge(s_par, 16 * 10)
                for n in range(2):
                    link(dve.tensor_tensor(lam4[:, 2 * n, :], lam4[:, 2 * n, :], lam4[:, 2 * n + 1, :], ALU.mult))
                    red = dve.tensor_reduce(lam_s[:, n:n + 1], lam4[:, 2 * n, :], AX, ALU.add)
                    if n == 0:
                        link(red)
                red.then_inc(lam_sum, 1)

            def parameters_2():
                dve.wait_ge(sp_exp, 1)
                link(dve.tensor_scalar(sp[:, 3, :], sp[:, 1, :], 2.0, None, ALU.add))
                link(dve.reciprocal(sp[:, 4, :], sp[:, 3, :]))
                link(dve.tensor_tensor(sp[:, 5, :], sp[:, 1, :], sp[:, 4, :], ALU.mult))
                link(dve.tensor_tensor(sp[:, 6, :], sp[:, 5, :], sp[:, 5, :], ALU.mult))
                link(dve.tensor_scalar(sp[:, 7, :], sp[:, 6, :], 1.0 / 17, None, ALU.mult))
                for c in (15, 13, 11, 9, 7, 5, 3):
                    link(dve.scalar_tensor_tensor(sp[:, 7, :], sp[:, 7, :], 1.0 / c, sp[:, 6, :], ALU.add, ALU.mult))
                link(dve.scalar_tensor_tensor(sp[:, 7, :], sp[:, 7, :], 1.0, sp[:, 5, :], ALU.add, ALU.mult))
                link(dve.tensor_scalar(sp[:, 2, :], sp[:, 2, :], 0.0, None, ALU.max))
                link(dve.scalar_tensor_tensor(sp[:, 7, :], sp[:, 7, :], 2.0, sp[:, 2, :], ALU.mult, ALU.add))
                link(dve.tensor_scalar(sp[:, 8, :], sp[:, 7, :], LRU_C, None, ALU.mult))
                dve.tensor_scalar(sp[:, 9, :], sp[:, 7, :], -LRU_C, None, ALU.mult).then_inc(sp_ready, 1)
                dve.wait_ge(lam_exp, 1)
                link(dve.tensor_tensor(lam_s[:, 0:1], lam_s[:, 3:4], lam_s[:, 2:3], ALU.subtract))
                link(dve.tensor_scalar(lam_s[:, 0:1], lam_s[:, 0:1], -LAM_INIT, None, ALU.add))
                link(dve.tensor_scalar(cols[:, C_DH:C_DH + 1], cols[:, C_DH:C_DH + 1], 1.0 - LAM_INIT, None, ALU.mult))
                link(dve.tensor_copy(wr[:, :, 0:NG], wr_g[:, :, :]))
                dve.tensor_copy(wr[:, :, NG:NR], wr_e[:, :, :]).then_inc(wr_ready, 1)

            def convolve(f):
                dve.wait_ge(xpad_ready, f + 1)
                tap = [xpad[:, f % 2, j:j + S] for j in range(CONV)]
                wcol = [cols[:, C_CONV + NF * j + f:C_CONV + NF * j + f + 1] for j in range(CONV)]
                link(dve.tensor_scalar(xc[:, f, :], tap[3], wcol[3], cols[:, C_CB + f:C_CB + f + 1], ALU.mult, ALU.add))
                for j in range(CONV - 1):
                    ins = dve.scalar_tensor_tensor(xc[:, f, :], tap[j], wcol[j], xc[:, f, :], ALU.mult, ALU.add)
                    if j < CONV - 2:
                        link(ins)
                ins.then_inc(xc_ready, 1)

            def inputs():
                dve.wait_ge(xc_ready, NF)
                for f in range(NF):
                    dve.wait_ge(a_ready, f + 1)
                    link(dve.tensor_tensor(xpad[:, f % 2, 0:S], ra[:, f, :], ra[:, f, :], ALU.mult))
                    dve.scalar_tensor_tensor(th[:, f, :], xpad[:, f % 2, 0:S], 1.0, th[:, f, :], ALU.add, ALU.mult).then_inc(b2_ready, 1)

            def recurrence():
                for f in range(NF):
                    dve.wait_ge(b_ready, f + 1)
                    dve.wait_ge(gated, f + 1)
                    link(dve.tensor_tensor(ix[:, f, :], ix[:, f, :], th[:, f, :], ALU.mult))
                    dve.tensor_tensor_scan(xc[:, f, :], ra[:, f, :], ix[:, f, :], 0.0, ALU.mult, ALU.add).then_inc(scanned, 1)

            def scaled(k, src, scale, g):
                n = NT[k]
                if n >= 2:
                    dve.wait_ge(pt_done, PT[normed[n - 2]] + 1)
                dve.tensor_tensor(sc[:, n % 2, :].rearrange("p (g d) -> p g d", g=g), src[:, :].rearrange("p (g d) -> p g d", g=g),
                                  scale.unsqueeze(2).to_broadcast([P, g, GW // g]), ALU.mult).then_inc(sc_ready, 1)

            def sum_squares(k):
                n, g = SM[k], groups_of[k[0]]
                dve.wait_ge(sq_ready, n + 1)
                dve.tensor_reduce(st[:, 0, n, 0:g], sq[:, n % 2, :].rearrange("p (g d) -> p g d", g=g), AX, ALU.add).then_inc(ss_ready, 1)

            def scale(k):
                kind, b = k
                if kind == 'ym':
                    dve.wait_ge(mem_exp, 4 * b + 4)
                    link(dve.reciprocal(rr[:, 4 * b:4 * b + 4], rs[:, 4 * b:4 * b + 4]))
                    dve.wait_ge(pv_done, 2 * b + 2)
                    scaled(k, po[b % 2], rr[:, 4 * b:4 * b + 4], 4)
                else:
                    n, g = SM[k], groups_of[kind]
                    dve.wait_ge(rstd_ready, n + 1)
                    scaled(k, po[(TB + b) % 2] if kind == 'yd' else pa[PA[k] % 2], st[:, 1, n, 0:g], g)

            def tile(k):
                if k in SM:
                    sum_squares(k)
                elif k in WO:
                    b, half = k[1]
                    o = slice(half * 512, half * 512 + 512)
                    dve.wait_ge(s_x_again[b], 16)
                    dve.wait_ge(pa_done, PA[k] + 1)
                    dve.tensor_tensor(x_sb[:, b, o], pa[PA[k] % 2][:, :], x_sb[:, b, o], ALU.add).then_inc(wo_added, 1)

            def mem_max(u):
                n = PS[('sm', u)]
                dve.wait_ge(ps_done, n + 1)
                link(dve.tensor_reduce(mx[:, 2 * u:2 * u + 2], ps[n % 2][:, :].rearrange("p (i m) -> p i m", i=2), AX, ALU.max))
                dve.tensor_scalar(nb[:, 2 * u:2 * u + 2], mx[:, 2 * u:2 * u + 2], -HD ** -0.5, None, ALU.mult).then_inc(mem_nb, 1)

            def diff_max(u):
                b, h = diff_units[u]
                n = (b + 1) * P
                for c in range(2):
                    k = PS[('sd', u, c)]
                    i = 16 + 2 * (u % 16) + c
                    dve.wait_ge(ps_done, k + 1)
                    link(dve.tensor_tensor(ps[k % 2][:, b * P:n], ps[k % 2][:, b * P:n], cmask[:, :], ALU.add))
                    link(dve.tensor_reduce(mx[:, i:i + 1], ps[k % 2][:, 0:n], AX, ALU.max))
                    dve.tensor_scalar(nb[:, i:i + 1], mx[:, i:i + 1], -QK_DIM ** -0.5, None, ALU.mult).then_inc(diff_nb, 1)

            def difference(u):
                n, i = (diff_units[u][0] + 1) * P, 16 + 2 * (u % 16)
                dve.wait_ge(diff_exp, 2 * u + 2)
                link(dve.reciprocal(rr[:, i:i + 2], rs[:, i:i + 2]))
                link(dve.tensor_scalar(rr[:, i + 1:i + 2], rr[:, i + 1:i + 2], lam_s[:, 0:1], None, ALU.mult))
                link(dve.tensor_scalar(e_sb[:, u % 2, 0, 0:n], e_sb[:, u % 2, 0, 0:n], rr[:, i:i + 1], None, ALU.mult))
                dve.scalar_tensor_tensor(e_sb[:, u % 2, 0, 0:n], e_sb[:, u % 2, 1, 0:n], rr[:, i + 1:i + 2],
                                         e_sb[:, u % 2, 0, 0:n], ALU.mult, ALU.add).then_inc(p_ready, 1)

            def scale2(b):
                n = TB + MB + b
                dve.wait_ge(rstd2, b + 1)
                if b == 0:
                    dve.wait_ge(pa_done, PA[('v', TB - 1)] + 1)
                if b >= 2:
                    dve.wait_ge(pt_done, PT[('x2', b - 2, 1)] + 1)
                    dve.wait_ge(xn_stored[b - 2], 16)
                dve.tensor_scalar(xs2[b % 2], x_sb[:, b, :], st_in[:, 1, n:n + 1], None, ALU.mult).then_inc(scaled2, 1)

            def x2_features(b):
                if b >= 2:
                    dve.wait_ge(ps_done, PS[('lo', b - 2)] + 1)
                for h in range(2):
                    k = ('x2', b, h)
                    dve.wait_ge(pt_done, PT[k] + 1)
                    gained(x2_t[b % 2][:, 4 * h:4 * h + 4, :], k, 2, h).then_inc(x2_ready, 1)

            def route(b):
                lg, iota8 = lg_sb[:, b, :], iota_s[:, 0:8]
                grp, gexp, gmax, w, gsel = rt[:, 0, b, :], rt[:, 1, b, :], rt[:, 2, b, :], rt[:, 3, b, :], rt[:, 4, b, :]
                le, emax, one, two, tmp = (rt[:, c, b, :] for c in (6, 7, 8, 9, 11))
                dve.wait_ge(logits_ready, b + 1)
                link(dve.memset(grp, NEG))
                link(dve.tensor_copy(grp[:, 0:NG], lg[:, 0:NG]))
                link(dve.max(out=gmax, in_=grp))
                link(dve.max_index(out=rti[:, 0, b, :], in_max=gmax, in_values=grp))
                dve.tensor_scalar(gexp[:, 0:NG], lg[:, 0:NG], gmax[:, 0:1], None, ALU.subtract)
                link(dve.tensor_copy(w[:, 0:2], rti[:, 0, b, 0:2]))
                link(dve.tensor_scalar(gsel, iota8, w[:, 0:1], None, ALU.is_equal))
                pr = rprod[:, b, :].rearrange("p (e g) -> p e g", g=NG)
                link(dve.tensor_tensor(pr, lg[:, NG:NR].rearrange("p (g e) -> p e g", g=NG),
                                       gsel[:, 0:NG].unsqueeze(1).to_broadcast([P, NE_G, NG]), ALU.mult))
                link(dve.tensor_reduce(le, pr, AX, ALU.add))
                link(dve.max(out=emax, in_=le))
                link(dve.max_index(out=rti[:, 1, b, :], in_max=emax, in_values=le))
                dve.tensor_scalar(gexp[:, NG:8], emax[:, 1:2].to_broadcast([P, 8 - NG]), emax[:, 0:1], None, ALU.subtract).then_inc(r_exp_in, 1)
                link(dve.tensor_copy(w[:, 2:4], rti[:, 1, b, 0:2]))
                dve.tensor_scalar(one, iota8, w[:, 2:3], None, ALU.is_equal)
                link(dve.tensor_scalar(two, iota8, w[:, 3:4], None, ALU.is_equal))
                gs = gsel[:, 0:NG].unsqueeze(2).to_broadcast([P, NG, NE_G])

                def by_expert(t):
                    return t.unsqueeze(1).to_broadcast([P, NG, NE_G])

                def by_group(t):
                    return t.rearrange("p (g e) -> p g e", g=NG)
                dve.scalar_tensor_tensor(by_group(tab_r[:, b, :, 2]), gs, float(S), by_expert(two), ALU.mult, ALU.mult)
                link(dve.tensor_tensor(tmp, one, two, ALU.add))
                dve.tensor_tensor(by_group(sel[:, b, :]), gs, by_expert(tmp), ALU.mult).then_inc(sel_ready, 1)

            def weigh(b):
                gexp, w, gsel, one, two, both = (rt[:, c, b, :] for c in (1, 3, 4, 8, 9, 10))
                gs = gsel[:, 0:NG].unsqueeze(2).to_broadcast([P, NG, NE_G])

                def by_expert(t):
                    return t.unsqueeze(1).to_broadcast([P, NG, NE_G])

                def by_group(t):
                    return t.rearrange("p (g e) -> p g e", g=NG)
                dve.tensor_scalar(tab_r[:, b, :, 0], ones[:, 0:NE], tok[:, b:b + 1], None, ALU.mult)
                dve.wait_ge(r_exp_out, b + 1)
                link(dve.tensor_reduce(w[:, 4:5], gexp[:, 0:NG], AX, ALU.add))
                link(dve.tensor_scalar(w[:, 5:6], gexp[:, NG:NG + 1], 1.0, None, ALU.add))
                link(dve.tensor_tensor(w[:, 5:6], w[:, 5:6], w[:, 4:5], ALU.mult))
                link(dve.reciprocal(w[:, 5:6], w[:, 5:6]))
                link(dve.tensor_tensor(w[:, 6:7], w[:, 5:6], gexp[:, NG:NG + 1], ALU.mult))
                link(dve.tensor_scalar(both, one, w[:, 5:6], None, ALU.mult))
                link(dve.scalar_tensor_tensor(both, two, w[:, 6:7], both, ALU.mult, ALU.add))
                dve.tensor_tensor(by_group(tab_r[:, b, :, 1]), gs, by_expert(both), ALU.mult)
                link(dve.tensor_scalar(tab_r[:, b, :, 2], tab_r[:, b, :, 2], tok[:, b:b + 1], None, ALU.add))

            for k in plan:
                if k[0] == 'split_x':
                    n = k[1]
                    o = in_order[n] * P
                    dve.wait_ge(xh_ready, n + 1)
                    for hi, k0, nk in input_high(n):
                        ins = dve.tensor_tensor(act_lo[:, k0:k0 + nk, o:o + P], act[:, k0:k0 + nk, o:o + P], hi, ALU.subtract)
                    ins.then_inc(xl_ready, 1)
                if k[0] == 'split_c':
                    name, quarter = k[1:]
                    dve.wait_ge(chunk_hi_ready, QUARTERS * dense.index(name) + quarter + 1)
                    h = slice(quarter * KT // QUARTERS, (quarter + 1) * KT // QUARTERS)
                    dve.tensor_tensor(chunk_lo(name)[:, h, :], chunk(name)[:, h, :], chunk_hi(name)[:, h, :],
                                      ALU.subtract).then_inc(chunk_lo_ready, 1)
                if k[0] == 'split_w' and k[1] >= 2:
                    raw, u = lru_weights(k[1])
                    if k[1] == 2:
                        dve.wait_ge(lw_lo_ready, 2)
                    dve.wait_ge(lw_hi_ready, k[1] + 1)
                    dve.tensor_tensor(lw[:, 1, u, :, :], raw, lw[:, 0, u, :, :], ALU.subtract).then_inc(lw_lo_ready, 1)
                if k[0] == 'route':
                    route(k[1])
                if k[0] == 'weigh':
                    weigh(k[1])
                if k[0] == 'rs':
                    scale_in(k[1])
                if k[0] == 'rt':
                    row_features(k[1])
                if k[0] == 'par':
                    parameters_1()
                if k == ('gate', 'ga', 0):
                    parameters_2()
                if k[0] == 'tile':
                    tile(k[1:])
                if k[0] == 'conv':
                    convolve(k[1])
                if k[0] == 'lru_a':
                    inputs()
                if k[0] == 'lru_b':
                    recurrence()
                if k[0] == 'ms':
                    mem_max(k[1])
                if k[0] == 'scale':
                    scale(k[1:])
                if k[0] == 'ds':
                    diff_max(k[1])
                if k[0] == 'dc':
                    difference(k[1])
                if k[0] == 'dv' and diff_units[k[1]][1] == NF - 1:
                    sum_squares(('yd', diff_units[k[1]][0]))
                if k[0] == 'xs':
                    scale2(k[1])
                if k[0] == 'x2':
                    x2_features(k[1])
                if k[0] == 'lo':
                    b = k[1]
                    dve.wait_ge(ps_done, PS[k] + 1)
                    if b == 0:
                        dve.wait_ge(more_consts, 1)
                    dve.tensor_tensor(lg_sb[:, b, :], ps[PS[k] % 2][:, 0:NR], br[:, :], ALU.add).then_inc(logits_ready, 1)
            dve.wait_ge(logits_ready, TB)

            dve.wait_ge(ps_done, PS[('cum', 0)] + 1)
            dve.scalar_tensor_tensor(posm[:, :, :], ps[PS[('cum', 0)] % 2][:, 0:TB * NE].rearrange("p (b e) -> p b e", b=TB),
                                     1.0, sel[:, :, :], ALU.add, ALU.mult).then_inc(cum_read, 1)
            dve.wait_ge(cum_read, 1)
            link(dve.tensor_scalar(posm[:, :, :], posm[:, :, :], -1.0, None, ALU.add))

            def count_rounds():
                dve.wait_ge(ps_done, PS[('cnt', 0)] + 1)
                link(dve.tensor_reduce(cnt[:, 0:1], h_bank[:, 0:NE], AX, ALU.max))
                link(dve.tensor_scalar(cnt[:, 1:9], iota_s[:, 0:8], float(CAP), cnt[:, 0:1], ALU.mult, ALU.is_lt))
                link(dve.tensor_reduce(cnt[:, 9:10], cnt[:, 1:9], AX, ALU.add))
                dve.tensor_copy(nr_i[:, :], cnt[:, 9:10]).then_inc(nr_ready, 1)

            def low_bits(i, raw):
                dve.tensor_tensor(w_lo[:, i, :, :, :], raw, w_hi[:, i, :, :, :], ALU.subtract).then_inc(lo_ready, 1)

            def split_low(r, e, j, d, half):
                if exists(e, d):
                    dve.wait_ge(hi_ready, 2 * (r * NE + e) + (2 * d + half + 1))
                split(dve, r, e, j, d, half, low_bits)

            def one_hot(r, e, j, d):
                n, u = r * NE + e + d, (j + d) % 2
                if d >= 2 or not isinstance(e, int) or not isinstance(r, int):
                    dve.wait_ge(tab_done, n - 1)
                dve.tensor_copy(tab_e[:, u, :, :], tab_r[:, :, e + d, :])
                dve.tensor_tensor(onehot[:, u, :, :], iota_s[:, :].unsqueeze(1).to_broadcast([P, TB, CAP]),
                                  posm[:, :, e + d].unsqueeze(2).to_broadcast([P, TB, CAP]), ALU.is_equal).then_inc(oh_ready, 1)

            def indices(r, e, j, d):
                j_ = (j + d) % UN
                dve.wait_ge(tab_done, r * NE + e + (d + 1))
                dve.tensor_scalar(idx[0:CAP, j_, :], tab_bank[0:CAP, 0:1], BIG, None, ALU.add)
                dve.tensor_scalar(idy[0:CAP, j_, :], tab_bank[0:CAP, 2:3], BIG, None, ALU.add)
                dve.tensor_copy(gw[0:CAP, j_, :], tab_bank[0:CAP, 1:2]).then_inc(idx_ready, 1)

            def x_features(n, u):
                dve.wait_ge(xt_done, n + 4)
                dve.tensor_tensor(xg_t[:, u, :, :], pt[0][:, :].rearrange("p (k s) -> p k s", k=KT),
                                  gain_in[:, 2, :].unsqueeze(2).to_broadcast([P, KT, CAP]), ALU.mult).then_inc(xt_ready, 1)

            def x_low(n, u):
                dve.wait_ge(x_hi_ready, n + 1)
                dve.tensor_tensor(x_hl[:, u, :, CAP:2 * CAP], xg_t[:, u, :, :], x_hl[:, u, :, 0:CAP], ALU.subtract).then_inc(x_lo_ready, 1)

            def y_half(n, u):
                dve.wait_ge(y_done, n + 1)
                dve.wait_ge(scattered[u], n * 8 - 8 * u)
                dve.tensor_copy(y_sb[:, u, 512:1024], po[1][0:CAP, :]).then_inc(y_copied1, 1)

            def round_(r):
                if not isinstance(r, int):
                    for u in range(2):
                        dve.wait_ge(scattered[u], r * (8 * NE))
                    dve.tensor_scalar(posm[:, :, :], posm[:, :, :], -float(CAP), None, ALU.add).then_inc(round_done, 1)
                    dve.wait_ge(round_done, r)
                for d in range(3):
                    one_hot(r, 0, 0, d)
                    if d >= 1:
                        indices(r, 0, 0, d - 1)
                indices(r, 0, 0, 2)
                if not isinstance(r, int):
                    for p in range(PIECES):
                        split_low(r, 0, 0, p // 2, p % 2)
                x_features(r * NE, 0)
                x_low(r * NE, 0)
                if isinstance(r, int):
                    count_rounds()
                    dve.wait_ge(lo_ready, PIECES)

                def expert(e, j, first, last):
                    n, u = r * NE + e, j % 2
                    if exists(e, 3):
                        one_hot(r, e, j, 3)
                    split_low(r, e, j, 1, 1)
                    if not last:
                        x_features(n + 1, 1 - u)
                    dve.wait_ge(low_ready, n + 1)
                    dve.tensor_tensor(gu_sum, pa[u][0:CAP, :], gu_low, ALU.add).then_inc(sum_ready, 1)
                    if not last:
                        x_low(n + 1, 1 - u)
                    dve.wait_ge(silu_ready, n + 1)
                    dve.scalar_tensor_tensor(h_sb[0:CAP, u, :], silu, gw[0:CAP, j, :], gu_sum[:, FE:2 * FE],
                                             ALU.mult, ALU.mult).then_inc(h_ready, 1)
                    split_low(r, e, j, 2, 0)
                    if not first:
                        y_half(n - 1, 1 - u)
                    if not exists(e, 3):
                        return
                    if not isinstance(e, int) or e + 3 >= UN:
                        dve.wait_ge(scattered[1 - u], n * 8 - 8 - 8 * (1 - u))
                    indices(r, e, j, 3)
                bodies(dve, expert)
                y_half(r * NE + NE - 1, (NE - 1) % 2)
            all_rounds(dve, round_)

            for b in tb:
                for c in range(2):
                    dve.wait_ge(res_in[b][c], 16)
                    ins = dve.tensor_tensor(x_sb[:, b, :], x_sb[:, b, :], res[:, b, c, :], ALU.add)
                    if c == 0:
                        link(ins)
                ins.then_inc(res_added, 1)


def kernel(**inputs):
    import numpy as _np
    import concourse.bacc as _bacc
    from concourse import mybir as _mybir
    from concourse.bass_utils import run_bass_kernel_spmd as _run

    nc = _bacc.Bacc("TRN2", target_bir_lowering=False, num_devices=1)
    arrays, args = {}, {}
    for name in INS:
        arr = _np.ascontiguousarray(inputs[name])
        arrays[f"in_{name}"] = arr
        args[name] = nc.dram_tensor(f"in_{name}", arr.shape, _mybir.dt.from_np(arr.dtype), kind="ExternalInput").ap()
    out = nc.dram_tensor("out_0", (1, S, D), _mybir.dt.float32, kind="ExternalOutput").ap()
    build(nc, args, out)
    r = _run(nc, [arrays], core_ids=[0])
    return r.results[0]["out_0"]
```
